# Optimizing a Trainium2 kernel written in Bass

```python
import jax
import jax.numpy as jnp
from jax import lax
import numpy as np
import math
import jax, jax.numpy as jnp

D_MODEL = 1024
BATCH = 1
SEQ = 512
DEPTH = 1

GRID_W = 64
CTX_LEN = 256

NA_HEADS = 8
NA_HEAD_DIM = 64
NA_WIDTH = NA_HEADS * NA_HEAD_DIM
NA_KH = 8
NA_KW = 16
NA_QB_W = 16
NA_KB_W = NA_QB_W + NA_KW
NA_NCB = GRID_W // NA_QB_W

HG_HEADS = 4
HG_DK = 128
HG_WIDTH = HG_HEADS * HG_DK
HG_CHUNK = 64

MIX_WIDTH = NA_WIDTH + HG_WIDTH
IN_COLS = 3 * NA_WIDTH + 5 * HG_WIDTH

PEER_HEADS = 8
PEER_NKEYS = 128
PEER_EXPERTS = PEER_NKEYS * PEER_NKEYS
PEER_TOPK = 16
PEER_DQ = 256
PEER_BLOCK = 128

N_MOD = 6
EPS = 1e-6


def rms_norm(x, g):
    xf = x.astype(jnp.float32)
    y = xf * lax.rsqrt(jnp.mean(xf * xf, axis=-1, keepdims=True) + EPS)
    return (y * g.astype(jnp.float32)).astype(x.dtype)

def modulate(h, shift, scale):
    return h * (1 + scale) + shift

def neighbourhood_attention(q, k, v, k_ctx, v_ctx, rpb):
    B, S, H, Dh = q.shape
    rows = S // GRID_W
    kh = min(NA_KH, rows)
    scale = Dh ** -0.5
    qg = q.reshape(B, rows, GRID_W, H, Dh)
    kg = k.reshape(B, rows, GRID_W, H, Dh)
    vg = v.reshape(B, rows, GRID_W, H, Dh)
    qcol = np.arange(GRID_W).reshape(NA_NCB, NA_QB_W)
    kc0 = np.clip(qcol[:, 0] - NA_KW // 2, 0, GRID_W - NA_KB_W)
    kcol = kc0[:, None] + np.arange(NA_KB_W)[None, :]
    cstart = np.clip(qcol - NA_KW // 2, 0, GRID_W - NA_KW)
    col_ok = (kcol[:, None, :] >= cstart[..., None]) & (kcol[:, None, :] < cstart[..., None] + NA_KW)
    dc_idx = np.clip(kcol[:, None, :] - qcol[..., None] + NA_KW - 1, 0, 2 * NA_KW - 2)
    n_win = kh * NA_KB_W

    def row_block(r):
        rs = jnp.clip(r - kh // 2, 0, rows - kh)
        q_r = lax.dynamic_index_in_dim(qg, r, axis=1, keepdims=False).reshape(B, NA_NCB, NA_QB_W, H, Dh)
        k_rows = lax.dynamic_slice_in_dim(kg, rs, kh, axis=1)
        v_rows = lax.dynamic_slice_in_dim(vg, rs, kh, axis=1)
        kb = k_rows[:, :, kcol]
        vb = v_rows[:, :, kcol]
        dr_idx = rs + jnp.arange(kh) - r + NA_KH - 1
        bias = rpb[:, dr_idx[None, None, :, None], dc_idx[:, :, None, :]]
        s_win = jnp.einsum('bcqhd,bkcjhd->bhcqkj', q_r, kb).astype(jnp.float32) * scale
        s_win = jnp.where(col_ok[None, None, :, :, None, :], s_win + bias.astype(jnp.float32)[None], -jnp.inf)
        s_ctx = jnp.einsum('bcqhd,blhd->bhcql', q_r, k_ctx).astype(jnp.float32) * scale
        p = jax.nn.softmax(jnp.concatenate([s_win.reshape(B, H, NA_NCB, NA_QB_W, n_win), s_ctx], axis=-1), axis=-1)
        p = p.astype(v.dtype)
        p_win = p[..., :n_win].reshape(B, H, NA_NCB, NA_QB_W, kh, NA_KB_W)
        o = (jnp.einsum('bhcqkj,bkcjhd->bcqhd', p_win, vb)
             + jnp.einsum('bhcql,blhd->bcqhd', p[..., n_win:], v_ctx))
        return o.reshape(B, GRID_W, H, Dh)

    out = lax.map(row_block, jnp.arange(rows))
    return jnp.moveaxis(out, 0, 1).reshape(B, S, H * Dh)

def context_attention(q, k, v):
    B, L, H, Dh = q.shape
    s = jnp.einsum('blhd,bmhd->bhlm', q, k).astype(jnp.float32) * Dh ** -0.5
    p = jax.nn.softmax(s, axis=-1).astype(v.dtype)
    return jnp.einsum('bhlm,bmhd->blhd', p, v).reshape(B, L, H * Dh)

def _na_heads(t):
    B, T, _ = t.shape
    return t.reshape(B, T, NA_HEADS, NA_HEAD_DIM)

def _hg_heads(t):
    B, T, _ = t.shape
    return t.reshape(B, T, HG_HEADS, HG_DK).transpose(0, 2, 1, 3)

def _forget(z, lb):
    lb = lb.reshape(HG_HEADS, 1, HG_DK)
    f = lb + (1 - lb) * jax.nn.sigmoid(z.astype(jnp.float32))
    return jnp.log(f), 1 - f

def _time_flip(t, rev):
    return jnp.flip(t, axis=2) if rev else t

def gla_chunked(q, k, v, log_f, s0, with_output):
    B, H, T, _ = q.shape
    n_chunks = T // HG_CHUNK

    def chunks(t):
        return t.astype(jnp.float32).reshape(B, H, n_chunks, HG_CHUNK, t.shape[-1]).transpose(2, 0, 1, 3, 4)

    kc, vc, lfc = chunks(k), chunks(v), chunks(log_f)

    def update(S, k_n, v_n, b):
        b_last = b[:, :, -1:, :]
        k_dec = k_n * jnp.exp(b_last - b)
        return jnp.exp(b_last[:, :, 0, :])[..., None] * S + jnp.einsum('bhsd,bhsv->bhdv', k_dec, v_n)

    if not with_output:
        def state_step(S, xs):
            k_n, v_n, lf_n = xs
            return update(S, k_n, v_n, jnp.cumsum(lf_n, axis=2)), None
        s_fin, _ = lax.scan(state_step, s0, (kc, vc, lfc))
        return None, s_fin

    qc = chunks(q)
    causal = jnp.tril(jnp.ones((HG_CHUNK, HG_CHUNK), dtype=bool))

    def step(S, xs):
        q_n, k_n, v_n, lf_n = xs
        b = jnp.cumsum(lf_n, axis=2)
        pair = b[:, :, :, None, :] - b[:, :, None, :, :]
        decay = jnp.exp(jnp.where(causal[:, :, None], pair, -jnp.inf))
        A = jnp.einsum('bhtd,bhsd,bhtsd->bhts', q_n, k_n, decay)
        o = jnp.einsum('bhts,bhsv->bhtv', A, v_n) + jnp.einsum('bhtd,bhdv->bhtv', q_n * jnp.exp(b), S)
        return update(S, k_n, v_n, b), o

    s_fin, o = lax.scan(step, s0, (qc, kc, vc, lfc))
    o = o.transpose(1, 2, 0, 3, 4).reshape(B, H, T, -1)
    return o, s_fin

def _gated_out(o, g, norm_g):
    B, H, T, Dv = o.shape
    o = o * lax.rsqrt(jnp.mean(o * o, axis=-1, keepdims=True) + EPS) * norm_g.astype(jnp.float32).reshape(H, 1, Dv)
    o = o * jax.nn.silu(_hg_heads(g).astype(jnp.float32))
    return o.transpose(0, 2, 1, 3).reshape(B, T, H * Dv).astype(g.dtype)

def hgrn2_mixer(px, pc, lb, norm_g, need_ctx):
    qx, vx = jax.nn.silu(_hg_heads(px[0])), _hg_heads(px[3])
    qc, vc = jax.nn.silu(_hg_heads(pc[0])), _hg_heads(pc[3])
    s0 = jnp.zeros((qx.shape[0], HG_HEADS, HG_DK, HG_DK), jnp.float32)
    outs_x, outs_c = [], []
    for d in range(2):
        rev = d == 1
        lf_c, k_c = _forget(_hg_heads(pc[1 + d]), lb[d])
        lf_x, k_x = _forget(_hg_heads(px[1 + d]), lb[d])
        o_c, s_c = gla_chunked(_time_flip(qc, rev), _time_flip(k_c, rev), _time_flip(vc, rev),
                               _time_flip(lf_c, rev), s0, need_ctx)
        o_x, _ = gla_chunked(_time_flip(qx, rev), _time_flip(k_x, rev), _time_flip(vx, rev),
                             _time_flip(lf_x, rev), s_c, True)
        outs_x.append(_time_flip(o_x, rev))
        if need_ctx:
            outs_c.append(_time_flip(o_c, rev))
    y_x = _gated_out(outs_x[0] + outs_x[1], px[4], norm_g)
    y_c = _gated_out(outs_c[0] + outs_c[1], pc[4], norm_g) if need_ctx else None
    return y_x, y_c

def peer_ffn(h, wq, sub_keys, u, v):
    B, T, D = h.shape
    tok = h.reshape(-1, PEER_BLOCK, D)

    def block(t):
        q = (t @ wq).reshape(PEER_BLOCK, PEER_HEADS, 2, PEER_DQ // 2)
        s = jnp.einsum('tpcd,pckd->tpck', q, sub_keys).astype(jnp.float32)
        s1, i1 = lax.top_k(s[:, :, 0], PEER_TOPK)
        s2, i2 = lax.top_k(s[:, :, 1], PEER_TOPK)
        cand = (s1[..., :, None] + s2[..., None, :]).reshape(PEER_BLOCK, PEER_HEADS, PEER_TOPK * PEER_TOPK)
        cidx = (i1[..., :, None] * PEER_NKEYS + i2[..., None, :]).reshape(PEER_BLOCK, PEER_HEADS, PEER_TOPK * PEER_TOPK)
        top, pos = lax.top_k(cand, PEER_TOPK)
        idx = jnp.take_along_axis(cidx, pos, axis=-1)
        g = jax.nn.softmax(top, axis=-1)
        a = jax.nn.gelu(jnp.einsum('tpkd,td->tpk', u[idx], t).astype(jnp.float32), approximate=False)
        return jnp.einsum('tpk,tpkd->td', (g * a).astype(t.dtype), v[idx])

    return lax.map(block, tok).reshape(B, T, D)

def first_inputs(seed: int = 0) -> dict:
    key = jax.random.key(seed)
    ks = jax.random.split(key, 18)

    def nrm(k, shape, scale):
        return jax.random.normal(k, shape, jnp.float32) * scale

    return {
        'x': nrm(ks[0], (BATCH, SEQ, D_MODEL), 1.0),
        'c': nrm(ks[1], (BATCH, D_MODEL), 1.0),
        'ctx': nrm(ks[2], (BATCH, CTX_LEN, D_MODEL), 1.0),
        'c_ctx': nrm(ks[3], (D_MODEL,), 1.0),
        'w_mod': nrm(ks[4], (DEPTH, D_MODEL, N_MOD * D_MODEL), 0.5 * D_MODEL ** -0.5),
        'b_mod': nrm(ks[5], (DEPTH, N_MOD * D_MODEL), 0.01),
        'norm1': 1.0 + nrm(ks[6], (DEPTH, D_MODEL), 0.05),
        'norm2': 1.0 + nrm(ks[7], (DEPTH, D_MODEL), 0.05),
        'w_in': nrm(ks[8], (DEPTH, D_MODEL, IN_COLS), D_MODEL ** -0.5),
        'w_out': nrm(ks[9], (DEPTH, MIX_WIDTH, D_MODEL), MIX_WIDTH ** -0.5),
        'na_rpb': nrm(ks[10], (DEPTH, NA_HEADS, 2 * NA_KH - 1, 2 * NA_KW - 1), 0.2),
        'hg_lb': nrm(ks[11], (DEPTH + 1, 2, HG_WIDTH), 1.0),
        'hg_norm': 1.0 + nrm(ks[12], (DEPTH, HG_WIDTH), 0.05),
        'peer_wq': nrm(ks[13], (DEPTH, D_MODEL, PEER_HEADS * PEER_DQ), D_MODEL ** -0.5),
        'peer_keys': nrm(ks[14], (DEPTH, PEER_HEADS, 2, PEER_NKEYS, PEER_DQ // 2), (PEER_DQ // 2) ** -0.5),
        'peer_u': nrm(ks[15], (DEPTH, PEER_EXPERTS, D_MODEL), D_MODEL ** -0.5),
        'peer_v': nrm(ks[16], (DEPTH, PEER_EXPERTS, D_MODEL), PEER_HEADS ** -0.5),
        'norm_f': 1.0 + nrm(ks[17], (D_MODEL,), 0.05),
    }

def first_block(x, c, ctx, c_ctx, w_mod, b_mod, norm1, norm2, w_in, w_out, na_rpb, hg_lb, hg_norm,
              peer_wq, peer_keys, peer_u, peer_v, norm_f):
    lb_all = jnp.cumsum(jax.nn.softmax(hg_lb.astype(jnp.float32), axis=0), axis=0)
    splits = [NA_WIDTH, 2 * NA_WIDTH, 3 * NA_WIDTH] + [3 * NA_WIDTH + j * HG_WIDTH for j in range(1, 5)]
    for l in range(DEPTH):
        need_ctx = l < DEPTH - 1
        mod_x = (jax.nn.silu(c) @ w_mod[l] + b_mod[l])[:, None, :]
        mod_c = jax.nn.silu(c_ctx) @ w_mod[l] + b_mod[l]
        sh1, sc1, gt1, sh2, sc2, gt2 = jnp.split(mod_x, N_MOD, axis=-1)
        csh1, csc1, cgt1, csh2, csc2, cgt2 = jnp.split(mod_c, N_MOD, axis=-1)

        px = jnp.split(modulate(rms_norm(x, norm1[l]), sh1, sc1) @ w_in[l], splits, axis=-1)
        pc = jnp.split(modulate(rms_norm(ctx, norm1[l]), csh1, csc1) @ w_in[l], splits, axis=-1)
        k_ctx, v_ctx = _na_heads(pc[1]), _na_heads(pc[2])
        na_x = neighbourhood_attention(_na_heads(px[0]), _na_heads(px[1]), _na_heads(px[2]),
                                       k_ctx, v_ctx, na_rpb[l])
        hg_x, hg_c = hgrn2_mixer(px[3:], pc[3:], lb_all[l], hg_norm[l], need_ctx)
        x = x + gt1 * (jnp.concatenate([na_x, hg_x], axis=-1) @ w_out[l])
        if need_ctx:
            na_c = context_attention(_na_heads(pc[0]), k_ctx, v_ctx)
            ctx = ctx + cgt1 * (jnp.concatenate([na_c, hg_c], axis=-1) @ w_out[l])
            ctx = ctx + cgt2 * peer_ffn(modulate(rms_norm(ctx, norm2[l]), csh2, csc2),
                                        peer_wq[l], peer_keys[l], peer_u[l], peer_v[l])

        x = x + gt2 * peer_ffn(modulate(rms_norm(x, norm2[l]), sh2, sc2),
                               peer_wq[l], peer_keys[l], peer_u[l], peer_v[l])
    return rms_norm(x, norm_f)


DEPTH_2 = 2

N_MEM = 256
HEAD_DIM = 64
N_MEM_HEADS = 4
MEM_WIDTH = N_MEM_HEADS * HEAD_DIM
CONV_WIDTH = D_MODEL - MEM_WIDTH
CONV_K = 3
N_Q_HEADS = CONV_WIDTH // HEAD_DIM
N_KV_HEADS = 4
GROUP = N_Q_HEADS // N_KV_HEADS
Q_WIDTH = N_Q_HEADS * HEAD_DIM
KV_WIDTH = N_KV_HEADS * HEAD_DIM
A_PROJ = 3 * CONV_WIDTH + MEM_WIDTH
B_PROJ = Q_WIDTH + MEM_WIDTH
WINDOW = 128
BLOCK = 128
REL_BUCKETS = 32
REL_MAX_DIST = 128
D_FF = ((8 * D_MODEL + 3 * 256 - 1) // (3 * 256)) * 256
N_A = DEPTH_2 // 2
N_B = DEPTH_2 - N_A
EPS_2 = 1e-5


def rmsnorm(x, g):
    x32 = x.astype(jnp.float32)
    y = x32 * lax.rsqrt(jnp.mean(x32 * x32, axis=-1, keepdims=True) + EPS_2)
    return (y * g.astype(jnp.float32)).astype(x.dtype)

def _rel_bucket(dist):
    max_exact = REL_BUCKETS // 2
    d = jnp.maximum(dist, 1).astype(jnp.float32)
    large = max_exact + (jnp.log(d / max_exact) / math.log(REL_MAX_DIST / max_exact)
                         * (REL_BUCKETS - max_exact)).astype(jnp.int32)
    large = jnp.minimum(large, REL_BUCKETS - 1)
    return jnp.where(dist < max_exact, dist, large)

def _band_geometry(n_blocks):
    qi = jnp.arange(BLOCK, dtype=jnp.int32)[:, None]
    kj = jnp.arange(2 * BLOCK, dtype=jnp.int32)[None, :]
    dist = qi + BLOCK - kj
    in_window = (dist >= 0) & (dist < WINDOW)
    first = (jnp.arange(n_blocks) == 0)[:, None, None]
    mask = in_window[None] & ~(first & (kj[None] < BLOCK))
    bucket = _rel_bucket(jnp.maximum(dist, 0))
    return mask, bucket

def _band(t):
    bsz, s = t.shape[0], t.shape[1]
    tb = t.reshape(bsz, s // BLOCK, BLOCK, N_KV_HEADS, HEAD_DIM)
    prev = jnp.concatenate([jnp.zeros_like(tb[:, :1]), tb[:, :-1]], axis=1)
    return jnp.concatenate([prev, tb], axis=2)

def _short_conv(u, b_gate, c_gate, w):
    v = c_gate * u
    s = v.shape[1]
    vp = jnp.pad(v, ((0, 0), (CONV_K - 1, 0), (0, 0)))
    conv = w[0] * vp[:, 0:s] + w[1] * vp[:, 1:s + 1] + w[2] * vp[:, 2:s + 2]
    return b_gate * conv

def _swa_sinks(q, k_band, v_band, sinks, rel_bias, mask, bucket):
    bsz, s, _ = q.shape
    nb = s // BLOCK
    qb = q.reshape(bsz, nb, BLOCK, N_KV_HEADS, GROUP, HEAD_DIM)
    logits = jnp.einsum('bnqhgd,bnjhd->bnhgqj', qb, k_band).astype(jnp.float32) * (HEAD_DIM ** -0.5)
    bias = jnp.transpose(rel_bias.astype(jnp.float32)[bucket], (2, 0, 1))
    bias = bias.reshape(N_KV_HEADS, GROUP, BLOCK, 2 * BLOCK)
    logits = jnp.where(mask[None, :, None, None], logits + bias, -jnp.inf)
    sink = sinks.astype(jnp.float32).reshape(N_KV_HEADS, GROUP, 1, 1)
    m = jnp.maximum(jnp.max(logits, axis=-1, keepdims=True), sink)
    p = jnp.exp(logits - m)
    denom = jnp.sum(p, axis=-1, keepdims=True) + jnp.exp(sink - m)
    probs = (p / denom).astype(v_band.dtype)
    out = jnp.einsum('bnhgqj,bnjhd->bnqhgd', probs, v_band)
    return out.reshape(bsz, s, Q_WIDTH)

def _mem_attention(q_mem, mem_k, mem_v):
    bsz, s = q_mem.shape[0], q_mem.shape[1]
    logits = jnp.einsum('bshd,bmhd->bhsm', q_mem, mem_k).astype(jnp.float32) * (HEAD_DIM ** -0.5)
    probs = jax.nn.softmax(logits, axis=-1).astype(mem_v.dtype)
    return jnp.einsum('bhsm,bmhd->bshd', probs, mem_v).reshape(bsz, s, MEM_WIDTH)

def second_inputs(seed: int = 0) -> dict:
    key = jax.random.key(seed)
    ks = jax.random.split(key, 20)

    def nrm(k, shape, scale):
        return jax.random.normal(k, shape, jnp.float32) * scale

    def gain(k, shape):
        return 1.0 + nrm(k, shape, 0.05)

    return {
        'x': nrm(ks[0], (BATCH, SEQ, D_MODEL), 1.0),
        'mem': nrm(ks[1], (BATCH, N_MEM, D_MODEL), 1.0),
        'norm_mix': gain(ks[2], (DEPTH_2, D_MODEL)),
        'norm_ffn': gain(ks[3], (DEPTH_2, D_MODEL)),
        'a_w_in': nrm(ks[4], (N_A, D_MODEL, A_PROJ), D_MODEL ** -0.5),
        'a_conv_w': nrm(ks[5], (N_A, CONV_K, CONV_WIDTH), CONV_K ** -0.5),
        'a_w_out': nrm(ks[6], (N_A, CONV_WIDTH + MEM_WIDTH, D_MODEL), (CONV_WIDTH + MEM_WIDTH) ** -0.5),
        'kv_norm': gain(ks[7], (D_MODEL,)),
        'w_kv': nrm(ks[8], (D_MODEL, 2 * KV_WIDTH), D_MODEL ** -0.5),
        'b_w_q': nrm(ks[9], (N_B, D_MODEL, B_PROJ), D_MODEL ** -0.5),
        'b_sinks': nrm(ks[10], (N_B, N_Q_HEADS), 0.5),
        'b_w_out': nrm(ks[11], (N_B, Q_WIDTH + MEM_WIDTH, D_MODEL), (Q_WIDTH + MEM_WIDTH) ** -0.5),
        'rel_bias': nrm(ks[12], (REL_BUCKETS, N_Q_HEADS), 0.5),
        'mem_norm': gain(ks[13], (D_MODEL,)),
        'w_mem_kv': nrm(ks[14], (DEPTH_2, D_MODEL, 2 * MEM_WIDTH), D_MODEL ** -0.5),
        'w_gate': nrm(ks[15], (DEPTH_2, D_MODEL, D_FF), D_MODEL ** -0.5),
        'w_up': nrm(ks[16], (DEPTH_2, D_MODEL, D_FF), D_MODEL ** -0.5),
        'w_down': nrm(ks[17], (DEPTH_2, D_FF, D_MODEL), D_FF ** -0.5),
        'final_norm': gain(ks[18], (D_MODEL,)),
    }

def second_block(x, mem, norm_mix, norm_ffn, a_w_in, a_conv_w, a_w_out, kv_norm, w_kv,
              b_w_q, b_sinks, b_w_out, rel_bias, mem_norm, w_mem_kv, w_gate, w_up, w_down,
              final_norm):
    bsz, s, _ = x.shape
    mask, bucket = _band_geometry(s // BLOCK)
    mem_n = rmsnorm(mem, mem_norm)
    k_band = None
    v_band = None
    for i in range(DEPTH_2):
        if i == N_A:
            kv = rmsnorm(x, kv_norm) @ w_kv
            k, v = jnp.split(kv, 2, axis=-1)
            k_band = _band(k.reshape(bsz, s, N_KV_HEADS, HEAD_DIM))
            v_band = _band(v.reshape(bsz, s, N_KV_HEADS, HEAD_DIM))
        mem_kv = mem_n @ w_mem_kv[i]
        mk, mv = jnp.split(mem_kv, 2, axis=-1)
        mk = mk.reshape(bsz, N_MEM, N_MEM_HEADS, HEAD_DIM)
        mv = mv.reshape(bsz, N_MEM, N_MEM_HEADS, HEAD_DIM)
        h = rmsnorm(x, norm_mix[i])
        if i < N_A:
            proj = h @ a_w_in[i]
            u, b_gate, c_gate, q_mem = jnp.split(
                proj, [CONV_WIDTH, 2 * CONV_WIDTH, 3 * CONV_WIDTH], axis=-1)
            y_tok = _short_conv(u, b_gate, c_gate, a_conv_w[i])
            w_out = a_w_out[i]
        else:
            j = i - N_A
            proj = h @ b_w_q[j]
            q, q_mem = jnp.split(proj, [Q_WIDTH], axis=-1)
            y_tok = _swa_sinks(q, k_band, v_band, b_sinks[j], rel_bias, mask, bucket)
            w_out = b_w_out[j]
        y_mem = _mem_attention(q_mem.reshape(bsz, s, N_MEM_HEADS, HEAD_DIM), mk, mv)
        x = x + jnp.concatenate([y_tok, y_mem], axis=-1) @ w_out
        h = rmsnorm(x, norm_ffn[i])
        x = x + (jax.nn.silu(h @ w_gate[i]) * (h @ w_up[i])) @ w_down[i]
    return rmsnorm(x, final_norm)


def setup_inputs(seed=0):
    out = dict(first_inputs(seed))
    for name, value in second_inputs(seed + 1).items():
        if name != "x":
            out[name + "_2"] = value
    return out


def reference(
    x, c, ctx, c_ctx, w_mod, b_mod, norm1, norm2, w_in, w_out, na_rpb, hg_lb, hg_norm, peer_wq,
    peer_keys, peer_u, peer_v, norm_f, mem_2, norm_mix_2, norm_ffn_2, a_w_in_2, a_conv_w_2,
    a_w_out_2, kv_norm_2, w_kv_2, b_w_q_2, b_sinks_2, b_w_out_2, rel_bias_2, mem_norm_2,
    w_mem_kv_2, w_gate_2, w_up_2, w_down_2, final_norm_2,
):
    x = first_block(
        x, c, ctx, c_ctx, w_mod, b_mod, norm1, norm2, w_in, w_out, na_rpb, hg_lb, hg_norm,
        peer_wq, peer_keys, peer_u, peer_v, norm_f,
    )
    return second_block(
        x, mem_2, norm_mix_2, norm_ffn_2, a_w_in_2, a_conv_w_2, a_w_out_2, kv_norm_2, w_kv_2,
        b_w_q_2, b_sinks_2, b_w_out_2, rel_bias_2, mem_norm_2, w_mem_kv_2, w_gate_2, w_up_2,
        w_down_2, final_norm_2,
    )


_drawn_inputs = setup_inputs


def setup_inputs(seed=0):
    import zlib

    import numpy as np

    out = dict(_drawn_inputs(seed))
    spreads = {}
    factors = {'b_mod': 3.397,
     'norm1': 3.205,
     'na_rpb': 8.0,
     'hg_lb': 3.259,
     'hg_norm': 4.134,
     'kv_norm_2': 6.553,
     'b_sinks_2': 8.0,
     'mem_norm_2': 8.0}
    for name, (base, spread) in spreads.items():
        noise = np.random.default_rng([zlib.crc32(name.encode()), seed]).standard_normal(out[name].shape)
        drawn = base * np.exp(spread * noise) if base else spread * noise
        out[name] = jnp.asarray(drawn.astype(out[name].dtype))
    for name, factor in factors.items():
        out[name] = (out[name] * factor).astype(out[name].dtype)
    return out
```

```python
from contextlib import ExitStack

import numpy as np
import concourse.bass as bass
from concourse import mybir
from concourse.alu_op_type import AluOpType as ALU

ACT = mybir.ActivationFunctionType
AX = mybir.AxisListType
F32 = mybir.dt.float32
U32 = mybir.dt.uint32
ds = bass.ds

P = 128
D, T, L, MEM = 1024, 512, 256, 256
KC = D // P
TT, LT = T // P, L // P
GRID_W = 64
NA_H, DH = 8, 64
NA_KH, NA_KW = 8, 16
NDR, NDC = 2 * NA_KH - 1, 2 * NA_KW - 1
HG_H, DK = 4, 128
CH = 128
NCH = T // CH
LEVELS = 7
PE_H, NKEYS, TOPK = 8, 128, 16
KV_H, GROUP, SWA_H = 4, 3, 12
BUCKETS, MAXD = 32, 128
D_FF = 2816
FT = D_FF // P
CONV = 768
Q_WIDTH = SWA_H * DH
EPS1, EPS2 = 1e-6, 1e-5
BIG = 1e30

ROWS_A = dict(c=0, c_ctx=8, b_mod=16, norm1=64, norm2=72, norm_f=80, hg_norm=88, hg_lb=92)
ROWS_B = dict(norm_mix=0, norm_ffn=16, kv_norm=32, mem_norm=40, final=48, conv=56)
NA_ROWS, NB_ROWS = 108, 74


def bucket_starts():
    half = BUCKETS // 2
    dist = np.arange(MAXD)
    near = np.maximum(dist, 1).astype(np.float32)
    far = half + (np.log(near / np.float32(half)) / np.float32(np.log(MAXD / half)) * np.float32(BUCKETS - half)).astype(np.int32)
    bucket = np.where(dist < half, dist, np.minimum(far, BUCKETS - 1))
    return [int(np.argmax(bucket >= b)) if (bucket >= b).any() else MAXD for b in range(BUCKETS)] + [MAXD]


class Chain:

    def __init__(self, engine, sem):
        self.engine, self.sem, self.done, self.turn = engine, sem, 0, 0

    def __call__(self, ins):
        self.done = self.done + 1
        ins.then_inc(self.sem, 1)
        self.engine.wait_ge(self.sem, self.turn + self.done)

    def loop(self, i, per):
        self.before, self.per, self.turn, self.done = self.done, per, i * per + self.done, 0

    def end(self, turns):
        assert self.done == self.per, (self.done, self.per)
        self.done, self.turn = self.before + turns * self.per, 0


def program(nc, io, out):
    whole = ExitStack()

    def sb(name, shape, dt=F32, on=whole):
        return on.enter_context(nc.sbuf_tensor(name, shape, dt))

    def sem(name):
        return whole.enter_context(nc.semaphore(name))

    ps = whole.enter_context(nc.psum_tensor("ps", [P, 8, 512], F32))

    ident = sb("ident", [P, P])
    ones = sb("ones", [P, P])
    xT = sb("xT", [P, KC, T])
    hT = sb("hT", [P, KC, T])
    yT = sb("yT", [P, KC, T])
    rstd = sb("rstd", [P, T])
    memT = sb("memT", [P, KC, MEM])
    vA = sb("vA", [P, NA_ROWS])
    vB = sb("vB", [P, NB_ROWS])
    mod = sb("mod", [P, 6 * KC, 2])
    gain1 = sb("gain1", [P, KC, 2])
    gain2 = sb("gain2", [P, KC])
    wring = sb("wring", [P, 6 * KC * P])
    wslot = wring[:, :].rearrange("p (s k n) -> p s k n", s=6, k=KC)

    SLOTS = 6
    w_landed = [sem(f"w_landed{u}") for u in range(SLOTS)]
    mm_done = [sem(f"mm_done{u}") for u in range(SLOTS)]
    evacuated = [sem(f"evacuated{u}") for u in range(SLOTS)]
    landed, turns, left = [0] * SLOTS, [1] * SLOTS, [1] * SLOTS

    def load_weights(sp, u, it, *pieces):
        sp.wait_ge(mm_done[u], turns[u] + it)
        sp.nop(nofuse=True)
        for dst, src in pieces:
            sp.dma_start(dst, src).then_inc(w_landed[u], 16)

    def weights_in(pe, u, it, pieces=1):
        pe.wait_ge(w_landed[u], 16 * (landed[u] + pieces * (it + 1)))

    def project(pe, u, it, bank, rhs, pieces=1):
        weights_in(pe, u, it, pieces)
        pe.wait_ge(evacuated[u], left[u] + it)
        for k in range(KC):
            mm = pe.matmul(bank, wslot[:, u, k, :], rhs[:, k, :], start=k == 0, stop=k == KC - 1)
        mm.then_inc(mm_done[u], 1)

    def projected(eng, u, it):
        eng.wait_ge(mm_done[u], turns[u] + it + 1)

    def end_ring(slots, times, pieces=1, evacuations=False):
        for u in range(slots):
            landed[u] += times * (pieces if isinstance(pieces, int) else pieces[u])
            turns[u] += times
            left[u] += times if evacuations else 0

    norm_squared, norm_summed, norm_meaned, norm_rooted, norm_scaled, norm_chain = [sem(f"norm_{s}") for s in ("squared", "summed", "meaned", "rooted", "scaled", "chain")]
    norms = dict(parts=0, scaled=0)

    def rms_block(name, parts, eps):
        base, scaled_before = norms["parts"], norms["scaled"]
        with ExitStack() as local:
            sq = sb(f"{name}_sq", [P, KC, T], on=local)
            with nc.Block() as block:
                @block.scalar
                def _(act):
                    done = scaled_before
                    for n, (src, N, outs) in enumerate(parts, base):
                        if n > base:
                            act.wait_ge(norm_summed, n)
                        for h in range(2):
                            act.activation(sq[:, 4 * h:4 * h + 4, 0:N], src[:, 4 * h:4 * h + 4, :], ACT.Square).then_inc(norm_squared, 1)
                        act.wait_ge(norm_meaned, n + 1)
                        act.activation(rstd[:, 0:N], rstd[:, 0:N], ACT.Sqrt).then_inc(norm_rooted, 1)
                        for dst, gain, shift in outs:
                            for k in range(KC):
                                done += 1
                                if shift is not None:
                                    act.wait_ge(norm_scaled, done)
                                    act.activation(dst[:, k, :], dst[:, k, :], ACT.Identity, bias=shift(k))

                @block.tensor
                def _(pe):
                    for n, (src, N, outs) in enumerate(parts, base):
                        for k in range(KC):
                            if k % 4 == 0:
                                pe.wait_ge(norm_squared, 2 * n + k // 4 + 1)
                            if n > base and k == 0:
                                pe.wait_ge(norm_meaned, n)
                            mm = pe.matmul(ps[:, 0, 0:N], ones[:, :], sq[:, k, 0:N], start=k == 0, stop=k == KC - 1)
                        mm.then_inc(norm_summed, 1)

                @block.vector
                def _(dve):
                    link = Chain(dve, norm_chain)
                    link.done = base
                    for n, (src, N, outs) in enumerate(parts, base):
                        dve.wait_ge(norm_summed, n + 1)
                        dve.tensor_scalar(rstd[:, 0:N], ps[:, 0, 0:N], 1.0 / D, eps[n - base], ALU.mult, ALU.add).then_inc(norm_meaned, 1)
                        dve.wait_ge(norm_rooted, n + 1)
                        link(dve.reciprocal(rstd[:, 0:N], rstd[:, 0:N]))
                        for dst, gain, shift in outs:
                            for k in range(KC):
                                dve.scalar_tensor_tensor(dst[:, k, :], src[:, k, :], gain(k), rstd[:, 0:N], ALU.mult, ALU.mult).then_inc(norm_scaled, 1)
        norms["parts"] += len(parts)
        norms["scaled"] += KC * sum(len(outs) for _, _, outs in parts)

    att_scored, att_logit_ready, att_exp_ready, att_prob_ready, att_turned, att_pT_ready, att_weighted = [
        sem(f"att_{x}") for x in ("scored", "logit_ready", "exp_ready", "prob_ready", "turned", "pT_ready", "weighted")]
    att_units = [1]

    class Attention:

        def __init__(self, name, local, units):
            self.units, self.n = units, len(units)
            self.s = sb(f"{name}_s", [P, 2, 768], on=local)
            self.pT = sb(f"{name}_pT", [P, 2, 768], on=local)
            self.small = sb(f"{name}_small", [P, 2, 8], on=local)
            self.before = att_units[0]

        def at(self, i):
            return self.before + self.n * i

        def end(self, turns):
            att_units[0] += self.n * turns

    def col(a, u, j):
        return a.small[:, u % 2, j:j + 1]

    def score_bank(u):
        b = 2 * (u % 2)
        return ps[:, b:b + 2, :].rearrange("p b n -> p (b n)")

    def keys_of(unit):
        return sum(w for _, w in unit["k"])

    def att_score(pe, a, i, u):
        pe.wait_ge(att_logit_ready, a.at(i) + max(u - 1, 0))
        at = 0
        for seg, w in a.units[u]["k"]:
            mm = pe.matmul(score_bank(u)[:, at:at + w], a.units[u]["q"], seg, start=True, stop=True)
            at += w
        mm.then_inc(att_scored, 1)

    def att_turn(pe, a, i, u):
        pe.wait_ge(att_prob_ready, a.at(i) + u + 1)
        pe.wait_ge(att_pT_ready, a.at(i) + u)
        for b in range(keys_of(a.units[u]) // P):
            mm = pe.transpose(ps[:, 4 + b // 4, (b % 4) * P:(b % 4 + 1) * P], a.s[:, u % 2, b * P:(b + 1) * P], ident[:, :])
        mm.then_inc(att_turned, 1)

    def att_weigh(pe, a, i, u, before):
        unit = a.units[u]
        pe.wait_ge(att_pT_ready, a.at(i) + u + 1)
        before(u)
        for b, v in enumerate(unit["v"]):
            mm = pe.matmul(unit["out"], v, a.pT[:, u % 2, b * P:(b + 1) * P], start=b == 0, stop=b == len(unit["v"]) - 1)
        mm.then_inc(att_weighted, 1)

    def att_pe(pe, a, i, before):
        for u in range(a.n + 2):
            if u < a.n:
                att_score(pe, a, i, u)
            if 1 <= u <= a.n:
                att_turn(pe, a, i, u - 1)
            if u >= 2:
                att_weigh(pe, a, i, u - 2, before)

    def att_links(a):
        return sum(2 + (x["sink"] is not None) for x in a.units)

    def att_logits(dve, a, i, u, link, zeros):
        unit = a.units[u]
        dve.wait_ge(att_scored, a.at(i) + u + 1)
        dve.wait_ge(att_turned, a.at(i) + max(u - 1, 0))
        dve.nop(nofuse=True)
        at, start = 0, -BIG if unit["sink"] is None else unit["sink"]
        for j, (seg, w) in enumerate(unit["k"]):
            bias = zeros[:, 0:w] if unit["bias"][j] is None else unit["bias"][j]
            last = dve.tensor_tensor_reduce(a.s[:, u % 2, at:at + w], score_bank(u)[:, at:at + w], bias,
                                            1.0, start, ALU.add, ALU.max, col(a, u, 4 + j))
            at += w
        link(last)
        dve.tensor_scalar(col(a, u, 0), col(a, u, 4), col(a, u, 3 + len(unit["k"])), -1.0, ALU.max, ALU.mult).then_inc(att_logit_ready, 1)

    def att_probs(dve, a, i, u, link):
        n = keys_of(a.units[u])
        dve.wait_ge(att_exp_ready, a.at(i) + u + 1)
        if a.units[u]["sink"] is not None:
            link(dve.tensor_tensor(col(a, u, 1), col(a, u, 1), col(a, u, 2), ALU.add))
        link(dve.reciprocal(col(a, u, 3), col(a, u, 1)))
        dve.tensor_scalar(a.s[:, u % 2, 0:n], a.s[:, u % 2, 0:n], col(a, u, 3), None, ALU.mult).then_inc(att_prob_ready, 1)

    def att_dve(dve, a, i, link, zeros):
        for u in range(a.n + 1):
            if u < a.n:
                att_logits(dve, a, i, u, link, zeros)
            if u >= 1:
                att_probs(dve, a, i, u - 1, link)

    def att_act(act, a, i, after=lambda v: None):
        for u in range(a.n + 1):
            if u < a.n:
                n = keys_of(a.units[u])
                act.wait_ge(att_logit_ready, a.at(i) + u + 1)
                if a.units[u]["sink"] is not None:
                    act.activation(col(a, u, 2), a.units[u]["sink"], ACT.Exp, bias=col(a, u, 0))
                act.activation(a.s[:, u % 2, 0:n], a.s[:, u % 2, 0:n], ACT.Exp, bias=col(a, u, 0),
                               accum_out=col(a, u, 1)).then_inc(att_exp_ready, 1)
            if u >= 1:
                v = u - 1
                n = keys_of(a.units[v])
                act.wait_ge(att_turned, a.at(i) + v + 1)
                act.wait_ge(att_weighted, a.at(i) + max(v - 1, 0))
                act.activation(a.pT[:, v % 2, 0:n], ps[:, 4:6, :].rearrange("p b n -> p (b n)")[:, 0:n],
                               ACT.Copy).then_inc(att_pT_ready, 1)
                after(v)

    def no_wait(u):
        pass

    def gain(v, at):
        return lambda k: v[:, at + k:at + k + 1]

    def weights(w, c0, n=P):
        return w.rearrange("(k p) n -> p k n", p=P)[:, :, ds(c0, n)]

    rpb_scr = nc.dram_tensor("rpb_scr", [NA_H * NDR, P], F32, kind="Internal")
    rel_scr = nc.dram_tensor("rel_scr", [SWA_H, 3 * P], F32, kind="Internal")
    swa_bias = sb("swa_bias", [P, SWA_H, 2 * P])
    sinks = sb("sinks", [P, SWA_H])
    lb = sb("lb", [P, 2, 2, HG_H])
    ctx_mem = ExitStack()
    with ctx_mem:
        ctxT = sb("ctxT", [P, KC, L], on=ctx_mem)
        na_stack = ctx_mem.enter_context(ExitStack())
        na_bias = sb("na_bias", [P, NA_H, 16, GRID_W], on=na_stack)
        with ExitStack() as local:
            tok = sb("tok", [P, TT + 2 * LT, D], on=local)
            rows = sb("rows", [P, 2, P], on=local)
            cT = sb("cT", [P, KC, 2], on=local)
            rpb = sb("rpb", [NA_H * NDR, NDC], on=local)
            rpbT = sb("rpbT", [NDC, NA_H * NDR], on=local)
            spread = sb("spread", [NDC, P], on=local)
            inbucket = sb("inbucket", [BUCKETS, 3 * P], on=local)
            relb = sb("relb", [BUCKETS, SWA_H], on=local)
            wide = sb("wide", [NA_H * NDR, P], on=local)
            far = sb("far", [SWA_H, 3 * P], on=local)
            farmask = sb("farmask", [SWA_H, 3 * P], on=local)
            sink1 = sb("sink1", [1, SWA_H], on=local)
            consts_in, rows_in, rpb_in = sem("consts_in"), sem("rows_in"), sem("rpb_in")
            tok_in = [sem(f"tok_in{n}") for n in range(TT + 2 * LT)]
            rows_turned, silu_ready = sem("rows_turned"), sem("silu_ready")
            x_turned, x_ready = sem("x_turned"), sem("x_ready")
            rpb_turned, rpb_ready, rpb_spread, bias_ready = sem("rpb_turned"), sem("rpb_ready"), sem("rpb_spread"), sem("bias_ready")
            scr_written, bias_in = sem("scr_written"), sem("bias_in")
            na_zero, setup_v, cT_ready = sem("na_zero"), sem("setup_v"), sem("cT_ready")
            MS = 3
            modw = wring[:, :].rearrange("p (s k n) -> p s k n", s=MS, k=KC)
            groups = [(0, k) for k in range(KC)] + [(TT, k) for k in range(0, KC, 2)] + [(TT + LT, k) for k in range(0, KC, 2)]
            with nc.Block() as block:
                @block.sync
                def _(sp):
                    for dst, name in ((ident, "ident"), (spread, "spread"), (inbucket, "inbucket"), (farmask, "farmask"), (ones, "ones")):
                        sp.dma_start(dst[:, :], io["const_" + name]).then_inc(consts_in, 16)
                    for at, names, where in ((0, ("c", "c_ctx", "b_mod", "norm1", "norm2", "norm_f", "hg_norm", "hg_lb"), ROWS_A),
                                             (1, ("norm_mix", "norm_ffn", "kv_norm", "mem_norm", "final", "conv"), ROWS_B)):
                        for name in names:
                            n = io[name].shape[0]
                            sp.dma_start(rows[where[name]:where[name] + n, at, :], io[name]).then_inc(rows_in, 16)
                    for n in range(TT + 2 * LT):
                        src, r = ((io["x"], n) if n < TT else (io["ctx"], n - TT) if n < TT + LT else (io["mem"], n - TT - LT))
                        sp.dma_start(tok[:, n, :], src[r * P:(r + 1) * P, :]).then_inc(tok_in[n], 16)
                    with sp.Fori(0, 6 * KC // 2 // MS) as i:
                        for u in range(MS):
                            load_weights(sp, u, i, (modw[:, u, :, :], weights(io["w_mod"], i * (MS * 2 * P) + u * 2 * P, 2 * P)))

                @block.gpsimd
                def _(pool):
                    pool.memset(na_bias[:, :, :, :], 0.0).then_inc(na_zero, 1)
                    pool.dma_start(rpb[:, :], io["rpb"]).then_inc(rpb_in, 16)
                    pool.dma_start(relb[:, :], io["rel_bias"]).then_inc(rpb_in, 16)
                    pool.dma_start(sink1[:, :], io["sinks"]).then_inc(rpb_in, 16)
                    pool.wait_ge(bias_ready, 2)
                    pool.dma_start(rpb_scr[:, :], wide[:, :]).then_inc(scr_written, 16)
                    pool.dma_start(rel_scr[:, :], far[:, :]).then_inc(scr_written, 16)
                    pool.wait_ge(scr_written, 32)
                    pool.wait_ge(na_zero, 1)
                    for half in range(2):
                        for h in range(NA_H):
                            pool.dma_start(na_bias[half * 64:half * 64 + 64, h, half:half + NDR, :],
                                           bass.AP(rpb_scr, h * NDR * P, [[1, GRID_W], [P, NDR], [1, GRID_W]])).then_inc(bias_in, 16)
                    pool.dma_start(swa_bias[:, :, :], bass.AP(rel_scr, 0, [[1, P], [3 * P, SWA_H], [1, 2 * P]])).then_inc(bias_in, 16)
                    pool.wait_ge(bias_in, 16 * (2 * NA_H + 1))

                @block.tensor
                def _(pe):
                    for u in range(SLOTS):
                        pe.sem_inc(mm_done[u], 1)
                        pe.sem_inc(evacuated[u], 1)
                    for credit in (att_scored, att_logit_ready, att_exp_ready, att_prob_ready, att_turned, att_pT_ready, att_weighted):
                        pe.sem_inc(credit, 1)
                    pe.wait_ge(consts_in, 16 * 5)
                    pe.wait_ge(rows_in, 16 * 14)
                    pe.transpose(ps[:, 7, 0:NA_ROWS], rows[0:NA_ROWS, 0, :], ident[0:NA_ROWS, 0:NA_ROWS])
                    pe.transpose(ps[:, 7, P:P + NB_ROWS], rows[0:NB_ROWS, 1, :], ident[0:NB_ROWS, 0:NB_ROWS]).then_inc(rows_turned, 1)
                    pe.wait_ge(rpb_in, 48)
                    pe.transpose(ps[0:NDC, 5, 0:NA_H * NDR], rpb[:, :], ident[0:NA_H * NDR, 0:NA_H * NDR])
                    pe.matmul(ps[0:SWA_H, 5, P:P + 3 * P], relb[:, :], inbucket[:, :], start=True, stop=True).then_inc(rpb_turned, 1)
                    pe.matmul(ps[:, 4, P:P + SWA_H], ones[0:1, :], sink1[:, :], start=True, stop=True)
                    pe.wait_ge(rpb_ready, 1)
                    pe.matmul(ps[0:NA_H * NDR, 4, 0:P], rpbT[:, :], spread[:, :], start=True, stop=True).then_inc(rpb_spread, 1)
                    for g, (t0, k) in enumerate(groups):
                        if g >= 4:
                            pe.wait_ge(x_ready, g - 3)
                        for b in range(4):
                            t, kk = (t0 + b, k) if t0 == 0 else (t0 + b % 2, k + b // 2)
                            if k == 0 and b < (4 if t0 == 0 else 2):
                                pe.wait_ge(tok_in[t], 16)
                            mm = pe.transpose(ps[:, g % 4, b * P:(b + 1) * P], tok[:, t, kk * P:(kk + 1) * P], ident[:, :])
                        mm.then_inc(x_turned, 1)
                    pe.wait_ge(silu_ready, 1)
                    with pe.Fori(0, 6 * KC // 2 // MS) as i:
                        for u in range(MS):
                            weights_in(pe, u, i)
                            for n in range(2):
                                for k in range(KC):
                                    mm = pe.matmul(ps[:, 6, ds(i * (4 * MS) + 4 * u + 2 * n, 2)], modw[:, u, k, n * P:(n + 1) * P], cT[:, k, :],
                                                   start=k == 0, stop=k == KC - 1)
                            mm.then_inc(mm_done[u], 1)

                @block.scalar
                def _(act):
                    act.wait_ge(cT_ready, 1)
                    act.activation(cT[:, :, :], cT[:, :, :], ACT.Silu).then_inc(silu_ready, 1)

                @block.vector
                def _(dve):
                    link = Chain(dve, setup_v)
                    dve.wait_ge(rows_turned, 1)
                    dve.tensor_copy(vA[:, :], ps[:, 7, 0:NA_ROWS])
                    link(dve.tensor_copy(vB[:, :], ps[:, 7, P:P + NB_ROWS]))
                    dve.tensor_copy(cT[:, :, :], vA[:, 0:2 * KC].rearrange("p (a k) -> p k a", a=2)).then_inc(cT_ready, 1)
                    dve.wait_ge(rpb_turned, 1)
                    dve.tensor_tensor(far[:, :], ps[0:SWA_H, 5, P:P + 3 * P], farmask[:, :], ALU.add).then_inc(bias_ready, 1)
                    dve.tensor_copy(rpbT[:, :], ps[0:NDC, 5, 0:NA_H * NDR]).then_inc(rpb_ready, 1)
                    dve.wait_ge(rpb_spread, 1)
                    dve.tensor_copy(sinks[:, :], ps[:, 4, P:P + SWA_H])
                    dve.tensor_copy(wide[:, :], ps[0:NA_H * NDR, 4, 0:P]).then_inc(bias_ready, 1)
                    for g, (t0, k) in enumerate(groups):
                        dve.wait_ge(x_turned, g + 1)
                        dst = (xT[:, k, :] if t0 == 0 else (ctxT if t0 == TT else memT)[:, k:k + 2, :].rearrange("p k n -> p (k n)"))
                        dve.tensor_copy(dst, ps[:, g % 4, :]).then_inc(x_ready, 1)
                    for u in range(MS):
                        dve.wait_ge(mm_done[u], turns[u] + 6 * KC // 2 // MS)
                    bm = vA[:, ROWS_A["b_mod"]:ROWS_A["b_mod"] + 6 * KC]
                    for a in range(2):
                        last = dve.tensor_tensor(mod[:, :, a], ps[:, 6, 0:12 * KC].rearrange("p (m a) -> p m a", a=2)[:, :, a], bm, ALU.add)
                    link(last)
                    for a in range(2):
                        n1 = vA[:, ROWS_A["norm1"]:ROWS_A["norm1"] + KC]
                        dve.scalar_tensor_tensor(gain1[:, :, a], mod[:, KC:2 * KC, a], 1.0, n1, ALU.add, ALU.mult)
                    n2 = vA[:, ROWS_A["norm2"]:ROWS_A["norm2"] + KC]
                    dve.scalar_tensor_tensor(gain2[:, :], mod[:, 4 * KC:5 * KC, 0], 1.0, n2, ALU.add, ALU.mult)
                    lo = vA[:, ROWS_A["hg_lb"]:ROWS_A["hg_lb"] + 16].rearrange("p (e d h) -> p e d h", e=2, d=2)
                    link(dve.tensor_tensor(lb[:, 0, :, :], lo[:, 0, :, :], lo[:, 1, :, :], ALU.subtract))
            end_ring(MS, 6 * KC // 2 // MS)

        mul1 = lambda a: (lambda k: gain1[:, k, a:a + 1])
        add1 = lambda a: (lambda k: mod[:, k, a:a + 1])
        rms_block("n1", [(xT, T, [(hT, mul1(0), add1(0))]), (ctxT, L, [(ctxT, mul1(1), add1(1))]),
                         (memT, MEM, [(memT, gain(vB, ROWS_B["mem_norm"]), None)])], [EPS1, EPS1, EPS2])

        with ExitStack() as local:
            qT = sb("na_q", [P, T], on=local)
            kT = sb("na_k", [P, T + L], on=local)
            v = sb("na_v", [P, TT + LT, P], on=local)
            bias = sb("na_bias_now", [P, 2, 16 * GRID_W], on=local)
            zeros = sb("na_zeros", [P, L], on=local)
            colmask = sb("na_colmask", [P, GRID_W], on=local)
            evac_qkv, pair_out, mask_in, na_v = sem("na_evac"), sem("na_pair_out"), sem("na_mask_in"), sem("na_chain")
            units = []
            for h in range(2):
                for t in range(TT):
                    off = (NA_KH - 1 - 2 * t) * GRID_W
                    hp = slice(64 * h, 64 * h + 64)
                    units.append(dict(q=qT[hp, t * P:(t + 1) * P], k=[(kT[hp, 0:T], T), (kT[hp, T:T + L], L)], sink=None,
                                      bias=[bias[:, h, off:off + T], None], v=[v[:, b, hp] for b in range(TT + LT)],
                                      out=ps[hp, 6, t * P:(t + 1) * P]))
            a = Attention("na", local, units)
            PAIRS = NA_H // 2
            with nc.Block() as block:
                @block.sync
                def _(sp):
                    sp.dma_start(colmask[:, :], io["const_colmask"]).then_inc(mask_in, 16)
                    with sp.Fori(0, PAIRS) as i:
                        for u in range(3):
                            load_weights(sp, u, i, (wslot[:, u, :, :], weights(io["w_in"], i * P + u * NA_H * DH)))

                @block.tensor
                def _(pe):
                    pe.sem_inc(evac_qkv, 5)
                    pe.sem_inc(pair_out, 1)
                    with pe.Fori(0, PAIRS) as i:
                        pe.wait_ge(att_logit_ready, a.at(i))
                        pe.wait_ge(evac_qkv, 5 * i + 5)
                        for u, (bank, rhs) in enumerate([(ps[:, 0, :], hT), (ps[:, 1, :], hT)]):
                            weights_in(pe, u, i)
                            for k in range(KC):
                                mm = pe.matmul(bank, wslot[:, u, k, :], rhs[:, k, :], start=k == 0, stop=k == KC - 1)
                            if u == 0:
                                mm.then_inc(mm_done[0], 1)
                        for k in range(KC):
                            mm = pe.matmul(ps[:, 2, 0:L], wslot[:, 1, k, :], ctxT[:, k, :], start=k == 0, stop=k == KC - 1)
                        mm.then_inc(mm_done[1], 1)
                        weights_in(pe, 2, i)
                        for t in range(TT + LT):
                            src, c = (hT, t) if t < TT else (ctxT, t - TT)
                            bank = ps[:, 3, t * P:(t + 1) * P] if t < TT else ps[:, 2, L + c * P:L + (c + 1) * P]
                            for k in range(KC):
                                mm = pe.matmul(bank, src[:, k, c * P:(c + 1) * P], wslot[:, 2, k, :], start=k == 0, stop=k == KC - 1)
                        mm.then_inc(mm_done[2], 1)
                        pe.wait_ge(evac_qkv, 5 * i + 10)
                        att_pe(pe, a, i, lambda u: pe.wait_ge(pair_out, i + 1) if u == 0 else None)

                @block.scalar
                def _(act):
                    with act.Fori(0, PAIRS) as i:
                        act.wait_ge(att_weighted, a.at(i))
                        act.wait_ge(mm_done[0], turns[0] + i + 1)
                        act.activation(qT[:, :], ps[:, 0, :], ACT.Copy, scale=DH ** -0.5).then_inc(evac_qkv, 1)
                        act.wait_ge(mm_done[2], turns[2] + i + 1)
                        act.activation(kT[:, T:T + L], ps[:, 2, 0:L], ACT.Copy).then_inc(evac_qkv, 1)
                        act.activation(v[:, TT:TT + LT, :].rearrange("p t n -> p (t n)"), ps[:, 2, L:2 * L], ACT.Copy).then_inc(evac_qkv, 1)
                        att_act(act, a, i)
                        act.wait_ge(att_weighted, a.at(i) + a.n)
                        act.activation(yT[:, i, :], ps[:, 6, :], ACT.Copy).then_inc(pair_out, 1)

                @block.vector
                def _(dve):
                    link = Chain(dve, na_v)
                    dve.wait_ge(mask_in, 16)
                    link(dve.memset(zeros[:, :], 0.0))
                    with dve.Fori(0, PAIRS) as i:
                        link.loop(i, att_links(a) + 1)
                        link(dve.tensor_tensor(bias[:, :, :].rearrange("p h (r c) -> p (h r) c", c=GRID_W)[:, :, ::-1],
                                               na_bias[:, ds(2 * i, 2), :, :].rearrange("p h r c -> p (h r) c"),
                                               colmask[:, :].unsqueeze(1).broadcast_to([P, 32, GRID_W]), ALU.add))
                        dve.wait_ge(att_weighted, a.at(i))
                        dve.wait_ge(mm_done[1], turns[1] + i + 1)
                        dve.tensor_copy(kT[:, 0:T], ps[:, 1, :]).then_inc(evac_qkv, 1)
                        dve.wait_ge(mm_done[2], turns[2] + i + 1)
                        dve.tensor_copy(v[:, 0:TT, :].rearrange("p t n -> p (t n)"), ps[:, 3, :]).then_inc(evac_qkv, 1)
                        att_dve(dve, a, i, link, zeros)
                    link.end(PAIRS)
            end_ring(3, PAIRS)
            a.end(PAIRS)
        na_stack.close()
        with ExitStack() as local:
            pairs = sb("hg_pairs", [P, 2, LEVELS + 1, CH], on=local)
            go = sb("hg_go", [P, 2, T], on=local)
            q = sb("hg_q", [P, T], on=local)
            gate = sb("hg_gate", [P, T], on=local)
            v = sb("hg_v", [P, TT + LT, P], on=local)
            f = sb("hg_f", [P, 2, T + L], on=local)
            key = sb("hg_key", [P, 2, T + L], on=local)
            b = sb("hg_b", [P, 2, T + L], on=local)
            cut = sb("hg_cut", [P, LEVELS, T], on=local)
            kd = sb("hg_kd", [P, T + L], on=local)
            eb = sb("hg_eb", [P, 2, T], on=local)
            qe = sb("hg_qe", [P, 2, T], on=local)
            kdT = sb("hg_kdT", [P, TT + LT, P], on=local)
            masked = sb("hg_masked", [P, 2, LEVELS + 1, CH], on=local)
            at_ = sb("hg_at", [P, 2, NCH, CH], on=local)
            state = sb("hg_state", [P, 2, NCH, P], on=local)
            cur = sb("hg_cur", [P, 5], on=local)
            sq = sb("hg_sq", [P, T], on=local)
            consts_in, hg_v, lb_ready = sem("hg_consts_in"), sem("hg_chain"), sem("hg_lb_ready")
            HG_LINKS = 1 + 1 + 1 + 2 * (1 + (NCH - 2) + NCH) + 2
            evac_hg, gates, logs, args, exps, cuts = sem("hg_evac"), sem("hg_gates"), sem("hg_logs"), sem("hg_args"), sem("hg_exps"), sem("hg_cuts")
            multiplied, masked_ready, kd_ready, turned, kdT_ready, states_summed = (sem("hg_multiplied"), sem("hg_masked_ready"), sem("hg_kd_ready"),
                                                                           sem("hg_turned"), sem("hg_kdT_ready"), sem("hg_states_summed"))
            states_ready, read_out, squared, summed, meaned, rooted, head_done = (sem("hg_states_ready"), sem("hg_read_out"), sem("hg_squared"), sem("hg_summed"),
                                                                       sem("hg_meaned"), sem("hg_rooted"), sem("hg_head_done"))
            COL0 = 3 * NA_H * DH
            HW = HG_H * DK
            order = [list(range(NCH)), list(range(NCH))[::-1]]
            last_of = [lambda c: c * CH + CH - 1, lambda c: c * CH]

            def halves(x, n, d):
                half = CH >> (n + 1)
                y = x.rearrange("p (b e j) -> p b e j", e=2, j=half)
                lo, hi = y[:, :, 0, :], y[:, :, 1, :]
                return (hi, lo, lo[:, :, half - 1:half]) if d == 0 else (lo, hi, hi[:, :, 0:1])

            with nc.Block() as block:
                @block.sync
                def _(sp):
                    sp.dma_start(pairs[:, :, :, :].rearrange("p a l t -> p (a l t)"), io["const_pairs"]).then_inc(consts_in, 16)
                    sp.dma_start(go[:, :, :].rearrange("p a t -> p (a t)"), io["const_go"]).then_inc(consts_in, 16)
                    with sp.Fori(0, HG_H) as i:
                        for u in range(5):
                            load_weights(sp, u, i, (wslot[:, u, :, :], weights(io["w_in"], i * DK + (COL0 + u * HW))))

                @block.tensor
                def _(pe):
                    pe.sem_inc(head_done, 1)
                    pe.sem_inc(masked_ready, 1)
                    with pe.Fori(0, HG_H) as i:
                        pe.wait_ge(head_done, i + 1)
                        for u, bank in ((0, 0), (1, 1), (2, 2)):
                            weights_in(pe, u, i)
                            for k in range(KC):
                                mm = pe.matmul(ps[:, bank, :], wslot[:, u, k, :], hT[:, k, :], start=k == 0, stop=k == KC - 1)
                            if u:
                                for k in range(KC):
                                    mm = pe.matmul(ps[:, 3, (u - 1) * L:u * L], wslot[:, u, k, :], ctxT[:, k, :], start=k == 0, stop=k == KC - 1)
                            mm.then_inc(mm_done[u], 1)
                        weights_in(pe, 3, i)
                        for t in range(TT + LT):
                            src, c = (hT, t) if t < TT else (ctxT, t - TT)
                            bank = ps[:, 4, t * P:(t + 1) * P] if t < TT else ps[:, 5, c * P:(c + 1) * P]
                            for k in range(KC):
                                mm = pe.matmul(bank, src[:, k, c * P:(c + 1) * P], wslot[:, 3, k, :], start=k == 0, stop=k == KC - 1)
                        mm.then_inc(mm_done[3], 1)
                        weights_in(pe, 4, i)
                        for k in range(KC):
                            mm = pe.matmul(ps[:, 6, :], wslot[:, 4, k, :], hT[:, k, :], start=k == 0, stop=k == KC - 1)
                        mm.then_inc(mm_done[4], 1)
                        pe.wait_ge(evac_hg, 4 * i + 4)
                        for d in range(2):
                            pe.wait_ge(kd_ready, 2 * i + d + 1)
                            if d:
                                pe.wait_ge(kdT_ready, 4 * i + 2)
                            for t in range(TT + LT):
                                mm = pe.transpose(ps[:, 4 + t // 4, t % 4 * P:(t % 4 + 1) * P], kd[:, t * P:(t + 1) * P], ident[:, :])
                            mm.then_inc(turned, 1)
                            pe.wait_ge(kdT_ready, 4 * i + 2 * d + 2)
                            if d:
                                pe.wait_ge(states_ready, 2 * i + 1)
                            for c in order[d][:-1]:
                                pe.matmul(ps[:, 6, c * P:(c + 1) * P], kdT[:, c, :], v[:, c, :], start=True, stop=True)
                            c = order[d][-1]
                            for t in range(LT):
                                mm = pe.matmul(ps[:, 6, c * P:(c + 1) * P], kdT[:, TT + t, :], v[:, TT + t, :], start=t == 0, stop=t == LT - 1)
                            mm.then_inc(states_summed, 1)
                            pe.wait_ge(cuts, 2 * i + d + 1)
                            for c in range(NCH):
                                n = NCH * d + c
                                tok_ = slice(c * CH, (c + 1) * CH)
                                pe.wait_ge(masked_ready, 8 * i + max(n - 1, 0) + 1)
                                for l in range(LEVELS + 1):
                                    lhs, rhs = (cut[:, l, tok_], cut[:, l, tok_]) if l < LEVELS else (key[:, d, tok_], q[:, tok_])
                                    mm = pe.matmul(ps[:, 2 * (n % 2) + l // 4, (l % 4) * P:(l % 4 + 1) * P], lhs, rhs, start=True, stop=True)
                                mm.then_inc(multiplied, 1)
                        pe.wait_ge(masked_ready, 8 * i + 9)
                        pe.wait_ge(states_ready, 2 * i + 2)
                        for c in range(NCH):
                            for d in range(2):
                                pe.matmul(ps[:, 7, c * CH:(c + 1) * CH], v[:, c, :], at_[:, d, c, :], start=d == 0, stop=False)
                                mm = pe.matmul(ps[:, 7, c * CH:(c + 1) * CH], state[:, d, c, :], qe[:, d, c * CH:(c + 1) * CH], start=False, stop=d == 1)
                        mm.then_inc(read_out, 1)
                        pe.wait_ge(squared, i + 1)
                        pe.matmul(ps[:, 6, :], ones[:, :], sq[:, :], start=True, stop=True).then_inc(summed, 1)

                @block.scalar
                def _(act):
                    act.activation(lb[:, 0, :, :], lb[:, 0, :, :], ACT.Sigmoid).then_inc(lb_ready, 1)
                    with act.Fori(0, HG_H) as i:
                        act.wait_ge(head_done, i + 1)
                        act.wait_ge(mm_done[0], turns[0] + i + 1)
                        act.activation(q[:, :], ps[:, 0, :], ACT.Silu).then_inc(evac_hg, 1)
                        act.wait_ge(mm_done[4], turns[4] + i + 1)
                        act.activation(gate[:, :], ps[:, 6, :], ACT.Silu).then_inc(evac_hg, 1)
                        for d in range(2):
                            act.activation(f[:, d, 0:T], ps[:, 1 + d, :], ACT.Sigmoid)
                        act.activation(f[:, :, T:T + L], ps[:, 3, :].rearrange("p (d n) -> p d n", d=2), ACT.Sigmoid).then_inc(gates, 1)
                        act.wait_ge(gates, 2 * i + 2)
                        act.activation(f[:, :, :], f[:, :, :], ACT.Ln).then_inc(logs, 1)
                        for d in range(2):
                            act.wait_ge(args, 4 * i + 2 * d + 1)
                            act.activation(kd[:, :], kd[:, :], ACT.Exp).then_inc(exps, 1)
                            act.activation(eb[:, d, :], b[:, d, 0:T], ACT.Exp).then_inc(exps, 1)
                            act.wait_ge(args, 4 * i + 2 * d + 2)
                            act.activation(cut[:, :, :], cut[:, :, :], ACT.Exp).then_inc(exps, 1)
                            act.wait_ge(turned, 2 * i + d + 1)
                            if d:
                                act.wait_ge(states_summed, 2 * i + 1)
                            act.activation(kdT[:, 0:TT, :].rearrange("p t n -> p (t n)"), ps[:, 4, :], ACT.Copy).then_inc(kdT_ready, 1)
                            act.activation(kdT[:, TT:, :].rearrange("p t n -> p (t n)"), ps[:, 5, 0:LT * P], ACT.Copy).then_inc(kdT_ready, 1)
                        act.wait_ge(read_out, i + 1)
                        act.activation(sq[:, :], ps[:, 7, :], ACT.Square).then_inc(squared, 1)
                        act.wait_ge(meaned, i + 1)
                        act.activation(rstd[:, :], rstd[:, :], ACT.Sqrt).then_inc(rooted, 1)

                @block.vector
                def _(dve):
                    link = Chain(dve, hg_v)
                    dve.wait_ge(lb_ready, 1)
                    link(dve.tensor_scalar(lb[:, 1, :, :], lb[:, 0, :, :], -1.0, 1.0, ALU.mult, ALU.add))
                    lbs = lb[:, :, :, :].rearrange("p e d h -> p (e d) h")
                    dve.wait_ge(consts_in, 32)
                    with dve.Fori(0, HG_H) as i:
                        link.loop(i, HG_LINKS)
                        dve.tensor_copy(cur[:, 0:4], lbs[:, :, ds(i, 1)].rearrange("p a h -> p (a h)"))
                        link(dve.tensor_copy(cur[:, 4:5], vA[:, ds(i + ROWS_A["hg_norm"], 1)]))
                        dve.wait_ge(mm_done[3], turns[3] + i + 1)
                        dve.tensor_copy(v[:, 0:TT, :].rearrange("p t n -> p (t n)"), ps[:, 4, :]).then_inc(evac_hg, 1)
                        dve.tensor_copy(v[:, TT:, :].rearrange("p t n -> p (t n)"), ps[:, 5, 0:LT * P]).then_inc(evac_hg, 1)
                        dve.wait_ge(gates, 2 * i + 1)
                        for d in range(2):
                            last = dve.tensor_scalar(f[:, d, :], f[:, d, :], cur[:, 2 + d:3 + d], cur[:, d:d + 1], ALU.mult, ALU.add)
                        link(last)
                        dve.tensor_scalar(key[:, :, :], f[:, :, :], -1.0, 1.0, ALU.mult, ALU.add).then_inc(gates, 1)
                        dve.wait_ge(logs, i + 1)
                        for d in range(2):
                            go_ctx = go[:, 1, 0:1].broadcast_to([P, L])
                            flip = (lambda x: x) if d == 0 else (lambda x: x[:, ::-1])
                            dve.tensor_tensor_scan(flip(b[:, d, 0:T]), flip(go[:, d, :]), flip(f[:, d, 0:T]), 0.0, ALU.mult, ALU.add)
                            last = dve.tensor_tensor_scan(flip(b[:, d, T:T + L]), go_ctx, flip(f[:, d, T:T + L]), 0.0, ALU.mult, ALU.add)
                        link(last)
                        for d in range(2):
                            b4 = b[:, d, 0:T].rearrange("p (c j) -> p c j", j=CH)
                            end = b4[:, :, CH - 1:CH] if d == 0 else b4[:, :, 0:1]
                            ctx_end = b[:, d, T + L - 1:T + L] if d == 0 else b[:, d, T:T + 1]
                            if d:
                                dve.wait_ge(turned, 2 * i + 1)
                            dve.tensor_tensor(kd[:, 0:T].rearrange("p (c j) -> p c j", j=CH), end.broadcast_to([P, NCH, CH]), b4, ALU.subtract)
                            dve.tensor_tensor(kd[:, T:T + L], ctx_end.broadcast_to([P, L]), b[:, d, T:T + L], ALU.subtract).then_inc(args, 1)
                            if d:
                                dve.wait_ge(multiplied, 8 * i + 4)
                            for l in range(LEVELS):
                                bq, bk, mid = halves(b[:, d, 0:T], l, d)
                                oq, ok, _ = halves(cut[:, l, :], l, d)
                                wide = mid.broadcast_to(list(bq.shape))
                                dve.tensor_tensor(oq, bq, wide, ALU.subtract)
                                last = dve.tensor_tensor(ok, wide, bk, ALU.subtract)
                            last.then_inc(args, 1)
                            dve.wait_ge(exps, 6 * i + 3 * d + 1)
                            dve.tensor_tensor(kd[:, :], kd[:, :], key[:, d, :], ALU.mult).then_inc(kd_ready, 1)
                            dve.wait_ge(exps, 6 * i + 3 * d + 2)
                            dve.tensor_tensor(qe[:, d, :], eb[:, d, :], q[:, :], ALU.mult)
                            dve.wait_ge(exps, 6 * i + 3 * d + 3)
                            for l in range(LEVELS):
                                oq, ok, _ = halves(cut[:, l, :], l, d)
                                qq, _, _ = halves(q[:, :], l, d)
                                _, kk, _ = halves(key[:, d, 0:T], l, d)
                                dve.tensor_tensor(oq, oq, qq, ALU.mult)
                                last = dve.tensor_tensor(ok, ok, kk, ALU.mult)
                            last.then_inc(cuts, 1)
                            dve.wait_ge(states_summed, 2 * i + d + 1)
                            c0 = order[d][0]
                            link(dve.tensor_copy(state[:, d, c0, :], ps[:, 6, order[d][-1] * P:(order[d][-1] + 1) * P]))
                            for n, c in enumerate(order[d][:-1]):
                                nxt = order[d][n + 1]
                                e = last_of[d](c)
                                ins = dve.scalar_tensor_tensor(state[:, d, nxt, :], state[:, d, c, :], eb[:, d, e:e + 1],
                                                               ps[:, 6, c * P:(c + 1) * P], ALU.mult, ALU.add)
                                if n < NCH - 2:
                                    link(ins)
                            ins.then_inc(states_ready, 1)
                            for c in range(NCH):
                                n = NCH * d + c
                                dve.wait_ge(multiplied, 8 * i + n + 1)
                                link(dve.tensor_tensor(masked[:, n % 2, :, :].rearrange("p l t -> p (l t)"), ps[:, 2 * (n % 2):2 * (n % 2) + 2, :].rearrange("p b n -> p (b n)"),
                                                       pairs[:, d, :, :].rearrange("p l t -> p (l t)"), ALU.mult))
                                dve.tensor_reduce(at_[:, d, c, :], masked[:, n % 2, :, :].rearrange("p l t -> p t l"), AX.X, ALU.add).then_inc(masked_ready, 1)
                        dve.wait_ge(summed, i + 1)
                        dve.tensor_scalar(rstd[:, :], ps[:, 6, :], 1.0 / DK, EPS1, ALU.mult, ALU.add).then_inc(meaned, 1)
                        dve.wait_ge(rooted, i + 1)
                        link(dve.reciprocal(rstd[:, :], rstd[:, :]))
                        link(dve.scalar_tensor_tensor(sq[:, :], ps[:, 7, :], cur[:, 4:5], rstd[:, :], ALU.mult, ALU.mult))
                        dve.tensor_tensor(yT[:, ds(i + NA_H * DH // P, 1), :].rearrange("p a t -> p (a t)"), sq[:, :], gate[:, :], ALU.mult).then_inc(head_done, 1)
                    link.end(HG_H)
            end_ring(5, HG_H)
    def residual_block(n, tiles, pieces, gate):
        per = 4
        with nc.Block() as block:
            @block.sync
            def _(sp):
                with sp.Fori(0, n // per) as i:
                    for u in range(per):
                        load_weights(sp, u, i, *tiles(u, i * (per * P) + u * P))

            @block.tensor
            def _(pe):
                with pe.Fori(0, n // per) as i:
                    for u in range(per):
                        project(pe, u, i, ps[:, u, :], yT, pieces)

            @block.vector
            def _(dve):
                with dve.Fori(0, n // per) as i:
                    for u in range(per):
                        projected(dve, u, i)
                        x = xT[:, ds(i * per + u, 1), :].rearrange("p a t -> p (a t)")
                        if gate is None:
                            dve.tensor_tensor(x, ps[:, u, :], x, ALU.add).then_inc(evacuated[u], 1)
                        else:
                            dve.scalar_tensor_tensor(x, ps[:, u, :], gate(i * per + u), x, ALU.mult, ALU.add).then_inc(evacuated[u], 1)
        end_ring(per, n // per, pieces, True)

    plain = lambda w: (lambda u, c0: [(wslot[:, u, :, :], weights(w, c0))])
    residual_block(KC, plain(io["w_out"]), 1, lambda j: mod[:, ds(j + 2 * KC, 1), 0])

    rms_block("n2", [(xT, T, [(hT, lambda k: gain2[:, k:k + 1], lambda k: mod[:, 3 * KC + k, 0:1])])], [EPS1])
    with ExitStack() as local:
        RING = TOPK
        htok = sb("pe_htok", [P, TT, D], on=local)
        ring = sb("pe_ring", [P, RING, D], on=local)
        qT = sb("pe_qT", [P, 2, T], on=local)
        keys = sb("pe_keys", [P, 2, P], on=local)
        keysT = sb("pe_keysT", [P, 2, P], on=local)
        s = sb("pe_s", [P, 2, TT, NKEYS], on=local)
        top = sb("pe_top", [P, 2, TT, TOPK], on=local)
        itop = sb("pe_itop", [P, 2, TT, TOPK], U32, on=local)
        itopf = sb("pe_itopf", [P, 2, TT, TOPK], on=local)
        cand = sb("pe_cand", [P, TT, TOPK, TOPK], on=local)
        best = sb("pe_best", [P, TT, TOPK], on=local)
        pos = sb("pe_pos", [P, TT, TOPK], U32, on=local)
        place = sb("pe_place", [P, 2, TT, TOPK], U32, on=local)
        placef = sb("pe_placef", [P, 2, TT, TOPK], on=local)
        pick = sb("pe_pick", [P, 2, TT * TOPK, TOPK], on=local)
        picked = sb("pe_picked", [P, 2, TT, TOPK], on=local)
        idx = sb("pe_idx", [P, 2, TT * TOPK], U32, on=local)
        g = sb("pe_g", [P, 2, TT, TOPK], on=local)
        soft = sb("pe_soft", [P, TT, TOPK], on=local)
        total = sb("pe_total", [P, TT], on=local)
        dots = sb("pe_dots", [P, TT * TOPK], on=local)
        act_ = sb("pe_act", [P, TT * TOPK], on=local)
        wgt = sb("pe_wgt", [P, TT * TOPK], on=local)
        DIAGS = 4
        diag = sb("pe_diag", [P, DIAGS, P], on=local)
        iota16 = sb("pe_iota16", [P, TOPK], on=local)
        acc = yT[:, :, :].rearrange("p (t h) n -> p t (h n)", t=TT)
        h_turned, h_left = sem("pe_h_turned"), sem("pe_h_left")
        with nc.Block() as block:
            @block.tensor
            def _(pe):
                for t in range(TT):
                    if t >= 2:
                        pe.wait_ge(h_left, t - 1)
                    for k in range(KC):
                        mm = pe.transpose(ps[:, 2 * (t % 2) + k // 4, k % 4 * P:(k % 4 + 1) * P], hT[:, k, t * P:(t + 1) * P], ident[:, :])
                    mm.then_inc(h_turned, 1)

            @block.scalar
            def _(act):
                for t in range(TT):
                    act.wait_ge(h_turned, t + 1)
                    act.activation(htok[:, t, :], ps[:, 2 * (t % 2):2 * (t % 2) + 2, :].rearrange("p b n -> p (b n)"), ACT.Copy).then_inc(h_left, 1)

        land = [sem(f"pe_land{k}") for k in range(RING)]
        dot_done, v_used, gelu_done, wgt_done, diag_done, added = (sem("pe_dot_done"), sem("pe_v_used"), sem("pe_gelu_done"),
                                                            sem("pe_wgt_done"), sem("pe_diag_done"), sem("pe_added"))
        keys_in, keys_turned, q_ready, scored, s_ready, top_done = (sem("pe_keys_in"), sem("pe_keys_turned"), sem("pe_q_ready"),
                                                            sem("pe_scored"), sem("pe_s_ready"), sem("pe_top_done"))
        soft_arg, soft_exp, idx_ready, pe_v, iota_in = sem("pe_soft_arg"), sem("pe_soft_exp"), sem("pe_idx_ready"), sem("pe_chain"), sem("pe_iota_in")
        BLOCKS = [("u", 0), ("u", 1), ("v", 0), ("u", 2), ("v", 1), ("u", 3), ("v", 2), ("v", 3)]
        CREDIT = TOPK
        PER = TT * TOPK
        NBLK = len(BLOCKS)
        HEAD_LINKS = 5 + 6 + 7

        def consumed(eng, kind, h, t, k):
            eng.wait_ge(dot_done if kind == "u" else v_used, h * PER + (t * TOPK + k + 1 + (CREDIT if kind == "v" else 0)))

        def arrived(eng, kind, h, t, k):
            eng.wait_ge(land[k], h * (16 * NBLK) + 16 * (BLOCKS.index((kind, t)) + 1))

        with nc.Block() as block:
            @block.sync
            def _(sp):
                sp.dma_start(iota16[:, :], io["const_iota16"]).then_inc(iota_in, 16)

                def load_head(r, head):
                    for side in range(2):
                        load_weights(sp, side, r, (wslot[:, side, :, :], weights(io["wq"], head * (2 * P) + side * P)))
                    sp.wait_ge(keys_turned, r)
                    sp.dma_start(keys[:, :, :], io["keys"][ds(head * (2 * P), 2 * P), :].rearrange("(s k) d -> k s d", s=2)).then_inc(keys_in, 16)

                load_head(0, 0)
                with sp.Fori(0, PE_H // 2) as i:
                    after = (i * 2 + 2) % PE_H
                    load_head(i * 2 + 1, i * 2 + 1)
                    load_head(i * 2 + 2, after)

            @block.gpsimd
            def _(pool):
                def gathers(h, par):
                    for n, (kind, t) in enumerate(BLOCKS):
                        if n == 0:
                            pool.wait_ge(idx_ready, h + 1)
                        for k in range(TOPK):
                            if n:
                                consumed(pool, BLOCKS[n - 1][0], h, BLOCKS[n - 1][1], k)
                            else:
                                pool.wait_ge(v_used, h * PER + k + 1)
                            j = t * TOPK + k
                            pool.nop(nofuse=True)
                            pool.indirect_dma_start(ring[:, k, :], None, io[kind], bass.IndirectOffsetOnAxis(idx[:, par, j:j + 1], 0)).then_inc(land[k], 16)

                with pool.Fori(0, PE_H // 2) as i:
                    for par in range(2):
                        gathers(i * 2 + par, par)

            @block.tensor
            def _(pe):
                def route(r):
                    pe.wait_ge(q_ready, r * 3)
                    for side in range(2):
                        weights_in(pe, side, r)
                        for k in range(KC):
                            mm = pe.matmul(ps[:, 4 + side, :], wslot[:, side, k, :], hT[:, k, :], start=k == 0, stop=k == KC - 1)
                        mm.then_inc(mm_done[side], 1)
                    pe.wait_ge(keys_in, r * 16 + 16)
                    pe.wait_ge(s_ready, r * 2)
                    for side in range(2):
                        mm = pe.transpose(ps[:, 6, side * P:(side + 1) * P], keys[:, side, :], ident[:, :])
                    mm.then_inc(keys_turned, 1)
                    pe.wait_ge(q_ready, r * 3 + 3)
                    for side in range(2):
                        for t in range(TT):
                            mm = pe.matmul(ps[:, 6 + side, t * P:(t + 1) * P], qT[:, side, t * P:(t + 1) * P], keysT[:, side, :], start=True, stop=True)
                    mm.then_inc(scored, 1)

                def sum_v(h, t):
                    pe.wait_ge(added, h * TT + t + 1)
                    for k in range(TOPK):
                        arrived(pe, "v", h, t, k)
                        pe.wait_ge(diag_done, h * PER + t * TOPK + k + 1)
                        for half in range(2):
                            mm = pe.matmul(ps[:, 2 * (t % 2) + half, :], diag[:, k % DIAGS, :], ring[:, k, half * 512:(half + 1) * 512],
                                           start=k == 0, stop=k == TOPK - 1)
                        mm.then_inc(v_used, 1)

                pe.sem_inc(v_used, CREDIT)
                route(0)
                with pe.Fori(0, PE_H // 2) as i:
                    for par in range(2):
                        route(i * 2 + par + 1)
                        for t in range(TT):
                            sum_v(i * 2 + par, t)

            @block.scalar
            def _(act):
                def route(r):
                    for side in range(2):
                        act.wait_ge(mm_done[side], turns[side] + r + 1)
                        act.activation(qT[:, side, :], ps[:, 4 + side, :], ACT.Copy).then_inc(q_ready, 1)
                    act.wait_ge(keys_turned, r + 1)
                    act.activation(keysT[:, :, :].rearrange("p s n -> p (s n)"), ps[:, 6, 0:2 * P], ACT.Copy).then_inc(q_ready, 1)
                    act.wait_ge(scored, r + 1)
                    act.wait_ge(top_done, r)
                    for side in range(2):
                        act.activation(s[:, side, :, :].rearrange("p t n -> p (t n)"), ps[:, 6 + side, :], ACT.Copy).then_inc(s_ready, 1)

                def route_exp(r):
                    act.wait_ge(soft_arg, r + 1)
                    act.activation(soft[:, :, :], soft[:, :, :], ACT.Exp).then_inc(soft_exp, 1)

                def gelu(h, t):
                    act.wait_ge(dot_done, h * PER + (t + 1) * TOPK)
                    act.activation(act_[:, t * TOPK:(t + 1) * TOPK], dots[:, t * TOPK:(t + 1) * TOPK], ACT.Gelu).then_inc(gelu_done, 1)

                def diags(h, t):
                    act.wait_ge(wgt_done, h * TT + t + 1)
                    for k in range(TOPK):
                        n = t * TOPK + k
                        act.wait_ge(v_used, h * PER + (n + 1 + CREDIT - DIAGS))
                        act.activation(diag[:, k % DIAGS, :], ident[:, :], ACT.Copy, scale=wgt[:, n:n + 1]).then_inc(diag_done, 1)

                route(0)
                route_exp(0)
                with act.Fori(0, PE_H // 2) as i:
                    for par in range(2):
                        h = i * 2 + par
                        gelu(h, 0)
                        route(h + 1)
                        gelu(h, 1)
                        diags(h, 0)
                        gelu(h, 2)
                        diags(h, 1)
                        gelu(h, 3)
                        route_exp(h + 1)
                        diags(h, 2)
                        diags(h, 3)

            @block.vector
            def _(dve):
                link = Chain(dve, pe_v)
                tiles = [(side, t) for side in range(2) for t in range(TT)]

                def best_keys(r):
                    dve.wait_ge(s_ready, r * 2 + 2)
                    for lo in (0, 8):
                        dve.nop(nofuse=True)
                        for side, t in tiles:
                            last = dve.max(top[:, side, t, lo:lo + 8], s[:, side, t, :])
                        link(last)
                        dve.nop(nofuse=True)
                        for side, t in tiles:
                            last = dve.max_index(itop[:, side, t, lo:lo + 8], top[:, side, t, lo:lo + 8], s[:, side, t, :])
                        if lo == 0:
                            link(last)
                            dve.nop(nofuse=True)
                            for side, t in tiles:
                                last = dve.match_replace(s[:, side, t, :], top[:, side, t, 0:8], s[:, side, t, :], -3e38)
                            link(last)
                        else:
                            link(last)
                    dve.tensor_copy(itopf[:, :, :, :], itop[:, :, :, :]).then_inc(top_done, 1)

                def best_pairs(r):
                    link(dve.tensor_tensor(cand[:, :, :, :], top[:, 0, :, :].unsqueeze(3).broadcast_to([P, TT, TOPK, TOPK]),
                                           top[:, 1, :, :].unsqueeze(2).broadcast_to([P, TT, TOPK, TOPK]), ALU.add))
                    flat = [cand[:, t, :, :].rearrange("p a b -> p (a b)") for t in range(TT)]
                    for lo in (0, 8):
                        dve.nop(nofuse=True)
                        for t in range(TT):
                            last = dve.max(best[:, t, lo:lo + 8], flat[t])
                        link(last)
                        dve.nop(nofuse=True)
                        for t in range(TT):
                            last = dve.max_index(pos[:, t, lo:lo + 8], best[:, t, lo:lo + 8], flat[t])
                        link(last)
                        if lo == 0:
                            dve.nop(nofuse=True)
                            for t in range(TT):
                                last = dve.match_replace(flat[t], best[:, t, 0:8], flat[t], -3e38)
                            link(last)
                    dve.tensor_tensor(soft[:, :, :], best[:, :, :], best[:, :, 0:1].broadcast_to([P, TT, TOPK]), ALU.subtract).then_inc(soft_arg, 1)

                def experts(r, par):
                    dve.tensor_scalar(place[:, 0, :, :], pos[:, :, :], 4, None, ALU.logical_shift_right)
                    link(dve.tensor_scalar(place[:, 1, :, :], pos[:, :, :], TOPK - 1, None, ALU.bitwise_and))
                    link(dve.tensor_copy(placef[:, :, :, :], place[:, :, :, :]))
                    for side in range(2):
                        last = dve.tensor_tensor(pick[:, side, :, :], placef[:, side, :, :].rearrange("p t k -> p (t k)").unsqueeze(2).broadcast_to([P, PER, TOPK]),
                                                 iota16[:, :].unsqueeze(1).broadcast_to([P, PER, TOPK]), ALU.is_equal)
                    link(last)
                    for side in range(2):
                        p4 = pick[:, side, :, :].rearrange("p (t k) a -> p t k a", t=TT)
                        last = dve.tensor_tensor(p4, p4, itopf[:, side, :, :].unsqueeze(2).broadcast_to([P, TT, TOPK, TOPK]), ALU.mult)
                    link(last)
                    for side in range(2):
                        last = dve.tensor_reduce(picked[:, side, :, :].rearrange("p t k -> p (t k)"), pick[:, side, :, :], AX.X, ALU.add)
                    link(last)
                    dve.wait_ge(soft_exp, r + 1)
                    link(dve.tensor_reduce(total[:, :], soft[:, :, :], AX.X, ALU.add))
                    link(dve.reciprocal(total[:, :], total[:, :]))
                    dve.tensor_tensor(g[:, par, :, :], soft[:, :, :], total[:, :].unsqueeze(2).broadcast_to([P, TT, TOPK]), ALU.mult)
                    flat = lambda x: x.rearrange("p t k -> p (t k)")
                    dve.scalar_tensor_tensor(idx[:, par, :], flat(picked[:, 0, :, :]), float(NKEYS), flat(picked[:, 1, :, :]), ALU.mult, ALU.add).then_inc(idx_ready, 1)

                def dot(h, t):
                    for k in range(TOPK):
                        arrived(dve, "u", h, t, k)
                        j = t * TOPK + k
                        dve.tensor_tensor_reduce(ring[:, k, :], ring[:, k, :], htok[:, t, :], 1.0, 0.0, ALU.mult, ALU.add, dots[:, j:j + 1]).then_inc(dot_done, 1)

                def weigh(h, t, par):
                    dve.wait_ge(gelu_done, h * TT + t + 1)
                    dve.tensor_tensor(wgt[:, t * TOPK:(t + 1) * TOPK], act_[:, t * TOPK:(t + 1) * TOPK], g[:, par, t, :], ALU.mult).then_inc(wgt_done, 1)

                def add_v(h, t):
                    dve.wait_ge(v_used, h * PER + (t * TOPK + TOPK + CREDIT))
                    dve.tensor_tensor(acc[:, t, :], ps[:, 2 * (t % 2):2 * (t % 2) + 2, :].rearrange("p b n -> p (b n)"), acc[:, t, :], ALU.add).then_inc(added, 1)

                dve.sem_inc(added, 2)
                dve.wait_ge(iota_in, 16)
                link(dve.memset(acc, 0.0))
                best_keys(0)
                best_pairs(0)
                link(dve.memset(total[:, :], 0.0))
                experts(0, 0)
                with dve.Fori(0, PE_H // 2) as i:
                    link.loop(i, 2 * HEAD_LINKS)
                    for par in range(2):
                        h = i * 2 + par
                        dot(h, 0)
                        dot(h, 1)
                        weigh(h, 0, par)
                        best_keys(h + 1)
                        dot(h, 2)
                        weigh(h, 1, par)
                        add_v(h, 0)
                        best_pairs(h + 1)
                        dot(h, 3)
                        weigh(h, 2, par)
                        add_v(h, 1)
                        experts(h + 1, 1 - par)
                        weigh(h, 3, par)
                        add_v(h, 2)
                        add_v(h, 3)
                link.end(PE_H // 2)
        end_ring(2, PE_H + 1)
        o_turned, o_left = sem("pe_o_turned"), sem("pe_o_left")
        with nc.Block() as block:
            @block.tensor
            def _(pe):
                for k in range(KC):
                    if k >= 4:
                        pe.wait_ge(o_left, k - 3)
                    for t in range(TT):
                        mm = pe.transpose(ps[:, k % 4, t * P:(t + 1) * P], acc[:, t, k * P:(k + 1) * P], ident[:, :])
                    mm.then_inc(o_turned, 1)

            @block.vector
            def _(dve):
                for k in range(KC):
                    dve.wait_ge(o_turned, k + 1)
                    dve.scalar_tensor_tensor(xT[:, k, :], ps[:, k % 4, :], mod[:, 5 * KC + k, 0:1], xT[:, k, :], ALU.mult, ALU.add).then_inc(o_left, 1)
    rms_block("nf", [(xT, T, [(xT, gain(vA, ROWS_A["norm_f"]), None)])], [EPS1])

    def memory_attention(name, layer, w_q, q0):
        PAIRS = 2
        with ExitStack() as local:
            qT = sb(f"{name}_q", [P, T], on=local)
            kT = sb(f"{name}_k", [P, MEM], on=local)
            v = sb(f"{name}_v", [P, MEM // P, P], on=local)
            zeros = sb(f"{name}_zeros", [P, MEM], on=local)
            evac, pair_out, chain = sem(f"{name}_evac"), sem(f"{name}_pair_out"), sem(f"{name}_chain")
            units = [dict(q=qT[64 * h:64 * h + 64, t * P:(t + 1) * P], k=[(kT[64 * h:64 * h + 64, :], MEM)], sink=None, bias=[None],
                          v=[v[:, m, 64 * h:64 * h + 64] for m in range(MEM // P)], out=ps[64 * h:64 * h + 64, 6, t * P:(t + 1) * P])
                     for h in range(2) for t in range(TT)]
            a = Attention(name, local, units)
            w_kv = io["mem_kv"][layer * D:(layer + 1) * D, :]
            with nc.Block() as block:
                @block.sync
                def _(sp):
                    with sp.Fori(0, PAIRS) as i:
                        for u, (w, c0) in enumerate([(w_q, q0), (w_kv, 0), (w_kv, 2 * P)]):
                            load_weights(sp, u, i, (wslot[:, u, :, :], weights(w, i * P + c0)))

                @block.tensor
                def _(pe):
                    pe.sem_inc(pair_out, 1)
                    with pe.Fori(0, PAIRS) as i:
                        pe.wait_ge(att_logit_ready, a.at(i))
                        for u, rhs, n in ((0, hT, T), (1, memT, MEM)):
                            weights_in(pe, u, i)
                            for k in range(KC):
                                mm = pe.matmul(ps[:, u, 0:n], wslot[:, u, k, :], rhs[:, k, :], start=k == 0, stop=k == KC - 1)
                            mm.then_inc(mm_done[u], 1)
                        weights_in(pe, 2, i)
                        for m in range(MEM // P):
                            for k in range(KC):
                                mm = pe.matmul(ps[:, 2, m * P:(m + 1) * P], memT[:, k, m * P:(m + 1) * P], wslot[:, 2, k, :], start=k == 0, stop=k == KC - 1)
                        mm.then_inc(mm_done[2], 1)
                        pe.wait_ge(evac, 3 * i + 3)
                        att_pe(pe, a, i, lambda u: pe.wait_ge(pair_out, i + 1) if u == 0 else None)

                @block.scalar
                def _(act):
                    with act.Fori(0, PAIRS) as i:
                        act.wait_ge(att_weighted, a.at(i))
                        projected(act, 0, i)
                        act.activation(qT[:, :], ps[:, 0, :], ACT.Copy, scale=DH ** -0.5).then_inc(evac, 1)
                        att_act(act, a, i)
                        act.wait_ge(att_weighted, a.at(i) + a.n)
                        act.activation(yT[:, i + CONV // P, :], ps[:, 6, :], ACT.Copy).then_inc(pair_out, 1)

                @block.vector
                def _(dve):
                    link = Chain(dve, chain)
                    link(dve.memset(zeros[:, :], 0.0))
                    with dve.Fori(0, PAIRS) as i:
                        link.loop(i, att_links(a))
                        dve.wait_ge(att_weighted, a.at(i))
                        projected(dve, 1, i)
                        dve.tensor_copy(kT[:, :], ps[:, 1, 0:MEM]).then_inc(evac, 1)
                        projected(dve, 2, i)
                        dve.tensor_copy(v[:, :, :].rearrange("p t n -> p (t n)"), ps[:, 2, 0:MEM]).then_inc(evac, 1)
                        att_dve(dve, a, i, link, zeros)
                    link.end(PAIRS)
            end_ring(3, PAIRS)
            a.end(PAIRS)

    def feed_forward(name, layer):
        per = 2
        with ExitStack() as local:
            hidden = sb(f"{name}_hidden", [P, FT, T], on=local)
            half = sb(f"{name}_half", [P, per, T], on=local)
            rows = slice(layer * D, (layer + 1) * D)
            with nc.Block() as block:
                @block.sync
                def _(sp):
                    with sp.Fori(0, FT // per) as i:
                        for u in range(2 * per):
                            w = io["gate" if u % 2 == 0 else "up"][rows, :]
                            load_weights(sp, u, i, (wslot[:, u, :, :], weights(w, i * (per * P) + u // 2 * P)))

                @block.tensor
                def _(pe):
                    with pe.Fori(0, FT // per) as i:
                        for u in range(2 * per):
                            project(pe, u, i, ps[:, u, :], hT)

                @block.scalar
                def _(act):
                    with act.Fori(0, FT // per) as i:
                        for n in range(per):
                            act.wait_ge(evacuated[2 * n + 1], left[2 * n + 1] + i)
                            projected(act, 2 * n, i)
                            act.activation(half[:, n, :], ps[:, 2 * n, :], ACT.Silu).then_inc(evacuated[2 * n], 1)

                @block.vector
                def _(dve):
                    with dve.Fori(0, FT // per) as i:
                        for n in range(per):
                            dve.wait_ge(evacuated[2 * n], left[2 * n] + i + 1)
                            projected(dve, 2 * n + 1, i)
                            dve.tensor_tensor(hidden[:, ds(i * per + n, 1), :].rearrange("p a t -> p (a t)"), half[:, n, :], ps[:, 2 * n + 1, :],
                                              ALU.mult).then_inc(evacuated[2 * n + 1], 1)
            end_ring(2 * per, FT // per, 1, True)
            wide = wring[:, 0:2 * FT * P].rearrange("p (s k n) -> p s k n", s=2, k=FT)
            down = io["down"][layer * D_FF:(layer + 1) * D_FF, :].rearrange("(k p) n -> p k n", p=P)
            with nc.Block() as block:
                @block.sync
                def _(sp):
                    with sp.Fori(0, KC // 2) as i:
                        for u in range(2):
                            load_weights(sp, u, i, (wide[:, u, :, :], down[:, :, ds(i * (2 * P) + u * P, P)]))

                @block.tensor
                def _(pe):
                    with pe.Fori(0, KC // 2) as i:
                        for u in range(2):
                            weights_in(pe, u, i)
                            pe.wait_ge(evacuated[u], left[u] + i)
                            for k in range(FT):
                                mm = pe.matmul(ps[:, u, :], wide[:, u, k, :], hidden[:, k, :], start=k == 0, stop=k == FT - 1)
                            mm.then_inc(mm_done[u], 1)

                @block.vector
                def _(dve):
                    with dve.Fori(0, KC // 2) as i:
                        for u in range(2):
                            projected(dve, u, i)
                            x = xT[:, ds(i * 2 + u, 1), :].rearrange("p a t -> p (a t)")
                            dve.tensor_tensor(x, ps[:, u, :], x, ALU.add).then_inc(evacuated[u], 1)
            end_ring(2, KC // 2, 1, True)

    rms_block("m0", [(xT, T, [(hT, gain(vB, ROWS_B["norm_mix"]), None)])], [EPS2])
    CT = CONV // P
    with ExitStack() as local:
        PAD = 2
        gated = sb("cv_gated", [P, PAD + T], on=local)
        uu = sb("cv_u", [P, T], on=local)
        conv = sb("cv_conv", [P, 2, T], on=local)
        taps = sb("cv_taps", [P, 3], on=local)
        cv_v = sem("cv_chain")
        with nc.Block() as block:
            @block.sync
            def _(sp):
                with sp.Fori(0, CT) as i:
                    for u, c0 in ((0, 0), (1, 2 * CONV), (2, CONV)):
                        load_weights(sp, u, i, (wslot[:, u, :, :], weights(io["a_in"], i * P + c0)))

            @block.tensor
            def _(pe):
                with pe.Fori(0, CT) as i:
                    for u in range(3):
                        project(pe, u, i, ps[:, u, :], hT)

            @block.scalar
            def _(act):
                with act.Fori(0, CT) as i:
                    act.wait_ge(evacuated[1], left[1] + i)
                    projected(act, 0, i)
                    act.activation(uu[:, :], ps[:, 0, :], ACT.Copy).then_inc(evacuated[0], 1)

            @block.vector
            def _(dve):
                link = Chain(dve, cv_v)
                link(dve.memset(gated[:, 0:PAD], 0.0))
                with dve.Fori(0, CT) as i:
                    link.loop(i, 3)
                    dve.tensor_copy(taps[:, :], vB[:, ROWS_B["conv"]:ROWS_B["conv"] + 3 * CT].rearrange("p (k j) -> p j k", k=3)[:, ds(i, 1), :].rearrange("p a k -> p (a k)"))
                    dve.wait_ge(evacuated[0], left[0] + i + 1)
                    projected(dve, 1, i)
                    dve.tensor_tensor(gated[:, PAD:], uu[:, :], ps[:, 1, :], ALU.mult).then_inc(evacuated[1], 1)
                    dve.wait_ge(evacuated[1], left[1] + i + 1)
                    link(dve.tensor_scalar(conv[:, 0, :], gated[:, 0:T], taps[:, 0:1], None, ALU.mult))
                    link(dve.scalar_tensor_tensor(conv[:, 1, :], gated[:, 1:T + 1], taps[:, 1:2], conv[:, 0, :], ALU.mult, ALU.add))
                    link(dve.scalar_tensor_tensor(conv[:, 0, :], gated[:, 2:T + 2], taps[:, 2:3], conv[:, 1, :], ALU.mult, ALU.add))
                    projected(dve, 2, i)
                    dve.tensor_tensor(yT[:, ds(i, 1), :].rearrange("p a t -> p (a t)"), conv[:, 0, :], ps[:, 2, :], ALU.mult).then_inc(evacuated[2], 1)
                link.end(CT)
        end_ring(3, CT, 1, True)
    memory_attention("ma0", 0, io["a_in"], 3 * CONV)
    residual_block(KC, plain(io["a_out"]), 1, None)
    rms_block("f0", [(xT, T, [(hT, gain(vB, ROWS_B["norm_ffn"]), None)])], [EPS2])
    feed_forward("ff0", 0)

    with ExitStack() as local:
        hkv = sb("sw_hkv", [P, KC, T], on=local)
        rms_block("m1", [(xT, T, [(hkv, gain(vB, ROWS_B["kv_norm"]), None), (hT, gain(vB, ROWS_B["norm_mix"] + KC), None)])], [EPS2])
        HALVES = KV_H // 2
        HPT = 2 * GROUP
        qT = sb("sw_q", [P, GROUP, T], on=local)
        kT = sb("sw_k", [P, T], on=local)
        v = sb("sw_v", [P, TT, P], on=local)
        bias = sb("sw_bias_now", [P, HPT, 2 * P], on=local)
        sink = sb("sw_sink_now", [P, HPT], on=local)
        evac, tile_out, sw_v = sem("sw_evac"), sem("sw_tile_out"), sem("sw_chain")
        units = []
        for j in range(GROUP):
            for kv in range(2):
                hp, h = slice(64 * kv, 64 * kv + 64), kv * GROUP + j
                for n in range(TT):
                    first = max(n - 1, 0)
                    w = (n + 1 - first) * P
                    units.append(dict(q=qT[hp, j, n * P:(n + 1) * P], k=[(kT[hp, first * P:(n + 1) * P], w)], sink=sink[:, h:h + 1],
                                      bias=[bias[:, h, 2 * P - w:2 * P]], v=[v[:, b, hp] for b in range(first, n + 1)],
                                      out=ps[hp, 6 + j % 2, n * P:(n + 1) * P]))
        a = Attention("sw", local, units)
        PERJ = 2 * TT
        QW = HPT * DH
        with nc.Block() as block:
            @block.sync
            def _(sp):
                with sp.Fori(0, HALVES) as i:
                    for j in range(GROUP):
                        load_weights(sp, j, i, *[(wslot[:, j, :, kv * DH:(kv + 1) * DH], weights(io["b_q"], i * QW + (kv * GROUP * DH + j * DH), DH))
                                                 for kv in range(2)])
                    for u, c0 in ((3, 0), (4, KV_H * DH)):
                        load_weights(sp, u, i, (wslot[:, u, :, :], weights(io["w_kv"], i * P + c0)))

            @block.tensor
            def _(pe):
                pe.sem_inc(tile_out, 1)
                with pe.Fori(0, HALVES) as i:
                    pe.wait_ge(att_logit_ready, a.at(i))
                    pe.wait_ge(att_pT_ready, a.at(i))
                    for u in range(GROUP + 1):
                        weights_in(pe, u, i, 2 if u < GROUP else 1)
                        for k in range(KC):
                            mm = pe.matmul(ps[:, u, :], wslot[:, u, k, :], (hT if u < GROUP else hkv)[:, k, :], start=k == 0, stop=k == KC - 1)
                        mm.then_inc(mm_done[u], 1)
                    weights_in(pe, 4, i)
                    for t in range(TT):
                        for k in range(KC):
                            mm = pe.matmul(ps[:, 4, t * P:(t + 1) * P], hkv[:, k, t * P:(t + 1) * P], wslot[:, 4, k, :], start=k == 0, stop=k == KC - 1)
                    mm.then_inc(mm_done[4], 1)
                    pe.wait_ge(evac, 5 * i + 5)

                    def accumulator_free(u):
                        if u == 0:
                            pe.wait_ge(tile_out, GROUP * i + 1)
                        if u == 2 * PERJ:
                            pe.wait_ge(tile_out, GROUP * i + 2)

                    att_pe(pe, a, i, accumulator_free)

            @block.scalar
            def _(act):
                with act.Fori(0, HALVES) as i:
                    act.wait_ge(att_weighted, a.at(i))
                    for j in range(GROUP):
                        projected(act, j, i)
                        act.activation(qT[:, j, :], ps[:, j, :], ACT.Copy, scale=DH ** -0.5).then_inc(evac, 1)

                    def tile_done(j):
                        act.wait_ge(att_weighted, a.at(i) + PERJ * (j + 1))
                        act.activation(yT[:, i * GROUP + j, :], ps[:, 6 + j % 2, :], ACT.Copy).then_inc(tile_out, 1)

                    att_act(act, a, i, lambda u: tile_done(u // PERJ - 1) if u >= PERJ and u % PERJ == 1 else None)
                    tile_done(GROUP - 1)

            @block.vector
            def _(dve):
                link = Chain(dve, sw_v)
                with dve.Fori(0, HALVES) as i:
                    link.loop(i, att_links(a) + 1)
                    dve.wait_ge(att_weighted, a.at(i))
                    dve.tensor_copy(sink[:, :], sinks[:, ds(i * HPT, HPT)])
                    link(dve.tensor_copy(bias[:, :, ::-1], swa_bias[:, ds(i * HPT, HPT), :]))
                    projected(dve, 3, i)
                    dve.tensor_copy(kT[:, :], ps[:, 3, :]).then_inc(evac, 1)
                    projected(dve, 4, i)
                    dve.tensor_copy(v[:, :, :].rearrange("p t n -> p (t n)"), ps[:, 4, :]).then_inc(evac, 1)
                    att_dve(dve, a, i, link, None)
                link.end(HALVES)
        end_ring(5, HALVES, [2, 2, 2, 1, 1])
        a.end(HALVES)
    memory_attention("ma1", 1, io["b_q"], Q_WIDTH)
    def heads_tiles(u, c0):
        w = io["b_out"]
        pieces = [(wslot[64 * kv:64 * kv + 64, u, GROUP * n:GROUP * n + GROUP, :],
                   w[n * QW + kv * GROUP * DH:n * QW + (kv + 1) * GROUP * DH, :].rearrange("(j d) n -> d j n", d=DH)[:, :, ds(c0, P)])
                  for n in range(HALVES) for kv in range(2)]
        return pieces + [(wslot[:, u, CT:, :], w[Q_WIDTH:, :].rearrange("(k p) n -> p k n", p=P)[:, :, ds(c0, P)])]

    residual_block(KC, heads_tiles, 5, None)
    rms_block("f1", [(xT, T, [(hT, gain(vB, ROWS_B["norm_ffn"] + KC), None)])], [EPS2])
    feed_forward("ff1", 1)
    rms_block("fin", [(xT, T, [(hT, gain(vB, ROWS_B["final"]), None)])], [EPS2])

    with ExitStack() as local:
        rows = sb("out_rows", [P, TT, D], on=local)
        turned, rows_ready, stored = sem("out_turned"), sem("out_ready"), sem("out_stored")
        with nc.Block() as block:
            @block.tensor
            def _(pe):
                for t in range(TT):
                    for k in range(KC):
                        mm = pe.transpose(ps[:, 2 * t + k // 4, k % 4 * P:(k % 4 + 1) * P], hT[:, k, t * P:(t + 1) * P], ident[:, :])
                    mm.then_inc(turned, 1)

            @block.vector
            def _(dve):
                for t in range(TT):
                    dve.wait_ge(turned, t + 1)
                    dve.tensor_copy(rows[:, t, :], ps[:, 2 * t:2 * t + 2, :].rearrange("p b n -> p (b n)")).then_inc(rows_ready, 1)

            @block.sync
            def _(sp):
                for t in range(TT):
                    sp.wait_ge(rows_ready, t + 1)
                    sp.dma_start(out[t * P:(t + 1) * P, :], rows[:, t, :]).then_inc(stored, 16)
                sp.wait_ge(stored, 16 * TT)


def constants():
    c = {}
    c["ident"] = np.eye(P, dtype=np.float32)
    c["ones"] = np.ones((P, P), np.float32)
    dc, m = np.arange(NDC)[:, None], np.arange(P)[None, :]
    c["spread"] = (dc + m == GRID_W - 1 + NA_KW - 1).astype(np.float32)
    start = np.asarray(bucket_starts())
    dist = np.arange(3 * P)[None, :] - (P - 1)
    c["inbucket"] = ((dist >= start[:-1, None]) & (dist < start[1:, None])).astype(np.float32)
    c["farmask"] = np.where((dist >= 0) & (dist < MAXD), 0.0, -BIG).astype(np.float32) * np.ones((SWA_H, 1), np.float32)
    col, key = (np.arange(P) % GRID_W)[:, None], np.arange(GRID_W)[None, ::-1]
    first = np.clip(col - NA_KW // 2, 0, GRID_W - NA_KW)
    c["colmask"] = np.where((key >= first) & (key < first + NA_KW), 0.0, -BIG).astype(np.float32)
    s, t = np.arange(CH)[:, None], np.arange(CH)[None, :]
    pairs = np.zeros((P, 2, LEVELS + 1, CH), np.float32)
    for n in range(LEVELS):
        half = CH >> (n + 1)
        same = s // (2 * half) == t // (2 * half)
        pairs[:, 0, n] = same & (s // half % 2 == 0) & (t // half % 2 == 1)
        pairs[:, 1, n] = same & (s // half % 2 == 1) & (t // half % 2 == 0)
    pairs[:, :, LEVELS] = (s == t)[:, None, :]
    c["pairs"] = pairs.reshape(P, -1)
    go = np.ones((P, 2, T), np.float32)
    go[:, 0, 0::CH] = 0
    go[:, 1, CH - 1::CH] = 0
    c["go"] = go.reshape(P, -1)
    c["iota16"] = np.broadcast_to(np.arange(TOPK, dtype=np.float32), (P, TOPK)).copy()
    return c


def layout(inputs):
    a = {k: np.ascontiguousarray(np.asarray(v)) for k, v in inputs.items()}
    rows = lambda x: x.reshape(-1, P)
    out = {
        "x": a["x"].reshape(T, D), "ctx": a["ctx"].reshape(L, D), "mem": a["mem_2"].reshape(MEM, D),
        "c": rows(a["c"]), "c_ctx": rows(a["c_ctx"]), "b_mod": rows(a["b_mod"]), "norm1": rows(a["norm1"]),
        "norm2": rows(a["norm2"]), "norm_f": rows(a["norm_f"]), "hg_norm": rows(a["hg_norm"]), "hg_lb": rows(a["hg_lb"]),
        "norm_mix": rows(a["norm_mix_2"]), "norm_ffn": rows(a["norm_ffn_2"]), "kv_norm": rows(a["kv_norm_2"]),
        "mem_norm": rows(a["mem_norm_2"]), "final": rows(a["final_norm_2"]), "conv": rows(a["a_conv_w_2"]),
        "w_mod": a["w_mod"][0], "w_in": a["w_in"][0], "w_out": a["w_out"][0], "rpb": a["na_rpb"].reshape(NA_H * NDR, NDC),
        "wq": a["peer_wq"][0], "keys": a["peer_keys"][0].reshape(PE_H * 2 * NKEYS, DK), "u": a["peer_u"][0], "v": a["peer_v"][0],
        "a_in": a["a_w_in_2"][0], "a_out": a["a_w_out_2"][0], "w_kv": a["w_kv_2"], "b_q": a["b_w_q_2"][0],
        "sinks": a["b_sinks_2"].reshape(1, SWA_H), "b_out": a["b_w_out_2"][0], "rel_bias": a["rel_bias_2"],
        "mem_kv": a["w_mem_kv_2"].reshape(2 * D, -1), "gate": a["w_gate_2"].reshape(2 * D, D_FF),
        "up": a["w_up_2"].reshape(2 * D, D_FF), "down": a["w_down_2"].reshape(2 * D_FF, D),
    }
    out.update({"const_" + k: v for k, v in constants().items()})
    return out


def kernel(**inputs):
    import concourse.bacc as bacc
    from concourse.bass_utils import run_bass_kernel_spmd

    nc = bacc.Bacc("TRN2", target_bir_lowering=False, num_devices=1)
    arrays, io = {}, {}
    for name, a in layout(inputs).items():
        arrays[f"in_{name}"] = a
        io[name] = nc.dram_tensor(f"in_{name}", a.shape, mybir.dt.from_np(a.dtype), kind="ExternalInput").ap()
    out = nc.dram_tensor("out", (T, D), F32, kind="ExternalOutput").ap()
    program(nc, io, out)
    r = run_bass_kernel_spmd(nc, [arrays], core_ids=[0])
    return r.results[0]["out"].reshape(1, T, D)
```

```python
from contextlib import ExitStack

import numpy as np
import concourse.bass as bass
from concourse import mybir
from concourse.alu_op_type import AluOpType as ALU

ACT = mybir.ActivationFunctionType
AX = mybir.AxisListType
F32 = mybir.dt.float32
F32R = mybir.dt.float32r
U32 = mybir.dt.uint32
ds = bass.ds

P = 128
D, T, L, MEM = 1024, 512, 256, 256
KC = D // P
TT, LT = T // P, L // P
GRID_W = 64
NA_H, DH = 8, 64
NA_KH, NA_KW = 8, 16
NDR, NDC = 2 * NA_KH - 1, 2 * NA_KW - 1
HG_H, DK = 4, 128
CH = 128
NCH = T // CH
LEVELS = 7
PE_H, NKEYS, TOPK = 8, 128, 16
KV_H, GROUP, SWA_H = 4, 3, 12
BUCKETS, MAXD = 32, 128
D_FF = 2816
FT = D_FF // P
CONV = 768
Q_WIDTH = SWA_H * DH
EPS1, EPS2 = 1e-6, 1e-5
BIG = 1e30

ROWS_A = dict(c=0, c_ctx=8, b_mod=16, norm1=64, norm2=72, norm_f=80, hg_norm=88, hg_lb=92)
ROWS_B = dict(norm_mix=0, norm_ffn=16, kv_norm=32, mem_norm=40, final=48, conv=56)
NA_ROWS, NB_ROWS = 108, 74


def bucket_starts():
    half = BUCKETS // 2
    dist = np.arange(MAXD)
    near = np.maximum(dist, 1).astype(np.float32)
    far = half + (np.log(near / np.float32(half)) / np.float32(np.log(MAXD / half)) * np.float32(BUCKETS - half)).astype(np.int32)
    bucket = np.where(dist < half, dist, np.minimum(far, BUCKETS - 1))
    return [int(np.argmax(bucket >= b)) if (bucket >= b).any() else MAXD for b in range(BUCKETS)] + [MAXD]


class Chain:

    def __init__(self, engine, sem):
        self.engine, self.sem, self.done, self.turn = engine, sem, 0, 0

    def __call__(self, ins):
        self.done = self.done + 1
        ins.then_inc(self.sem, 1)
        self.engine.wait_ge(self.sem, self.turn + self.done)

    def loop(self, i, per):
        self.before, self.per, self.turn, self.done = self.done, per, i * per + self.done, 0

    def end(self, turns):
        assert self.done == self.per, (self.done, self.per)
        self.done, self.turn = self.before + turns * self.per, 0


def program(nc, io, out):
    whole = ExitStack()

    def sb(name, shape, dt=F32, on=whole):
        return on.enter_context(nc.sbuf_tensor(name, shape, dt))

    def sem(name):
        return whole.enter_context(nc.semaphore(name))

    ps = whole.enter_context(nc.psum_tensor("ps", [P, 8, 512], F32))

    ident = sb("ident", [P, P])
    ones = sb("ones", [P, P])
    xT = sb("xT", [P, KC, T])
    hT = sb("hT", [P, KC, T])
    yT = sb("yT", [P, KC, T])
    rstd = sb("rstd", [P, T])
    memT = sb("memT", [P, KC, MEM])
    vA = sb("vA", [P, NA_ROWS])
    vB = sb("vB", [P, NB_ROWS])
    mod = sb("mod", [P, 6 * KC, 2])
    gain1 = sb("gain1", [P, KC, 2])
    gain2 = sb("gain2", [P, KC])
    wring = sb("wring", [P, 6 * KC * P])
    wslot = wring[:, :].rearrange("p (s k n) -> p s k n", s=6, k=KC)

    SLOTS = 6
    w_landed = [sem(f"w_landed{u}") for u in range(SLOTS)]
    mm_done = [sem(f"mm_done{u}") for u in range(SLOTS)]
    evacuated = [sem(f"evacuated{u}") for u in range(SLOTS)]
    landed, turns, left = [0] * SLOTS, [1] * SLOTS, [1] * SLOTS

    def load_weights(sp, u, it, *pieces):
        sp.wait_ge(mm_done[u], turns[u] + it)
        sp.nop(nofuse=True)
        for dst, src in pieces:
            sp.dma_start(dst, src).then_inc(w_landed[u], 16)

    def weights_in(pe, u, it, pieces=1):
        pe.wait_ge(w_landed[u], 16 * (landed[u] + pieces * (it + 1)))

    def projected(eng, u, it):
        eng.wait_ge(mm_done[u], turns[u] + it + 1)

    def end_ring(slots, times, pieces=1, evacuations=False):
        for u in range(slots):
            landed[u] += times * (pieces if isinstance(pieces, int) else pieces[u])
            turns[u] += times
            left[u] += times if evacuations else 0

    SPLIT = 4
    hi_ready = [sem(f"hi_ready{u}") for u in range(SPLIT)]
    split_done = [sem(f"split_done{u}") for u in range(SPLIT)]
    rhs_hi_ready, rhs_ready = sem("rhs_hi_ready"), sem("rhs_ready")
    his, splits = [0] * SPLIT, [1] * SPLIT
    rhs_chunks = [0]

    def split_buffers(on, name):
        return [sb(f"{name}_{x}", shape, F32R, on=on) for x, shape in
                (("w_hi", [P, SPLIT, KC, P]), ("w_lo", [P, SPLIT, KC, P]), ("r_hi", [P, KC, T]), ("r_lo", [P, KC, T]))]

    def load_split(sp, u, t, *pieces):
        sp.wait_ge(split_done[u], splits[u] + t)
        sp.nop(nofuse=True)
        for dst, src in pieces:
            sp.dma_start(dst, src).then_inc(w_landed[u], 16)

    def split_hi(act, parts, u, t, pieces=1):
        weights_in(act, u, t, pieces)
        act.wait_ge(mm_done[u], turns[u] + t)
        act.activation(parts[0][:, u, :, :], wslot[:, u, :, :], ACT.Copy).then_inc(hi_ready[u], 1)

    def split_lo(dve, parts, u, t):
        dve.wait_ge(hi_ready[u], his[u] + t + 1)
        dve.tensor_tensor(parts[1][:, u, :, :], wslot[:, u, :, :], parts[0][:, u, :, :].bitcast(F32), ALU.subtract).then_inc(split_done[u], 1)

    def rhs_hi(act, parts, src):
        for k in range(KC):
            act.activation(parts[2][:, k, :], src[:, k, :], ACT.Copy).then_inc(rhs_hi_ready, 1)

    def rhs_lo(dve, parts, src):
        for k in range(KC):
            dve.wait_ge(rhs_hi_ready, rhs_chunks[0] + k + 1)
            dve.tensor_tensor(parts[3][:, k, :], src[:, k, :], parts[2][:, k, :].bitcast(F32), ALU.subtract).then_inc(rhs_ready, 1)

    def product(pe, parts, u, t, bank, hi, lo, n=KC, chunk_in=None):
        pe.wait_ge(split_done[u], splits[u] + t + 1)
        pe.wait_ge(evacuated[u], left[u] + t)
        for k in range(n):
            if chunk_in is not None:
                chunk_in(k)
            pe.matmul(bank, parts[0][:, u, k, :], hi[:, k, :], start=k == 0, stop=False)
            pe.matmul(bank, parts[0][:, u, k, :], lo[:, k, :], start=False, stop=False)
            mm = pe.matmul(bank, parts[1][:, u, k, :], hi[:, k, :], start=False, stop=k == n - 1)
        mm.then_inc(mm_done[u], 1)

    def rhs_in(pe):
        return lambda k: pe.wait_ge(rhs_ready, rhs_chunks[0] + k + 1)

    def end_split(slots, times, pieces=1):
        end_ring(slots, times, pieces, True)
        rhs_chunks[0] += KC
        for u in range(slots):
            his[u] += times
            splits[u] += times

    norm_squared, norm_summed, norm_meaned, norm_rooted, norm_scaled, norm_chain = [sem(f"norm_{s}") for s in ("squared", "summed", "meaned", "rooted", "scaled", "chain")]
    norms = dict(parts=0, scaled=0, chain=0)

    def rms_block(name, parts, eps):
        base, scaled_before = norms["parts"], norms["scaled"]
        with ExitStack() as local:
            sq = sb(f"{name}_sq", [P, KC, T], on=local)
            with nc.Block() as block:
                @block.scalar
                def _(act):
                    done = scaled_before
                    for n, (src, N, outs) in enumerate(parts, base):
                        if n > base:
                            act.wait_ge(norm_summed, n)
                        for h in range(2):
                            act.activation(sq[:, 4 * h:4 * h + 4, 0:N], src[:, 4 * h:4 * h + 4, :], ACT.Square).then_inc(norm_squared, 1)
                        act.wait_ge(norm_meaned, n + 1)
                        act.activation(rstd[:, 0:N], rstd[:, 0:N], ACT.Sqrt).then_inc(norm_rooted, 1)
                        for dst, gain, shift in outs:
                            for k in range(KC):
                                done += 1
                                if shift is not None:
                                    act.wait_ge(norm_scaled, done)
                                    act.activation(dst[:, k, :], dst[:, k, :], ACT.Identity, bias=shift(k))

                @block.tensor
                def _(pe):
                    for n, (src, N, outs) in enumerate(parts, base):
                        for k in range(KC):
                            if k % 4 == 0:
                                pe.wait_ge(norm_squared, 2 * n + k // 4 + 1)
                            if n > base and k == 0:
                                pe.wait_ge(norm_meaned, n)
                            mm = pe.matmul(ps[:, 0, 0:N], ones[:, :], sq[:, k, 0:N], start=k == 0, stop=k == KC - 1)
                        mm.then_inc(norm_summed, 1)

                @block.vector
                def _(dve):
                    link = Chain(dve, norm_chain)
                    link.done = norms["chain"]
                    for n, (src, N, outs) in enumerate(parts, base):
                        dve.wait_ge(norm_summed, n + 1)
                        dve.tensor_scalar(rstd[:, 0:N], ps[:, 0, 0:N], 1.0 / D, eps[n - base], ALU.mult, ALU.add).then_inc(norm_meaned, 1)
                        dve.wait_ge(norm_rooted, n + 1)
                        link(dve.reciprocal(rstd[:, 0:N], rstd[:, 0:N]))
                        for dst, gain, shift in outs:
                            for k in range(KC):
                                dve.scalar_tensor_tensor(dst[:, k, :], src[:, k, :], gain(k), rstd[:, 0:N], ALU.mult, ALU.mult).then_inc(norm_scaled, 1)
        norms["parts"] += len(parts)
        norms["chain"] += len(parts)
        norms["scaled"] += KC * sum(len(outs) for _, _, outs in parts)

    att_scored, att_logit_ready, att_exp_ready, att_prob_ready, att_turned, att_pT_ready, att_weighted = [
        sem(f"att_{x}") for x in ("scored", "logit_ready", "exp_ready", "prob_ready", "turned", "pT_ready", "weighted")]
    att_units = [1]

    class Attention:

        def __init__(self, name, local, units, depth):
            self.units, self.n, self.depth, self.lag = units, len(units), depth, depth - 1
            width = max(keys_of(u) for u in units)
            self.s = sb(f"{name}_s", [P, depth, width], on=local)
            self.pT = sb(f"{name}_pT", [P, 2, width], on=local)
            self.small = sb(f"{name}_small", [P, depth, 8], on=local)
            self.before = att_units[0]

        def at(self, i):
            return self.before + self.n * i

        def end(self, turns):
            att_units[0] += self.n * turns

    def col(a, u, j):
        return a.small[:, u % a.depth, j:j + 1]

    def score_bank(a, u):
        b, per = 4 // a.depth * (u % a.depth), 4 // a.depth
        return ps[:, b:b + per, :].rearrange("p b n -> p (b n)")

    def turn_bank(a, u):
        banks = ps[:, 4:6, :] if a.depth == 2 else ps[:, 4 + u % 2:5 + u % 2, :]
        return banks.rearrange("p b n -> p (b n)")

    def keys_of(unit):
        return sum(w for _, w in unit["k"])

    def att_score(pe, a, i, u):
        pe.wait_ge(att_logit_ready, a.at(i) + max(u - a.lag, 0))
        at = 0
        for seg, w in a.units[u]["k"]:
            mm = pe.matmul(score_bank(a, u)[:, at:at + w], a.units[u]["q"], seg, start=True, stop=True)
            at += w
        mm.then_inc(att_scored, 1)

    def att_turn(pe, a, i, u):
        pe.wait_ge(att_prob_ready, a.at(i) + u + 1)
        pe.wait_ge(att_pT_ready, a.at(i) + (u if a.depth == 2 else max(u - 1, 0)))
        for b in range(keys_of(a.units[u]) // P):
            mm = pe.transpose(turn_bank(a, u)[:, b * P:(b + 1) * P], a.s[:, u % a.depth, b * P:(b + 1) * P], ident[:, :])
        mm.then_inc(att_turned, 1)

    def att_weigh(pe, a, i, u, before):
        unit = a.units[u]
        pe.wait_ge(att_pT_ready, a.at(i) + u + 1)
        before(u)
        for b, v in enumerate(unit["v"]):
            mm = pe.matmul(unit["out"], v, a.pT[:, u % 2, b * P:(b + 1) * P], start=b == 0, stop=b == len(unit["v"]) - 1)
        mm.then_inc(att_weighted, 1)

    def att_pe(pe, a, i, before, fresh=lambda u: None, between=lambda u: None):
        for u in range(a.n + a.lag + 1):
            if u < a.n:
                fresh(u)
                att_score(pe, a, i, u)
            if a.depth > 2 and a.lag <= u < a.n + a.lag:
                att_turn(pe, a, i, u - a.lag)
            if u > a.lag:
                att_weigh(pe, a, i, u - a.lag - 1, before)
            between(u)
            if a.depth == 2 and a.lag <= u < a.n + a.lag:
                att_turn(pe, a, i, u - a.lag)

    def att_links(a):
        return sum(2 + (x["sink"] is not None) for x in a.units)

    def att_logits(dve, a, i, u, link, zeros):
        unit = a.units[u]
        dve.wait_ge(att_scored, a.at(i) + u + 1)
        dve.wait_ge(att_turned, a.at(i) + max(u - a.lag, 0))
        dve.nop(nofuse=True)
        at, start = 0, -BIG if unit["sink"] is None else unit["sink"]
        for j, (seg, w) in enumerate(unit["k"]):
            bias = zeros[:, 0:w] if unit["bias"][j] is None else unit["bias"][j]
            last = dve.tensor_tensor_reduce(a.s[:, u % a.depth, at:at + w], score_bank(a, u)[:, at:at + w], bias,
                                            1.0, start, ALU.add, ALU.max, col(a, u, 4 + j))
            at += w
        link(last)
        dve.tensor_scalar(col(a, u, 0), col(a, u, 4), col(a, u, 3 + len(unit["k"])), -1.0, ALU.max, ALU.mult).then_inc(att_logit_ready, 1)

    def att_probs(dve, a, i, u, link):
        n = keys_of(a.units[u])
        dve.wait_ge(att_exp_ready, a.at(i) + u + 1)
        if a.units[u]["sink"] is not None:
            link(dve.tensor_tensor(col(a, u, 1), col(a, u, 1), col(a, u, 2), ALU.add))
        link(dve.reciprocal(col(a, u, 3), col(a, u, 1)))
        dve.tensor_scalar(a.s[:, u % a.depth, 0:n], a.s[:, u % a.depth, 0:n], col(a, u, 3), None, ALU.mult).then_inc(att_prob_ready, 1)

    def att_dve(dve, a, i, link, zeros, between=lambda u: None):
        for u in range(a.n + 1):
            if a.depth == 2 and u >= 1:
                att_probs(dve, a, i, u - 1, link)
            if u < a.n:
                att_logits(dve, a, i, u, link, zeros)
            if a.depth > 2 and u >= 1:
                att_probs(dve, a, i, u - 1, link)
            between(u)

    def att_act(act, a, i, after=lambda v: None):
        def exps(u):
            n = keys_of(a.units[u])
            act.wait_ge(att_logit_ready, a.at(i) + u + 1)
            if a.units[u]["sink"] is not None:
                act.activation(col(a, u, 2), a.units[u]["sink"], ACT.Exp, bias=col(a, u, 0))
            act.activation(a.s[:, u % a.depth, 0:n], a.s[:, u % a.depth, 0:n], ACT.Exp, bias=col(a, u, 0),
                           accum_out=col(a, u, 1)).then_inc(att_exp_ready, 1)

        def turned_probs(u):
            n = keys_of(a.units[u])
            act.wait_ge(att_turned, a.at(i) + u + 1)
            act.wait_ge(att_weighted, a.at(i) + max(u - 1, 0))
            act.activation(a.pT[:, u % 2, 0:n], turn_bank(a, u)[:, 0:n], ACT.Copy).then_inc(att_pT_ready, 1)
            after(u)

        for u in range(a.n + a.lag):
            if a.depth == 2 and u < a.n:
                exps(u)
            if u >= a.lag:
                turned_probs(u - a.lag)
            if a.depth > 2 and u < a.n:
                exps(u)

    def gain(v, at):
        return lambda k: v[:, at + k:at + k + 1]

    def weights(w, c0, n=P):
        return w.rearrange("(k p) n -> p k n", p=P)[:, :, ds(c0, n)]

    rpb_scr = nc.dram_tensor("rpb_scr", [NA_H * NDR, P], F32, kind="Internal")
    rel_scr = nc.dram_tensor("rel_scr", [SWA_H, 3 * P], F32, kind="Internal")
    swa_bias = sb("swa_bias", [P, SWA_H, 2 * P])
    sinks = sb("sinks", [P, SWA_H])
    lb = sb("lb", [P, 2, 2, HG_H])
    ctx_mem = ExitStack()
    with ctx_mem:
        ctxT = sb("ctxT", [P, KC, L], on=ctx_mem)
        rstds = sb("rstds", [P, T + L + MEM], on=ctx_mem)
        na_stack = ctx_mem.enter_context(ExitStack())
        na_bias = sb("na_bias", [P, NA_H, 16, GRID_W], on=na_stack)
        with ExitStack() as local:
            tok = [half.rearrange("p (t k) n -> p t (k n)", t=TT)[:, t, :] for half in (hT[:, :, :], yT[:, :, :]) for t in range(TT)]
            rows = sb("rows", [P, 2, P], on=local)
            cT = sb("cT", [P, KC, 2], on=local)
            mod_rows = sb("mod_rows", [2, 6 * D], on=local)
            SQ = 4
            sq = sb("setup_sq", [P, SQ, T], on=local)
            rpb = sb("rpb", [NA_H * NDR, NDC], on=local)
            rpbT = sb("rpbT", [NDC, NA_H * NDR], on=local)
            spread = sb("spread", [NDC, P], on=local)
            inbucket = sb("inbucket", [BUCKETS, 3 * P], on=local)
            relb = sb("relb", [BUCKETS, SWA_H], on=local)
            wide = sb("wide", [NA_H * NDR, P], on=local)
            far = sb("far", [SWA_H, 3 * P], on=local)
            farmask = sb("farmask", [SWA_H, 3 * P], on=local)
            sink1 = sb("sink1", [1, SWA_H], on=local)
            consts_in, rows_in, rpb_in = sem("consts_in"), sem("rows_in"), sem("rpb_in")
            tok_in = [sem(f"tok_in{n}") for n in range(TT + 2 * LT)]
            rows_turned, silu_ready = sem("rows_turned"), sem("silu_ready")
            x_turned, x_ready, x_squared, x_added = sem("x_turned"), sem("x_ready"), sem("x_squared"), sem("x_added")
            x_meaned, x_rooted, mod_turned = sem("x_meaned"), sem("x_rooted"), sem("mod_turned")
            rpb_turned, rpb_ready, rpb_spread, bias_ready = sem("rpb_turned"), sem("rpb_ready"), sem("rpb_spread"), sem("bias_ready")
            scr_written, bias_in = sem("scr_written"), sem("bias_in")
            na_zero, setup_v, cT_ready = sem("na_zero"), sem("setup_v"), sem("cT_ready")
            MS = 3
            modw = wring[:, :].rearrange("p (s k n) -> p s k n", s=MS, k=KC)
            sum_bank = [ps[:, 4, :], ps[:, 5, 0:L], ps[:, 6, 0:MEM]]
            mod_bank = [ps[0:2, u, 0:2 * P] for u in range(MS)]
            ends = [KC, KC + KC // 2, 2 * KC]
            rstd_of = [rstds[:, 0:T], rstds[:, T:T + L], rstds[:, T + L:]]
            groups = [(0, k) for k in range(KC)] + [(TT, k) for k in range(0, KC, 2)] + [(TT + LT, k) for k in range(0, KC, 2)]

            def in_group(t0, k):
                return xT[:, k, :] if t0 == 0 else (ctxT if t0 == TT else memT)[:, k:k + 2, :].rearrange("p k n -> p (k n)")

            with nc.Block() as block:
                @block.sync
                def _(sp):
                    for dst, name in ((ident, "ident"), (spread, "spread"), (inbucket, "inbucket"), (farmask, "farmask"), (ones, "ones")):
                        sp.dma_start(dst[:, :], io["const_" + name]).then_inc(consts_in, 16)
                    for at, names, where in ((0, ("c", "c_ctx", "b_mod", "norm1", "norm2", "norm_f", "hg_norm", "hg_lb"), ROWS_A),
                                             (1, ("norm_mix", "norm_ffn", "kv_norm", "mem_norm", "final", "conv"), ROWS_B)):
                        for name in names:
                            n = io[name].shape[0]
                            sp.dma_start(rows[where[name]:where[name] + n, at, :], io[name]).then_inc(rows_in, 16)
                    for n in range(TT + 2 * LT):
                        src, r = ((io["x"], n) if n < TT else (io["ctx"], n - TT) if n < TT + LT else (io["mem"], n - TT - LT))
                        sp.dma_start(tok[n], src[r * P:(r + 1) * P, :]).then_inc(tok_in[n], 16)
                    with sp.Fori(0, 6 * KC // 2 // MS) as i:
                        for u in range(MS):
                            load_weights(sp, u, i, (modw[:, u, :, :], weights(io["w_mod"], i * (MS * 2 * P) + u * 2 * P, 2 * P)))

                @block.gpsimd
                def _(pool):
                    pool.memset(na_bias[:, :, :, :], 0.0).then_inc(na_zero, 1)
                    pool.dma_start(rpb[:, :], io["rpb"]).then_inc(rpb_in, 16)
                    pool.dma_start(relb[:, :], io["rel_bias"]).then_inc(rpb_in, 16)
                    pool.dma_start(sink1[:, :], io["sinks"]).then_inc(rpb_in, 16)
                    pool.wait_ge(bias_ready, 2)
                    pool.dma_start(rpb_scr[:, :], wide[:, :]).then_inc(scr_written, 16)
                    pool.dma_start(rel_scr[:, :], far[:, :]).then_inc(scr_written, 16)
                    pool.wait_ge(scr_written, 32)
                    pool.wait_ge(na_zero, 1)
                    for half in range(2):
                        for h in range(NA_H):
                            pool.dma_start(na_bias[half * 64:half * 64 + 64, h, half:half + NDR, :],
                                           bass.AP(rpb_scr, h * NDR * P, [[1, GRID_W], [P, NDR], [1, GRID_W]])).then_inc(bias_in, 16)
                    pool.dma_start(swa_bias[:, :, :], bass.AP(rel_scr, 0, [[1, P], [3 * P, SWA_H], [1, 2 * P]])).then_inc(bias_in, 16)
                    pool.wait_ge(bias_in, 16 * (2 * NA_H + 1))

                @block.tensor
                def _(pe):
                    for u in range(SLOTS):
                        pe.sem_inc(mm_done[u], 1)
                        pe.sem_inc(evacuated[u], 1)
                    for u in range(SPLIT):
                        pe.sem_inc(split_done[u], 1)
                    for credit in (att_scored, att_logit_ready, att_exp_ready, att_prob_ready, att_turned, att_pT_ready, att_weighted):
                        pe.sem_inc(credit, 1)
                    pe.wait_ge(consts_in, 16 * 5)
                    pe.wait_ge(rows_in, 16 * 14)
                    pe.transpose(ps[:, 7, 0:NA_ROWS], rows[0:NA_ROWS, 0, :], ident[0:NA_ROWS, 0:NA_ROWS])
                    pe.transpose(ps[:, 7, P:P + NB_ROWS], rows[0:NB_ROWS, 1, :], ident[0:NB_ROWS, 0:NB_ROWS]).then_inc(rows_turned, 1)
                    pe.wait_ge(rpb_in, 48)
                    pe.transpose(ps[0:NDC, 5, 0:NA_H * NDR], rpb[:, :], ident[0:NA_H * NDR, 0:NA_H * NDR])
                    pe.matmul(ps[0:SWA_H, 5, P:P + 3 * P], relb[:, :], inbucket[:, :], start=True, stop=True).then_inc(rpb_turned, 1)
                    pe.matmul(ps[:, 4, P:P + SWA_H], ones[0:1, :], sink1[:, :], start=True, stop=True)
                    pe.wait_ge(rpb_ready, 1)
                    pe.matmul(ps[0:NA_H * NDR, 4, 0:P], rpbT[:, :], spread[:, :], start=True, stop=True).then_inc(rpb_spread, 1)
                    for g, (t0, k) in enumerate(groups):
                        if g >= 4:
                            pe.wait_ge(x_ready, g - 3)
                        for b in range(4):
                            t, kk = (t0 + b, k) if t0 == 0 else (t0 + b % 2, k + b // 2)
                            if k == 0 and b < (4 if t0 == 0 else 2):
                                pe.wait_ge(tok_in[t], 16)
                            mm = pe.transpose(ps[:, g % 4, b * P:(b + 1) * P], tok[t][:, kk * P:(kk + 1) * P], ident[:, :])
                        mm.then_inc(x_turned, 1)
                    pe.wait_ge(silu_ready, 1)
                    for g, (t0, k) in enumerate(groups):
                        pe.wait_ge(x_squared, g + 1)
                        if t0 == 0:
                            mm = pe.matmul(sum_bank[0], ones[:, :], sq[:, g % SQ, :], start=k == 0, stop=k == KC - 1)
                        else:
                            for b in range(2):
                                mm = pe.matmul(sum_bank[1 if t0 == TT else 2], ones[:, :], sq[:, g % SQ, b * L:(b + 1) * L],
                                               start=k + b == 0, stop=k + b == KC - 1)
                        mm.then_inc(x_added, 1)
                    with pe.Fori(0, 6 * KC // 2 // MS) as i:
                        for u in range(MS):
                            weights_in(pe, u, i)
                            pe.wait_ge(evacuated[u], left[u] + i)
                            for k in range(KC):
                                mm = pe.matmul(mod_bank[u], cT[:, k, :], modw[:, u, k, :], start=k == 0, stop=k == KC - 1)
                            mm.then_inc(mm_done[u], 1)
                    for u in range(MS):
                        pe.wait_ge(evacuated[u], left[u] + 6 * KC // 2 // MS)
                    for m in range(6 * KC):
                        mm = pe.transpose(ps[:, 7, 2 * m:2 * m + 2], mod_rows[:, m * P:(m + 1) * P], ident[0:2, 0:2])
                    mm.then_inc(mod_turned, 1)

                @block.scalar
                def _(act):
                    act.wait_ge(cT_ready, 1)
                    act.activation(cT[:, :, :], cT[:, :, :], ACT.Silu).then_inc(silu_ready, 1)
                    for g, (t0, k) in enumerate(groups):
                        act.wait_ge(x_ready, g + 1)
                        if g >= SQ:
                            act.wait_ge(x_added, g - SQ + 1)
                        act.activation(sq[:, g % SQ, :], in_group(t0, k), ACT.Square).then_inc(x_squared, 1)
                    for n in range(3):
                        act.wait_ge(x_meaned, n + 1)
                        act.activation(rstd_of[n], rstd_of[n], ACT.Sqrt).then_inc(x_rooted, 1)
                    with act.Fori(0, 6 * KC // 2 // MS) as i:
                        for u in range(MS):
                            projected(act, u, i)
                            act.activation(mod_rows[:, ds(i * (MS * 2 * P) + u * 2 * P, 2 * P)], mod_bank[u], ACT.Copy).then_inc(evacuated[u], 1)

                @block.vector
                def _(dve):
                    link = Chain(dve, setup_v)
                    dve.wait_ge(rows_turned, 1)
                    dve.tensor_copy(vA[:, :], ps[:, 7, 0:NA_ROWS])
                    link(dve.tensor_copy(vB[:, :], ps[:, 7, P:P + NB_ROWS]))
                    dve.tensor_copy(cT[:, :, :], vA[:, 0:2 * KC].rearrange("p (a k) -> p k a", a=2)).then_inc(cT_ready, 1)
                    dve.wait_ge(rpb_turned, 1)
                    dve.tensor_tensor(far[:, :], ps[0:SWA_H, 5, P:P + 3 * P], farmask[:, :], ALU.add).then_inc(bias_ready, 1)
                    dve.tensor_copy(rpbT[:, :], ps[0:NDC, 5, 0:NA_H * NDR]).then_inc(rpb_ready, 1)
                    dve.wait_ge(rpb_spread, 1)
                    dve.tensor_copy(sinks[:, :], ps[:, 4, P:P + SWA_H])
                    dve.tensor_copy(wide[:, :], ps[0:NA_H * NDR, 4, 0:P]).then_inc(bias_ready, 1)
                    for g, (t0, k) in enumerate(groups):
                        dve.wait_ge(x_turned, g + 1)
                        dve.tensor_copy(in_group(t0, k), ps[:, g % 4, :]).then_inc(x_ready, 1)
                    for n in range(3):
                        dve.wait_ge(x_added, ends[n])
                        dve.tensor_scalar(rstd_of[n], sum_bank[n], 1.0 / D, [EPS1, EPS1, EPS2][n], ALU.mult, ALU.add).then_inc(x_meaned, 1)
                    for n in range(3):
                        dve.wait_ge(x_rooted, n + 1)
                        link(dve.reciprocal(rstd_of[n], rstd_of[n]))
                    for k in range(KC):
                        dve.scalar_tensor_tensor(memT[:, k, :], memT[:, k, :], vB[:, ROWS_B["mem_norm"] + k:ROWS_B["mem_norm"] + k + 1], rstd_of[2], ALU.mult, ALU.mult)
                    dve.wait_ge(mod_turned, 1)
                    bm = vA[:, ROWS_A["b_mod"]:ROWS_A["b_mod"] + 6 * KC]
                    for a in range(2):
                        last = dve.tensor_tensor(mod[:, :, a], ps[:, 7, 0:12 * KC].rearrange("p (m a) -> p m a", a=2)[:, :, a], bm, ALU.add)
                    link(last)
                    for a in range(2):
                        n1 = vA[:, ROWS_A["norm1"]:ROWS_A["norm1"] + KC]
                        dve.scalar_tensor_tensor(gain1[:, :, a], mod[:, KC:2 * KC, a], 1.0, n1, ALU.add, ALU.mult)
                    n2 = vA[:, ROWS_A["norm2"]:ROWS_A["norm2"] + KC]
                    dve.scalar_tensor_tensor(gain2[:, :], mod[:, 4 * KC:5 * KC, 0], 1.0, n2, ALU.add, ALU.mult)
                    lo = vA[:, ROWS_A["hg_lb"]:ROWS_A["hg_lb"] + 16].rearrange("p (e d h) -> p e d h", e=2, d=2)
                    link(dve.tensor_tensor(lb[:, 0, :, :], lo[:, 0, :, :], lo[:, 1, :, :], ALU.subtract))
            end_ring(MS, 6 * KC // 2 // MS, 1, True)

        with nc.Block() as block:
            @block.vector
            def _(dve):
                for dst, src, N, a, r in ((hT, xT, T, 0, rstds[:, 0:T]), (ctxT, ctxT, L, 1, rstds[:, T:T + L])):
                    for k in range(KC):
                        dve.scalar_tensor_tensor(dst[:, k, :], src[:, k, :], gain1[:, k, a:a + 1], r, ALU.mult, ALU.mult).then_inc(norm_scaled, 1)

            @block.scalar
            def _(act):
                for n, (dst, a) in enumerate(((hT, 0), (ctxT, 1))):
                    for k in range(KC):
                        act.wait_ge(norm_scaled, n * KC + k + 1)
                        act.activation(dst[:, k, :], dst[:, k, :], ACT.Identity, bias=mod[:, k, a:a + 1])
        norms["scaled"] = 2 * KC

        with ExitStack() as local:
            qT = sb("na_q", [P, 2, T], on=local)
            kT = sb("na_k", [P, 2, T + L], on=local)
            v = sb("na_v", [P, 2, TT + LT, P], on=local)
            bias = sb("na_bias_now", [P, 2, 2, 16 * GRID_W], on=local)
            zeros = sb("na_zeros", [P, L], on=local)
            colmask = sb("na_colmask", [P, GRID_W], on=local)
            staged, k_done, pair_out, mask_in, na_v = sem("na_staged"), sem("na_k_done"), sem("na_pair_out"), sem("na_mask_in"), sem("na_chain")
            units = []
            for par in range(2):
                for h in range(2):
                    for t in range(TT):
                        off = (NA_KH - 1 - 2 * t) * GRID_W
                        hp = slice(64 * h, 64 * h + 64)
                        units.append(dict(q=qT[hp, par, t * P:(t + 1) * P], k=[(kT[hp, par, 0:T], T), (kT[hp, par, T:T + L], L)], sink=None,
                                          bias=[bias[:, par, h, off:off + T], None], v=[v[:, par, b, hp] for b in range(TT + LT)],
                                          out=ps[hp, 6, t * P:(t + 1) * P]))
            a = Attention("na", local, units, 2)
            PAIRS = NA_H // 2
            TURNS = PAIRS // 2
            U = a.n // 2
            STAGED = 5
            with nc.Block() as block:
                @block.sync
                def _(sp):
                    sp.dma_start(colmask[:, :], io["const_colmask"]).then_inc(mask_in, 16)
                    with sp.Fori(0, PAIRS) as i:
                        for u in range(3):
                            load_weights(sp, u, i, (wslot[:, u, :, :], weights(io["w_in"], i * P + u * NA_H * DH)))

                @block.tensor
                def _(pe):
                    def project_rows(r, u):
                        pe.wait_ge(staged, STAGED * r + (u + STAGED))
                        weights_in(pe, u, r)
                        for k in range(KC):
                            mm = pe.matmul(ps[:, 7, :], wslot[:, u, k, :], hT[:, k, :], start=k == 0, stop=k == KC - 1)
                        mm.then_inc(mm_done[0] if u == 0 else k_done, 1)

                    def project_ctx(r):
                        pe.wait_ge(staged, STAGED * r + (2 + STAGED))
                        weights_in(pe, 2, r)
                        for c in range(LT):
                            for k in range(KC):
                                pe.matmul(ps[:, 7, L + c * P:L + (c + 1) * P], ctxT[:, k, c * P:(c + 1) * P], wslot[:, 2, k, :], start=k == 0, stop=k == KC - 1)
                        for k in range(KC):
                            mm = pe.matmul(ps[:, 7, 0:L], wslot[:, 1, k, :], ctxT[:, k, :], start=k == 0, stop=k == KC - 1)
                        mm.then_inc(mm_done[1], 1)

                    def project_v(r):
                        pe.wait_ge(staged, STAGED * r + (4 + STAGED))
                        for t in range(TT):
                            for k in range(KC):
                                mm = pe.matmul(ps[:, 7, t * P:(t + 1) * P], hT[:, k, t * P:(t + 1) * P], wslot[:, 2, k, :], start=k == 0, stop=k == KC - 1)
                        mm.then_inc(mm_done[2], 1)

                    def turn(i, more):
                        def accumulator_free(u):
                            if u % U == 0:
                                pe.wait_ge(pair_out, 2 * i + (u // U + 1))

                        def fresh(u):
                            if u % U == 0:
                                pe.wait_ge(staged, STAGED * 2 * i + STAGED * (u // U + 2))

                        def between(u):
                            r, step = 2 * i + (u // U + 1), u % U
                            if u < U or (more and u < 2 * U):
                                if step == 1:
                                    project_rows(r, 0)
                                elif step == 2:
                                    project_rows(r, 1)
                                elif step == 4:
                                    project_ctx(r)
                                elif step == 6:
                                    project_v(r)

                        att_pe(pe, a, i, accumulator_free, fresh, between)

                    pe.sem_inc(staged, STAGED)
                    pe.sem_inc(pair_out, 1)
                    project_rows(0, 0)
                    project_rows(0, 1)
                    project_ctx(0)
                    project_v(0)
                    with pe.Fori(0, TURNS - 1) as i:
                        turn(i, True)
                    turn(TURNS - 1, False)

                @block.scalar
                def _(act):
                    def stage_q(r, par):
                        act.wait_ge(mm_done[0], turns[0] + r + 1)
                        act.activation(qT[:, par, :], ps[:, 7, :], ACT.Copy, scale=DH ** -0.5).then_inc(staged, 1)

                    def stage_k(r, par):
                        act.wait_ge(k_done, r + 1)
                        act.activation(kT[:, par, 0:T], ps[:, 7, :], ACT.Copy).then_inc(staged, 1)

                    def stage_ctx(r, par):
                        act.wait_ge(mm_done[1], turns[1] + r + 1)
                        act.activation(kT[:, par, T:T + L], ps[:, 7, 0:L], ACT.Copy).then_inc(staged, 1)
                        act.activation(v[:, par, TT:TT + LT, :].rearrange("p t n -> p (t n)"), ps[:, 7, L:2 * L], ACT.Copy).then_inc(staged, 1)

                    def stage_v(r, par):
                        act.wait_ge(mm_done[2], turns[2] + r + 1)
                        act.activation(v[:, par, 0:TT, :].rearrange("p t n -> p (t n)"), ps[:, 7, :], ACT.Copy).then_inc(staged, 1)

                    def turn(i, more):
                        def pair_done(par):
                            act.wait_ge(att_weighted, a.at(i) + U * (par + 1))
                            act.activation(yT[:, ds(2 * i + par, 1), :].rearrange("p a t -> p (a t)"), ps[:, 6, :], ACT.Copy).then_inc(pair_out, 1)

                        def after(u):
                            r, par, step = 2 * i + (u // U + 1), (u // U + 1) % 2, u % U
                            if u == U:
                                pair_done(0)
                            if u < U or more:
                                if step == 0:
                                    stage_q(r, par)
                                elif step == 1:
                                    stage_k(r, par)
                                elif step == 3:
                                    stage_ctx(r, par)
                                elif step == 5:
                                    stage_v(r, par)

                        att_act(act, a, i, after)
                        pair_done(1)

                    stage_q(0, 0)
                    stage_k(0, 0)
                    stage_ctx(0, 0)
                    stage_v(0, 0)
                    with act.Fori(0, TURNS - 1) as i:
                        turn(i, True)
                    turn(TURNS - 1, False)

                @block.vector
                def _(dve):
                    link = Chain(dve, na_v)

                    def window(r, par):
                        link(dve.tensor_tensor(bias[:, par, :, :].rearrange("p h (r c) -> p (h r) c", c=GRID_W)[:, :, ::-1],
                                               na_bias[:, ds(2 * r, 2), :, :].rearrange("p h r c -> p (h r) c"),
                                               colmask[:, :].unsqueeze(1).broadcast_to([P, 32, GRID_W]), ALU.add))

                    def turn(i, more):
                        def between(u):
                            if u % U == 2 and (u < U or more):
                                window(2 * i + (u // U + 1), (u // U + 1) % 2)

                        att_dve(dve, a, i, link, zeros, between)

                    dve.wait_ge(mask_in, 16)
                    link(dve.memset(zeros[:, :], 0.0))
                    window(0, 0)
                    with dve.Fori(0, TURNS - 1) as i:
                        link.loop(i, att_links(a) + 2)
                        turn(i, True)
                    link.end(TURNS - 1)
                    turn(TURNS - 1, False)
            end_ring(3, PAIRS)
            a.end(TURNS)
        na_stack.close()
        with ExitStack() as local:
            pairs = sb("hg_pairs", [P, 2, LEVELS + 1, CH], on=local)
            go = sb("hg_go", [P, 2, T], on=local)
            q = sb("hg_q", [P, T], on=local)
            gate = sb("hg_gate", [P, T], on=local)
            v = sb("hg_v", [P, TT + LT, P], on=local)
            f = sb("hg_f", [P, 2, T + L], on=local)
            key = sb("hg_key", [P, 2, T + L], on=local)
            b = sb("hg_b", [P, 2, T + L], on=local)
            cut = sb("hg_cut", [P, LEVELS, T], on=local)
            kd = sb("hg_kd", [P, T + L], on=local)
            eb = sb("hg_eb", [P, 2, T], on=local)
            qe = sb("hg_qe", [P, 2, T], on=local)
            kdT = sb("hg_kdT", [P, TT + LT, P], on=local)
            masked = sb("hg_masked", [P, 2, LEVELS + 1, CH], on=local)
            at_ = sb("hg_at", [P, 2, NCH, CH], on=local)
            state = sb("hg_state", [P, 2, NCH, P], on=local)
            cur = sb("hg_cur", [P, 5], on=local)
            sq = sb("hg_sq", [P, T], on=local)
            next_q = sb("hg_next_q", [P, T], on=local)
            next_f = sb("hg_next_f", [P, 2, T + L], on=local)
            next_v = sb("hg_next_v", [P, TT + LT, P], on=local)
            next_g = sb("hg_next_g", [P, T], on=local)
            consts_in, hg_v, lb_ready = sem("hg_consts_in"), sem("hg_chain"), sem("hg_lb_ready")
            HG_LINKS = 1 + 1 + 1 + 2 * (1 + (NCH - 2) + NCH) + 2
            staged, v_copied, gates, logs, args, exps, cuts = sem("hg_staged"), sem("hg_v_copied"), sem("hg_gates"), sem("hg_logs"), sem("hg_args"), sem("hg_exps"), sem("hg_cuts")
            multiplied, masked_ready, kd_ready, turned, kdT_ready, states_summed = (sem("hg_multiplied"), sem("hg_masked_ready"), sem("hg_kd_ready"),
                                                                           sem("hg_turned"), sem("hg_kdT_ready"), sem("hg_states_summed"))
            states_ready, read_out, squared, summed, meaned, rooted, head_done = (sem("hg_states_ready"), sem("hg_read_out"), sem("hg_squared"), sem("hg_summed"),
                                                                       sem("hg_meaned"), sem("hg_rooted"), sem("hg_head_done"))
            COL0 = 3 * NA_H * DH
            HW = HG_H * DK
            order = [list(range(NCH)), list(range(NCH))[::-1]]
            last_of = [lambda c: c * CH + CH - 1, lambda c: c * CH]

            def halves(x, n, d):
                half = CH >> (n + 1)
                y = x.rearrange("p (b e j) -> p b e j", e=2, j=half)
                lo, hi = y[:, :, 0, :], y[:, :, 1, :]
                return (hi, lo, lo[:, :, half - 1:half]) if d == 0 else (lo, hi, hi[:, :, 0:1])

            with nc.Block() as block:
                @block.sync
                def _(sp):
                    sp.dma_start(pairs[:, :, :, :].rearrange("p a l t -> p (a l t)"), io["const_pairs"]).then_inc(consts_in, 16)
                    sp.dma_start(go[:, :, :].rearrange("p a t -> p (a t)"), io["const_go"]).then_inc(consts_in, 16)
                    with sp.Fori(0, HG_H) as i:
                        for u in (0, 1, 3, 4, 2):
                            load_weights(sp, u, i, (wslot[:, u, :, :], weights(io["w_in"], i * DK + (COL0 + u * HW))))

                STAGED = 8

                @block.tensor
                def _(pe):
                    def project_rows(r, u, bank, ctx):
                        weights_in(pe, u, r)
                        for k in range(KC):
                            mm = pe.matmul(bank, wslot[:, u, k, :], hT[:, k, :], start=k == 0, stop=k == KC - 1)
                        if ctx is not None:
                            for k in range(KC):
                                mm = pe.matmul(ctx, wslot[:, u, k, :], ctxT[:, k, :], start=k == 0, stop=k == KC - 1)
                        mm.then_inc(mm_done[u], 1)

                    def project_v(r, tiles):
                        for t in tiles:
                            if t == 0:
                                weights_in(pe, 3, r)
                            src, c = (hT, t) if t < TT else (ctxT, t - TT)
                            bank = ps[:, 7, t * P:(t + 1) * P] if t < TT else ps[:, 5, L + c * P:L + (c + 1) * P]
                            for k in range(KC):
                                mm = pe.matmul(bank, src[:, k, c * P:(c + 1) * P], wslot[:, 3, k, :], start=k == 0, stop=k == KC - 1)
                            if t == TT + LT - 1:
                                mm.then_inc(mm_done[3], 1)

                    def project_q_forward(r):
                        project_rows(r, 0, ps[:, 0, :], None)
                        project_rows(r, 1, ps[:, 1, :], ps[:, 3, 0:L])

                    def project_g(r):
                        pe.wait_ge(staged, STAGED * r + 5)
                        project_rows(r, 4, ps[:, 7, :], None)

                    def project_backward(r):
                        pe.wait_ge(staged, STAGED * r + 6)
                        project_rows(r, 2, ps[:, 7, :], ps[:, 3, 0:L])

                    def head(i, more):
                        if more:
                            pe.wait_ge(staged, STAGED * i + STAGED)
                            project_q_forward(i + 1)
                        pe.wait_ge(head_done, i + 1)
                        for d in range(2):
                            pe.wait_ge(kd_ready, 2 * i + d + 1)
                            if d:
                                pe.wait_ge(kdT_ready, 4 * i + 2)
                            for t in range(TT + LT):
                                mm = pe.transpose(ps[:, 4 + t // 4, t % 4 * P:(t % 4 + 1) * P], kd[:, t * P:(t + 1) * P], ident[:, :])
                            mm.then_inc(turned, 1)
                            if more and d == 0:
                                project_v(i + 1, [0, 1])
                            if more and d == 1:
                                pe.wait_ge(masked_ready, 8 * i + 5)
                                project_backward(i + 1)
                            pe.wait_ge(kdT_ready, 4 * i + 2 * d + 2)
                            if d:
                                pe.wait_ge(states_ready, 2 * i + 1)
                            for c in order[d][:-1]:
                                pe.matmul(ps[:, 6, c * P:(c + 1) * P], kdT[:, c, :], v[:, c, :], start=True, stop=True)
                            c = order[d][-1]
                            for t in range(LT):
                                mm = pe.matmul(ps[:, 6, c * P:(c + 1) * P], kdT[:, TT + t, :], v[:, TT + t, :], start=t == 0, stop=t == LT - 1)
                            mm.then_inc(states_summed, 1)
                            pe.wait_ge(cuts, 2 * i + d + 1)
                            if more and d == 0:
                                pe.wait_ge(staged, STAGED * (i + 1) + 3)
                            for c in range(NCH):
                                n = NCH * d + c
                                tok_ = slice(c * CH, (c + 1) * CH)
                                pe.wait_ge(masked_ready, 8 * i + max(n - 1, 0) + 1)
                                if more and d == 1 and c == 1:
                                    pe.wait_ge(staged, STAGED * (i + 1) + STAGED)
                                for l in range(LEVELS + 1):
                                    lhs, rhs = (cut[:, l, tok_], cut[:, l, tok_]) if l < LEVELS else (key[:, d, tok_], q[:, tok_])
                                    mm = pe.matmul(ps[:, 2 * (n % 2) + l // 4, (l % 4) * P:(l % 4 + 1) * P], lhs, rhs, start=True, stop=True)
                                mm.then_inc(multiplied, 1)
                                if more and d == 0:
                                    project_v(i + 1, [c + 2])
                            if more and d == 0:
                                project_g(i + 1)
                        pe.wait_ge(masked_ready, 8 * i + 9)
                        pe.wait_ge(states_ready, 2 * i + 2)
                        for c in range(NCH):
                            for d in range(2):
                                pe.matmul(ps[:, 7, c * CH:(c + 1) * CH], v[:, c, :], at_[:, d, c, :], start=d == 0, stop=False)
                                mm = pe.matmul(ps[:, 7, c * CH:(c + 1) * CH], state[:, d, c, :], qe[:, d, c * CH:(c + 1) * CH], start=False, stop=d == 1)
                        mm.then_inc(read_out, 1)
                        pe.wait_ge(squared, i + 1)
                        pe.matmul(ps[:, 6, :], ones[:, :], sq[:, :], start=True, stop=True).then_inc(summed, 1)

                    pe.sem_inc(head_done, 1)
                    pe.sem_inc(masked_ready, 1)
                    pe.sem_inc(read_out, 1)
                    project_q_forward(0)
                    project_v(0, range(TT + LT))
                    project_g(0)
                    project_backward(0)
                    with pe.Fori(0, HG_H - 1) as i:
                        head(i, True)
                    head(HG_H - 1, False)

                @block.scalar
                def _(act):
                    def stage_rows(r, u, dst, src, ctx_dst=None):
                        act.wait_ge(mm_done[u], turns[u] + r + 1)
                        act.activation(dst, src, ACT.Copy).then_inc(staged, 1)
                        if ctx_dst is not None:
                            act.activation(ctx_dst, ps[:, 5, L:2 * L] if u == 3 else ps[:, 3, 0:L], ACT.Copy).then_inc(staged, 1)

                    def stage_q(r):
                        stage_rows(r, 0, next_q[:, :], ps[:, 0, :])

                    def stage_forward(r):
                        stage_rows(r, 1, next_f[:, 0, 0:T], ps[:, 1, :], next_f[:, 0, T:])

                    def stage_v(r):
                        stage_rows(r, 3, next_v[:, 0:TT, :].rearrange("p t n -> p (t n)"), ps[:, 7, :],
                                   next_v[:, TT:, :].rearrange("p t n -> p (t n)"))

                    def stage_g(r):
                        stage_rows(r, 4, next_g[:, :], ps[:, 7, :])

                    def stage_backward(r):
                        stage_rows(r, 2, next_f[:, 1, 0:T], ps[:, 7, :], next_f[:, 1, T:])

                    def decays(i, d):
                        act.wait_ge(args, 4 * i + 2 * d + 1)
                        act.activation(kd[:, :], kd[:, :], ACT.Exp).then_inc(exps, 1)
                        act.activation(eb[:, d, :], b[:, d, 0:T], ACT.Exp).then_inc(exps, 1)

                    def cut_decays(i, d):
                        act.wait_ge(args, 4 * i + 2 * d + 2)
                        act.activation(cut[:, :, :], cut[:, :, :], ACT.Exp).then_inc(exps, 1)

                    def turned_keys(i, d):
                        act.wait_ge(turned, 2 * i + d + 1)
                        if d:
                            act.wait_ge(states_summed, 2 * i + 1)
                        act.activation(kdT[:, 0:TT, :].rearrange("p t n -> p (t n)"), ps[:, 4, :], ACT.Copy).then_inc(kdT_ready, 1)
                        act.activation(kdT[:, TT:, :].rearrange("p t n -> p (t n)"), ps[:, 5, 0:LT * P], ACT.Copy).then_inc(kdT_ready, 1)

                    def head(i, more):
                        act.wait_ge(staged, STAGED * i + STAGED)
                        act.activation(q[:, :], next_q[:, :], ACT.Silu)
                        act.activation(f[:, :, :], next_f[:, :, :], ACT.Sigmoid).then_inc(gates, 1)
                        act.wait_ge(head_done, i + 1)
                        act.activation(gate[:, :], next_g[:, :], ACT.Silu)
                        act.wait_ge(gates, 2 * i + 2)
                        act.activation(f[:, :, :], f[:, :, :], ACT.Ln).then_inc(logs, 1)
                        decays(i, 0)
                        if more:
                            stage_q(i + 1)
                        cut_decays(i, 0)
                        if more:
                            stage_forward(i + 1)
                        turned_keys(i, 0)
                        if more:
                            act.wait_ge(v_copied, i + 1)
                            stage_v(i + 1)
                        decays(i, 1)
                        if more:
                            stage_g(i + 1)
                        cut_decays(i, 1)
                        turned_keys(i, 1)
                        if more:
                            stage_backward(i + 1)
                        act.wait_ge(read_out, i + 2)
                        act.activation(sq[:, :], ps[:, 7, :], ACT.Square).then_inc(squared, 1)
                        act.wait_ge(meaned, i + 1)
                        act.activation(rstd[:, :], rstd[:, :], ACT.Sqrt).then_inc(rooted, 1)

                    act.activation(lb[:, 0, :, :], lb[:, 0, :, :], ACT.Sigmoid).then_inc(lb_ready, 1)
                    stage_q(0)
                    stage_forward(0)
                    stage_v(0)
                    stage_g(0)
                    stage_backward(0)
                    with act.Fori(0, HG_H - 1) as i:
                        head(i, True)
                    head(HG_H - 1, False)

                @block.vector
                def _(dve):
                    link = Chain(dve, hg_v)
                    dve.wait_ge(lb_ready, 1)
                    link(dve.tensor_scalar(lb[:, 1, :, :], lb[:, 0, :, :], -1.0, 1.0, ALU.mult, ALU.add))
                    lbs = lb[:, :, :, :].rearrange("p e d h -> p (e d) h")
                    dve.wait_ge(consts_in, 32)

                    def head(i):
                        dve.tensor_copy(cur[:, 0:4], lbs[:, :, ds(i, 1)].rearrange("p a h -> p (a h)"))
                        link(dve.tensor_copy(cur[:, 4:5], vA[:, ds(i + ROWS_A["hg_norm"], 1)]))
                        dve.wait_ge(read_out, i + 1)
                        dve.wait_ge(staged, STAGED * i + 5)
                        dve.tensor_copy(v[:, :, :], next_v[:, :, :]).then_inc(v_copied, 1)
                        dve.wait_ge(gates, 2 * i + 1)
                        for d in range(2):
                            last = dve.tensor_scalar(f[:, d, :], f[:, d, :], cur[:, 2 + d:3 + d], cur[:, d:d + 1], ALU.mult, ALU.add)
                        link(last)
                        dve.tensor_scalar(key[:, :, :], f[:, :, :], -1.0, 1.0, ALU.mult, ALU.add).then_inc(gates, 1)
                        dve.wait_ge(logs, i + 1)
                        for d in range(2):
                            go_ctx = go[:, 1, 0:1].broadcast_to([P, L])
                            flip = (lambda x: x) if d == 0 else (lambda x: x[:, ::-1])
                            dve.tensor_tensor_scan(flip(b[:, d, 0:T]), flip(go[:, d, :]), flip(f[:, d, 0:T]), 0.0, ALU.mult, ALU.add)
                            last = dve.tensor_tensor_scan(flip(b[:, d, T:T + L]), go_ctx, flip(f[:, d, T:T + L]), 0.0, ALU.mult, ALU.add)
                        link(last)
                        for d in range(2):
                            b4 = b[:, d, 0:T].rearrange("p (c j) -> p c j", j=CH)
                            end = b4[:, :, CH - 1:CH] if d == 0 else b4[:, :, 0:1]
                            ctx_end = b[:, d, T + L - 1:T + L] if d == 0 else b[:, d, T:T + 1]
                            if d:
                                dve.wait_ge(turned, 2 * i + 1)
                            dve.tensor_tensor(kd[:, 0:T].rearrange("p (c j) -> p c j", j=CH), end.broadcast_to([P, NCH, CH]), b4, ALU.subtract)
                            dve.tensor_tensor(kd[:, T:T + L], ctx_end.broadcast_to([P, L]), b[:, d, T:T + L], ALU.subtract).then_inc(args, 1)
                            if d:
                                dve.wait_ge(multiplied, 8 * i + 4)
                            for l in range(LEVELS):
                                bq, bk, mid = halves(b[:, d, 0:T], l, d)
                                oq, ok, _ = halves(cut[:, l, :], l, d)
                                wide = mid.broadcast_to(list(bq.shape))
                                dve.tensor_tensor(oq, bq, wide, ALU.subtract)
                                last = dve.tensor_tensor(ok, wide, bk, ALU.subtract)
                            last.then_inc(args, 1)
                            dve.wait_ge(exps, 6 * i + 3 * d + 1)
                            dve.tensor_tensor(kd[:, :], kd[:, :], key[:, d, :], ALU.mult).then_inc(kd_ready, 1)
                            dve.wait_ge(exps, 6 * i + 3 * d + 2)
                            dve.tensor_tensor(qe[:, d, :], eb[:, d, :], q[:, :], ALU.mult)
                            dve.wait_ge(exps, 6 * i + 3 * d + 3)
                            for l in range(LEVELS):
                                oq, ok, _ = halves(cut[:, l, :], l, d)
                                qq, _, _ = halves(q[:, :], l, d)
                                _, kk, _ = halves(key[:, d, 0:T], l, d)
                                dve.tensor_tensor(oq, oq, qq, ALU.mult)
                                last = dve.tensor_tensor(ok, ok, kk, ALU.mult)
                            last.then_inc(cuts, 1)
                            dve.wait_ge(states_summed, 2 * i + d + 1)
                            c0 = order[d][0]
                            link(dve.tensor_copy(state[:, d, c0, :], ps[:, 6, order[d][-1] * P:(order[d][-1] + 1) * P]))
                            for n, c in enumerate(order[d][:-1]):
                                nxt = order[d][n + 1]
                                e = last_of[d](c)
                                ins = dve.scalar_tensor_tensor(state[:, d, nxt, :], state[:, d, c, :], eb[:, d, e:e + 1],
                                                               ps[:, 6, c * P:(c + 1) * P], ALU.mult, ALU.add)
                                if n < NCH - 2:
                                    link(ins)
                            ins.then_inc(states_ready, 1)
                            for c in range(NCH):
                                n = NCH * d + c
                                dve.wait_ge(multiplied, 8 * i + n + 1)
                                link(dve.tensor_tensor(masked[:, n % 2, :, :].rearrange("p l t -> p (l t)"), ps[:, 2 * (n % 2):2 * (n % 2) + 2, :].rearrange("p b n -> p (b n)"),
                                                       pairs[:, d, :, :].rearrange("p l t -> p (l t)"), ALU.mult))
                                dve.tensor_reduce(at_[:, d, c, :], masked[:, n % 2, :, :].rearrange("p l t -> p t l"), AX.X, ALU.add).then_inc(masked_ready, 1)
                        dve.wait_ge(summed, i + 1)
                        dve.tensor_scalar(rstd[:, :], ps[:, 6, :], 1.0 / DK, EPS1, ALU.mult, ALU.add).then_inc(meaned, 1)
                        dve.wait_ge(rooted, i + 1)
                        link(dve.reciprocal(rstd[:, :], rstd[:, :]))
                        link(dve.scalar_tensor_tensor(sq[:, :], ps[:, 7, :], cur[:, 4:5], rstd[:, :], ALU.mult, ALU.mult))
                        dve.tensor_tensor(yT[:, ds(i + NA_H * DH // P, 1), :].rearrange("p a t -> p (a t)"), sq[:, :], gate[:, :], ALU.mult).then_inc(head_done, 1)

                    with dve.Fori(0, HG_H - 1) as i:
                        link.loop(i, HG_LINKS)
                        head(i)
                    link.end(HG_H - 1)
                    head(HG_H - 1)
            end_ring(5, HG_H)
    def residual_block(name, n, tiles, pieces, gate):
        per, turns_ = SPLIT, n // SPLIT
        with ExitStack() as local:
            parts = split_buffers(local, name)
            with nc.Block() as block:
                @block.sync
                def _(sp):
                    with sp.Fori(0, turns_) as i:
                        for u in range(per):
                            load_split(sp, u, i, *tiles(u, i * (per * P) + u * P))

                @block.tensor
                def _(pe):
                    for u in range(per):
                        product(pe, parts, u, 0, ps[:, u, :], parts[2], parts[3], chunk_in=rhs_in(pe) if u == 0 else None)
                    with pe.Fori(1, turns_) as i:
                        for u in range(per):
                            product(pe, parts, u, i, ps[:, u, :], parts[2], parts[3])

                @block.scalar
                def _(act):
                    rhs_hi(act, parts, yT)
                    with act.Fori(0, turns_) as i:
                        for u in range(per):
                            split_hi(act, parts, u, i, pieces)

                @block.vector
                def _(dve):
                    def add(u, i):
                        projected(dve, u, i)
                        x = xT[:, ds(i * per + u, 1), :].rearrange("p a t -> p (a t)")
                        if gate is None:
                            dve.tensor_tensor(x, ps[:, u, :], x, ALU.add).then_inc(evacuated[u], 1)
                        else:
                            dve.scalar_tensor_tensor(x, ps[:, u, :], gate(i * per + u), x, ALU.mult, ALU.add).then_inc(evacuated[u], 1)

                    rhs_lo(dve, parts, yT)
                    for u in range(per):
                        split_lo(dve, parts, u, 0)
                    with dve.Fori(1, turns_) as i:
                        for u in range(per):
                            add(u, i - 1)
                            split_lo(dve, parts, u, i)
                    for u in range(per):
                        add(u, turns_ - 1)
            end_split(per, turns_, pieces)

    plain = lambda w: (lambda u, c0: [(wslot[:, u, :, :], weights(w, c0))])
    residual_block("wo", KC, plain(io["w_out"]), 1, lambda j: mod[:, ds(j + 2 * KC, 1), 0])

    rms_block("n2", [(xT, T, [(hT, lambda k: gain2[:, k:k + 1], lambda k: mod[:, 3 * KC + k, 0:1])])], [EPS1])
    with ExitStack() as local:
        RING = TOPK
        htok = sb("pe_htok", [P, TT, D], on=local)
        ring = sb("pe_ring", [P, RING, D], on=local)
        qT = sb("pe_qT", [P, 2, T], on=local)
        keys = sb("pe_keys", [P, 2, P], on=local)
        keysT = sb("pe_keysT", [P, 2, P], on=local)
        s = sb("pe_s", [P, 2, TT, NKEYS], on=local)
        top = sb("pe_top", [P, 2, TT, TOPK], on=local)
        itop = sb("pe_itop", [P, 2, TT, TOPK], U32, on=local)
        itopf = sb("pe_itopf", [P, 2, TT, TOPK], on=local)
        cand = sb("pe_cand", [P, TT, TOPK, TOPK], on=local)
        best = sb("pe_best", [P, TT, TOPK], on=local)
        pos = sb("pe_pos", [P, TT, TOPK], U32, on=local)
        place = sb("pe_place", [P, 2, TT, TOPK], U32, on=local)
        placef = sb("pe_placef", [P, 2, TT, TOPK], on=local)
        pick = sb("pe_pick", [P, 2, TT * TOPK, TOPK], on=local)
        picked = sb("pe_picked", [P, 2, TT, TOPK], on=local)
        idx = sb("pe_idx", [P, 2, TT * TOPK], U32, on=local)
        g = sb("pe_g", [P, 2, TT, TOPK], on=local)
        soft = sb("pe_soft", [P, TT, TOPK], on=local)
        total = sb("pe_total", [P, TT], on=local)
        dots = sb("pe_dots", [P, TT * TOPK], on=local)
        act_ = sb("pe_act", [P, TT * TOPK], on=local)
        wgt = sb("pe_wgt", [P, TT * TOPK], on=local)
        DIAGS = 4
        diag = sb("pe_diag", [P, DIAGS, P], on=local)
        iota16 = sb("pe_iota16", [P, TOPK], on=local)
        acc = yT[:, :, :].rearrange("p (t h) n -> p t (h n)", t=TT)
        h_turned, h_left = sem("pe_h_turned"), sem("pe_h_left")
        with nc.Block() as block:
            @block.tensor
            def _(pe):
                for t in range(TT):
                    if t >= 2:
                        pe.wait_ge(h_left, t - 1)
                    for k in range(KC):
                        mm = pe.transpose(ps[:, 2 * (t % 2) + k // 4, k % 4 * P:(k % 4 + 1) * P], hT[:, k, t * P:(t + 1) * P], ident[:, :])
                    mm.then_inc(h_turned, 1)

            @block.scalar
            def _(act):
                for t in range(TT):
                    act.wait_ge(h_turned, t + 1)
                    act.activation(htok[:, t, :], ps[:, 2 * (t % 2):2 * (t % 2) + 2, :].rearrange("p b n -> p (b n)"), ACT.Copy).then_inc(h_left, 1)

        land = [sem(f"pe_land{k}") for k in range(RING)]
        dot_done, v_used, gelu_done, wgt_done, diag_done, added = (sem("pe_dot_done"), sem("pe_v_used"), sem("pe_gelu_done"),
                                                            sem("pe_wgt_done"), sem("pe_diag_done"), sem("pe_added"))
        keys_in, keys_turned, q_ready, scored, s_ready, top_done = (sem("pe_keys_in"), sem("pe_keys_turned"), sem("pe_q_ready"),
                                                            sem("pe_scored"), sem("pe_s_ready"), sem("pe_top_done"))
        soft_arg, soft_exp, idx_ready, pe_v, iota_in = sem("pe_soft_arg"), sem("pe_soft_exp"), sem("pe_idx_ready"), sem("pe_chain"), sem("pe_iota_in")
        BLOCKS = [("u", 0), ("u", 1), ("v", 0), ("u", 2), ("v", 1), ("u", 3), ("v", 2), ("v", 3)]
        CREDIT = TOPK
        PER = TT * TOPK
        NBLK = len(BLOCKS)
        HEAD_LINKS = 5 + 6 + 7

        def consumed(eng, kind, h, t, k):
            eng.wait_ge(dot_done if kind == "u" else v_used, h * PER + (t * TOPK + k + 1 + (CREDIT if kind == "v" else 0)))

        def arrived(eng, kind, h, t, k):
            eng.wait_ge(land[k], h * (16 * NBLK) + 16 * (BLOCKS.index((kind, t)) + 1))

        with nc.Block() as block:
            @block.sync
            def _(sp):
                sp.dma_start(iota16[:, :], io["const_iota16"]).then_inc(iota_in, 16)

                def load_head(r, head):
                    for side in range(2):
                        load_weights(sp, side, r, (wslot[:, side, :, :], weights(io["wq"], head * (2 * P) + side * P)))
                    sp.wait_ge(keys_turned, r)
                    sp.dma_start(keys[:, :, :], io["keys"][ds(head * (2 * P), 2 * P), :].rearrange("(s k) d -> k s d", s=2)).then_inc(keys_in, 16)

                load_head(0, 0)
                with sp.Fori(0, PE_H // 2) as i:
                    after = (i * 2 + 2) % PE_H
                    load_head(i * 2 + 1, i * 2 + 1)
                    load_head(i * 2 + 2, after)

            @block.gpsimd
            def _(pool):
                def gathers(h, par):
                    for n, (kind, t) in enumerate(BLOCKS):
                        if n == 0:
                            pool.wait_ge(idx_ready, h + 1)
                        for k in range(TOPK):
                            if n:
                                consumed(pool, BLOCKS[n - 1][0], h, BLOCKS[n - 1][1], k)
                            else:
                                pool.wait_ge(v_used, h * PER + k + 1)
                            j = t * TOPK + k
                            pool.nop(nofuse=True)
                            pool.indirect_dma_start(ring[:, k, :], None, io[kind], bass.IndirectOffsetOnAxis(idx[:, par, j:j + 1], 0)).then_inc(land[k], 16)

                with pool.Fori(0, PE_H // 2) as i:
                    for par in range(2):
                        gathers(i * 2 + par, par)

            @block.tensor
            def _(pe):
                def route(r):
                    pe.wait_ge(q_ready, r * 3)
                    for side in range(2):
                        weights_in(pe, side, r)
                        for k in range(KC):
                            mm = pe.matmul(ps[:, 4 + side, :], wslot[:, side, k, :], hT[:, k, :], start=k == 0, stop=k == KC - 1)
                        mm.then_inc(mm_done[side], 1)
                    pe.wait_ge(keys_in, r * 16 + 16)
                    pe.wait_ge(s_ready, r * 2)
                    for side in range(2):
                        mm = pe.transpose(ps[:, 6, side * P:(side + 1) * P], keys[:, side, :], ident[:, :])
                    mm.then_inc(keys_turned, 1)
                    pe.wait_ge(q_ready, r * 3 + 3)
                    for side in range(2):
                        for t in range(TT):
                            mm = pe.matmul(ps[:, 6 + side, t * P:(t + 1) * P], qT[:, side, t * P:(t + 1) * P], keysT[:, side, :], start=True, stop=True)
                    mm.then_inc(scored, 1)

                def sum_v(h, t):
                    pe.wait_ge(added, h * TT + t + 1)
                    for k in range(TOPK):
                        arrived(pe, "v", h, t, k)
                        pe.wait_ge(diag_done, h * PER + t * TOPK + k + 1)
                        for half in range(2):
                            mm = pe.matmul(ps[:, 2 * (t % 2) + half, :], diag[:, k % DIAGS, :], ring[:, k, half * 512:(half + 1) * 512],
                                           start=k == 0, stop=k == TOPK - 1)
                        mm.then_inc(v_used, 1)

                pe.sem_inc(v_used, CREDIT)
                route(0)
                with pe.Fori(0, PE_H // 2) as i:
                    for par in range(2):
                        route(i * 2 + par + 1)
                        for t in range(TT):
                            sum_v(i * 2 + par, t)

            @block.scalar
            def _(act):
                def route(r):
                    for side in range(2):
                        act.wait_ge(mm_done[side], turns[side] + r + 1)
                        act.activation(qT[:, side, :], ps[:, 4 + side, :], ACT.Copy).then_inc(q_ready, 1)
                    act.wait_ge(keys_turned, r + 1)
                    act.activation(keysT[:, :, :].rearrange("p s n -> p (s n)"), ps[:, 6, 0:2 * P], ACT.Copy).then_inc(q_ready, 1)
                    act.wait_ge(scored, r + 1)
                    act.wait_ge(top_done, r)
                    for side in range(2):
                        act.activation(s[:, side, :, :].rearrange("p t n -> p (t n)"), ps[:, 6 + side, :], ACT.Copy).then_inc(s_ready, 1)

                def route_exp(r):
                    act.wait_ge(soft_arg, r + 1)
                    act.activation(soft[:, :, :], soft[:, :, :], ACT.Exp).then_inc(soft_exp, 1)

                def gelu(h, t):
                    act.wait_ge(dot_done, h * PER + (t + 1) * TOPK)
                    act.activation(act_[:, t * TOPK:(t + 1) * TOPK], dots[:, t * TOPK:(t + 1) * TOPK], ACT.Gelu).then_inc(gelu_done, 1)

                def diags(h, t):
                    act.wait_ge(wgt_done, h * TT + t + 1)
                    for k in range(TOPK):
                        n = t * TOPK + k
                        act.wait_ge(v_used, h * PER + (n + 1 + CREDIT - DIAGS))
                        act.activation(diag[:, k % DIAGS, :], ident[:, :], ACT.Copy, scale=wgt[:, n:n + 1]).then_inc(diag_done, 1)

                route(0)
                route_exp(0)
                with act.Fori(0, PE_H // 2) as i:
                    for par in range(2):
                        h = i * 2 + par
                        gelu(h, 0)
                        route(h + 1)
                        gelu(h, 1)
                        diags(h, 0)
                        gelu(h, 2)
                        diags(h, 1)
                        gelu(h, 3)
                        route_exp(h + 1)
                        diags(h, 2)
                        diags(h, 3)

            @block.vector
            def _(dve):
                link = Chain(dve, pe_v)
                tiles = [(side, t) for side in range(2) for t in range(TT)]

                def best_keys(r):
                    dve.wait_ge(s_ready, r * 2 + 2)
                    for lo in (0, 8):
                        dve.nop(nofuse=True)
                        for side, t in tiles:
                            last = dve.max(top[:, side, t, lo:lo + 8], s[:, side, t, :])
                        link(last)
                        dve.nop(nofuse=True)
                        for side, t in tiles:
                            last = dve.max_index(itop[:, side, t, lo:lo + 8], top[:, side, t, lo:lo + 8], s[:, side, t, :])
                        if lo == 0:
                            link(last)
                            dve.nop(nofuse=True)
                            for side, t in tiles:
                                last = dve.match_replace(s[:, side, t, :], top[:, side, t, 0:8], s[:, side, t, :], -3e38)
                            link(last)
                        else:
                            link(last)
                    dve.tensor_copy(itopf[:, :, :, :], itop[:, :, :, :]).then_inc(top_done, 1)

                def best_pairs(r):
                    link(dve.tensor_tensor(cand[:, :, :, :], top[:, 0, :, :].unsqueeze(3).broadcast_to([P, TT, TOPK, TOPK]),
                                           top[:, 1, :, :].unsqueeze(2).broadcast_to([P, TT, TOPK, TOPK]), ALU.add))
                    flat = [cand[:, t, :, :].rearrange("p a b -> p (a b)") for t in range(TT)]
                    for lo in (0, 8):
                        dve.nop(nofuse=True)
                        for t in range(TT):
                            last = dve.max(best[:, t, lo:lo + 8], flat[t])
                        link(last)
                        dve.nop(nofuse=True)
                        for t in range(TT):
                            last = dve.max_index(pos[:, t, lo:lo + 8], best[:, t, lo:lo + 8], flat[t])
                        link(last)
                        if lo == 0:
                            dve.nop(nofuse=True)
                            for t in range(TT):
                                last = dve.match_replace(flat[t], best[:, t, 0:8], flat[t], -3e38)
                            link(last)
                    dve.tensor_tensor(soft[:, :, :], best[:, :, :], best[:, :, 0:1].broadcast_to([P, TT, TOPK]), ALU.subtract).then_inc(soft_arg, 1)

                def experts(r, par):
                    dve.tensor_scalar(place[:, 0, :, :], pos[:, :, :], 4, None, ALU.logical_shift_right)
                    link(dve.tensor_scalar(place[:, 1, :, :], pos[:, :, :], TOPK - 1, None, ALU.bitwise_and))
                    link(dve.tensor_copy(placef[:, :, :, :], place[:, :, :, :]))
                    for side in range(2):
                        last = dve.tensor_tensor(pick[:, side, :, :], placef[:, side, :, :].rearrange("p t k -> p (t k)").unsqueeze(2).broadcast_to([P, PER, TOPK]),
                                                 iota16[:, :].unsqueeze(1).broadcast_to([P, PER, TOPK]), ALU.is_equal)
                    link(last)
                    for side in range(2):
                        p4 = pick[:, side, :, :].rearrange("p (t k) a -> p t k a", t=TT)
                        last = dve.tensor_tensor(p4, p4, itopf[:, side, :, :].unsqueeze(2).broadcast_to([P, TT, TOPK, TOPK]), ALU.mult)
                    link(last)
                    for side in range(2):
                        last = dve.tensor_reduce(picked[:, side, :, :].rearrange("p t k -> p (t k)"), pick[:, side, :, :], AX.X, ALU.add)
                    link(last)
                    dve.wait_ge(soft_exp, r + 1)
                    link(dve.tensor_reduce(total[:, :], soft[:, :, :], AX.X, ALU.add))
                    link(dve.reciprocal(total[:, :], total[:, :]))
                    dve.tensor_tensor(g[:, par, :, :], soft[:, :, :], total[:, :].unsqueeze(2).broadcast_to([P, TT, TOPK]), ALU.mult)
                    flat = lambda x: x.rearrange("p t k -> p (t k)")
                    dve.scalar_tensor_tensor(idx[:, par, :], flat(picked[:, 0, :, :]), float(NKEYS), flat(picked[:, 1, :, :]), ALU.mult, ALU.add).then_inc(idx_ready, 1)

                def dot(h, t):
                    for k in range(TOPK):
                        arrived(dve, "u", h, t, k)
                        j = t * TOPK + k
                        dve.tensor_tensor_reduce(ring[:, k, :], ring[:, k, :], htok[:, t, :], 1.0, 0.0, ALU.mult, ALU.add, dots[:, j:j + 1]).then_inc(dot_done, 1)

                def weigh(h, t, par):
                    dve.wait_ge(gelu_done, h * TT + t + 1)
                    dve.tensor_tensor(wgt[:, t * TOPK:(t + 1) * TOPK], act_[:, t * TOPK:(t + 1) * TOPK], g[:, par, t, :], ALU.mult).then_inc(wgt_done, 1)

                def add_v(h, t):
                    dve.wait_ge(v_used, h * PER + (t * TOPK + TOPK + CREDIT))
                    dve.tensor_tensor(acc[:, t, :], ps[:, 2 * (t % 2):2 * (t % 2) + 2, :].rearrange("p b n -> p (b n)"), acc[:, t, :], ALU.add).then_inc(added, 1)

                dve.sem_inc(added, 2)
                dve.wait_ge(iota_in, 16)
                link(dve.memset(acc, 0.0))
                best_keys(0)
                best_pairs(0)
                link(dve.memset(total[:, :], 0.0))
                experts(0, 0)
                with dve.Fori(0, PE_H // 2) as i:
                    link.loop(i, 2 * HEAD_LINKS)
                    for par in range(2):
                        h = i * 2 + par
                        dot(h, 0)
                        dot(h, 1)
                        weigh(h, 0, par)
                        best_keys(h + 1)
                        dot(h, 2)
                        weigh(h, 1, par)
                        add_v(h, 0)
                        best_pairs(h + 1)
                        dot(h, 3)
                        weigh(h, 2, par)
                        add_v(h, 1)
                        experts(h + 1, 1 - par)
                        weigh(h, 3, par)
                        add_v(h, 2)
                        add_v(h, 3)
                link.end(PE_H // 2)
        end_ring(2, PE_H + 1)
        o_turned, o_left = sem("pe_o_turned"), sem("pe_o_left")
        with nc.Block() as block:
            @block.tensor
            def _(pe):
                for k in range(KC):
                    if k >= 4:
                        pe.wait_ge(o_left, k - 3)
                    for t in range(TT):
                        mm = pe.transpose(ps[:, k % 4, t * P:(t + 1) * P], acc[:, t, k * P:(k + 1) * P], ident[:, :])
                    mm.then_inc(o_turned, 1)

            @block.vector
            def _(dve):
                for k in range(KC):
                    dve.wait_ge(o_turned, k + 1)
                    dve.scalar_tensor_tensor(xT[:, k, :], ps[:, k % 4, :], mod[:, 5 * KC + k, 0:1], xT[:, k, :], ALU.mult, ALU.add).then_inc(o_left, 1)
    rms_block("nf", [(xT, T, [(xT, gain(vA, ROWS_A["norm_f"]), None)])], [EPS1])

    def memory_attention(name, layer, w_q, q0):
        PAIRS = 2
        with ExitStack() as local:
            qT = sb(f"{name}_q", [P, T], on=local)
            kT = sb(f"{name}_k", [P, MEM], on=local)
            v = sb(f"{name}_v", [P, MEM // P, P], on=local)
            zeros = sb(f"{name}_zeros", [P, MEM], on=local)
            evac, pair_out, chain = sem(f"{name}_evac"), sem(f"{name}_pair_out"), sem(f"{name}_chain")
            units = [dict(q=qT[64 * h:64 * h + 64, t * P:(t + 1) * P], k=[(kT[64 * h:64 * h + 64, :], MEM)], sink=None, bias=[None],
                          v=[v[:, m, 64 * h:64 * h + 64] for m in range(MEM // P)], out=ps[64 * h:64 * h + 64, 6, t * P:(t + 1) * P])
                     for h in range(2) for t in range(TT)]
            a = Attention(name, local, units, 4)
            w_kv = io["mem_kv"][layer * D:(layer + 1) * D, :]
            with nc.Block() as block:
                @block.sync
                def _(sp):
                    with sp.Fori(0, PAIRS) as i:
                        for u, (w, c0) in enumerate([(w_q, q0), (w_kv, 0), (w_kv, 2 * P)]):
                            load_weights(sp, u, i, (wslot[:, u, :, :], weights(w, i * P + c0)))

                @block.tensor
                def _(pe):
                    pe.sem_inc(pair_out, 1)
                    with pe.Fori(0, PAIRS) as i:
                        pe.wait_ge(att_logit_ready, a.at(i))
                        for u, rhs, n in ((0, hT, T), (1, memT, MEM)):
                            weights_in(pe, u, i)
                            for k in range(KC):
                                mm = pe.matmul(ps[:, u, 0:n], wslot[:, u, k, :], rhs[:, k, :], start=k == 0, stop=k == KC - 1)
                            mm.then_inc(mm_done[u], 1)
                        weights_in(pe, 2, i)
                        for m in range(MEM // P):
                            for k in range(KC):
                                mm = pe.matmul(ps[:, 2, m * P:(m + 1) * P], memT[:, k, m * P:(m + 1) * P], wslot[:, 2, k, :], start=k == 0, stop=k == KC - 1)
                        mm.then_inc(mm_done[2], 1)
                        pe.wait_ge(evac, 3 * i + 3)
                        att_pe(pe, a, i, lambda u: pe.wait_ge(pair_out, i + 1) if u == 0 else None)

                @block.scalar
                def _(act):
                    with act.Fori(0, PAIRS) as i:
                        act.wait_ge(att_weighted, a.at(i))
                        projected(act, 0, i)
                        act.activation(qT[:, :], ps[:, 0, :], ACT.Copy, scale=DH ** -0.5).then_inc(evac, 1)
                        att_act(act, a, i)
                        act.wait_ge(att_weighted, a.at(i) + a.n)
                        act.activation(yT[:, i + CONV // P, :], ps[:, 6, :], ACT.Copy).then_inc(pair_out, 1)

                @block.vector
                def _(dve):
                    link = Chain(dve, chain)
                    link(dve.memset(zeros[:, :], 0.0))
                    with dve.Fori(0, PAIRS) as i:
                        link.loop(i, att_links(a))
                        dve.wait_ge(att_weighted, a.at(i))
                        projected(dve, 1, i)
                        dve.tensor_copy(kT[:, :], ps[:, 1, 0:MEM]).then_inc(evac, 1)
                        projected(dve, 2, i)
                        dve.tensor_copy(v[:, :, :].rearrange("p t n -> p (t n)"), ps[:, 2, 0:MEM]).then_inc(evac, 1)
                        att_dve(dve, a, i, link, zeros)
                    link.end(PAIRS)
            end_ring(3, PAIRS)
            a.end(PAIRS)

    def feed_forward(name, layer):
        per = 2
        stages, t0 = [], 0
        for f0 in range(0, FT, KC):
            n = min(KC, FT - f0)
            stages += [("in", f0, n, t0, n // per), ("out", f0, n, t0 + n // per, KC // SPLIT)]
            t0 += n // per + KC // SPLIT
        TURNS = t0
        with ExitStack() as local:
            parts = split_buffers(local, name)
            hid_hi = sb(f"{name}_hid_hi", [P, KC, T], F32R, on=local)
            hid_lo = sb(f"{name}_hid_lo", [P, KC, T], F32R, on=local)
            half = sb(f"{name}_half", [P, per, T], on=local)
            hidden = sb(f"{name}_hidden", [P, per, T], on=local)
            hid_hi_ready, hid_ready = sem(f"{name}_hid_hi_ready"), sem(f"{name}_hid_ready")
            rows = slice(layer * D, (layer + 1) * D)
            with nc.Block() as block:
                @block.sync
                def _(sp):
                    for kind, f0, n, b, count in stages:
                        down = io["down"][layer * D_FF + f0 * P:layer * D_FF + (f0 + n) * P, :].rearrange("(k p) n -> p k n", p=P)
                        with sp.Fori(0, count) as i:
                            for u in range(SPLIT):
                                if kind == "in":
                                    w = io["gate" if u % 2 == 0 else "up"][rows, :]
                                    load_split(sp, u, i + b, (wslot[:, u, :, :], weights(w, i * (per * P) + (f0 + u // 2) * P)))
                                else:
                                    load_split(sp, u, i + b, (wslot[:, u, 0:n, :], down[:, :, ds(i * (SPLIT * P) + u * P, P)]))

                @block.tensor
                def _(pe):
                    for kind, f0, n, b, count in stages:
                        def turn(t, chunk_in):
                            for u in range(SPLIT):
                                hi, lo = (parts[2], parts[3]) if kind == "in" else (hid_hi, hid_lo)
                                product(pe, parts, u, t, ps[:, u, :], hi, lo, KC if kind == "in" else n, chunk_in if u == 0 else None)

                        if kind == "in":
                            turn(b, rhs_in(pe) if f0 == 0 else None)
                        else:
                            turn(b, lambda k: pe.wait_ge(hid_ready, f0 + k + 1))
                        with pe.Fori(b + 1, b + count) as t:
                            turn(t, None)

                @block.scalar
                def _(act):
                    rhs_hi(act, parts, hT)
                    for u in range(SPLIT):
                        split_hi(act, parts, u, 0)
                    for kind, f0, n, b, count in stages:
                        def turn(i, last):
                            t = i + b
                            if kind == "in":
                                for m in range(per):
                                    projected(act, 2 * m, t)
                                    act.activation(half[:, m, :], ps[:, 2 * m, :], ACT.Silu).then_inc(evacuated[2 * m], 1)
                                    split_hi(act, parts, 2 * m, t + 1)
                                    act.wait_ge(evacuated[2 * m + 1], left[2 * m + 1] + t + 1)
                                    act.activation(hid_hi[:, ds(i * per + m, 1), :].rearrange("p a t -> p (a t)"), hidden[:, m, :],
                                                   ACT.Copy).then_inc(hid_hi_ready, 1)
                                    split_hi(act, parts, 2 * m + 1, t + 1)
                            elif not last:
                                for u in range(SPLIT):
                                    split_hi(act, parts, u, t + 1)

                        end = b + count == TURNS
                        with act.Fori(0, count - end) as i:
                            turn(i, False)
                        if end:
                            turn(count - 1, True)

                @block.vector
                def _(dve):
                    rhs_lo(dve, parts, hT)
                    for u in range(SPLIT):
                        split_lo(dve, parts, u, 0)
                    for kind, f0, n, b, count in stages:
                        def turn(i, last):
                            t = i + b
                            if kind == "in":
                                for m in range(per):
                                    split_lo(dve, parts, 2 * m, t + 1)
                                    dve.wait_ge(evacuated[2 * m], left[2 * m] + t + 1)
                                    projected(dve, 2 * m + 1, t)
                                    dve.tensor_tensor(hidden[:, m, :], half[:, m, :], ps[:, 2 * m + 1, :], ALU.mult).then_inc(evacuated[2 * m + 1], 1)
                                    dve.wait_ge(hid_hi_ready, i * per + (f0 + m + 1))
                                    dve.tensor_tensor(hid_lo[:, ds(i * per + m, 1), :].rearrange("p a t -> p (a t)"), hidden[:, m, :],
                                                      hid_hi[:, ds(i * per + m, 1), :].rearrange("p a t -> p (a t)").bitcast(F32), ALU.subtract).then_inc(hid_ready, 1)
                                    split_lo(dve, parts, 2 * m + 1, t + 1)
                            else:
                                for u in range(SPLIT):
                                    projected(dve, u, t)
                                    x = xT[:, ds(i * SPLIT + u, 1), :].rearrange("p a t -> p (a t)")
                                    dve.tensor_tensor(x, ps[:, u, :], x, ALU.add).then_inc(evacuated[u], 1)
                                    if not last:
                                        split_lo(dve, parts, u, t + 1)

                        end = b + count == TURNS
                        with dve.Fori(0, count - end) as i:
                            turn(i, False)
                        if end:
                            turn(count - 1, True)
            end_split(SPLIT, TURNS)

    rms_block("m0", [(xT, T, [(hT, gain(vB, ROWS_B["norm_mix"]), None)])], [EPS2])
    CT = CONV // P
    with ExitStack() as local:
        PAD = 2
        parts = split_buffers(local, "cv")
        gated = sb("cv_gated", [P, PAD + T], on=local)
        uu = sb("cv_u", [P, T], on=local)
        conv = sb("cv_conv", [P, 2, T], on=local)
        taps = sb("cv_taps", [P, 3], on=local)
        cv_v = sem("cv_chain")
        with nc.Block() as block:
            @block.sync
            def _(sp):
                with sp.Fori(0, CT) as i:
                    for u, c0 in ((0, 0), (1, 2 * CONV), (2, CONV)):
                        load_split(sp, u, i, (wslot[:, u, :, :], weights(io["a_in"], i * P + c0)))

            @block.tensor
            def _(pe):
                for u in range(3):
                    product(pe, parts, u, 0, ps[:, u, :], parts[2], parts[3], chunk_in=rhs_in(pe) if u == 0 else None)
                with pe.Fori(1, CT) as i:
                    for u in range(3):
                        product(pe, parts, u, i, ps[:, u, :], parts[2], parts[3])

            @block.scalar
            def _(act):
                rhs_hi(act, parts, hT)
                for u in range(3):
                    split_hi(act, parts, u, 0)

                def turn(i, last):
                    act.wait_ge(evacuated[1], left[1] + i)
                    projected(act, 0, i)
                    act.activation(uu[:, :], ps[:, 0, :], ACT.Copy).then_inc(evacuated[0], 1)
                    for u in range(0 if last else 3):
                        split_hi(act, parts, u, i + 1)

                with act.Fori(0, CT - 1) as i:
                    turn(i, False)
                turn(CT - 1, True)

            @block.vector
            def _(dve):
                link = Chain(dve, cv_v)
                rhs_lo(dve, parts, hT)
                for u in range(3):
                    split_lo(dve, parts, u, 0)
                link(dve.memset(gated[:, 0:PAD], 0.0))

                def turn(i, last):
                    dve.tensor_copy(taps[:, :], vB[:, ROWS_B["conv"]:ROWS_B["conv"] + 3 * CT].rearrange("p (k j) -> p j k", k=3)[:, ds(i, 1), :].rearrange("p a k -> p (a k)"))
                    dve.wait_ge(evacuated[0], left[0] + i + 1)
                    projected(dve, 1, i)
                    dve.tensor_tensor(gated[:, PAD:], uu[:, :], ps[:, 1, :], ALU.mult).then_inc(evacuated[1], 1)
                    if not last:
                        split_lo(dve, parts, 0, i + 1)
                    dve.wait_ge(evacuated[1], left[1] + i + 1)
                    link(dve.tensor_scalar(conv[:, 0, :], gated[:, 0:T], taps[:, 0:1], None, ALU.mult))
                    link(dve.scalar_tensor_tensor(conv[:, 1, :], gated[:, 1:T + 1], taps[:, 1:2], conv[:, 0, :], ALU.mult, ALU.add))
                    link(dve.scalar_tensor_tensor(conv[:, 0, :], gated[:, 2:T + 2], taps[:, 2:3], conv[:, 1, :], ALU.mult, ALU.add))
                    if not last:
                        split_lo(dve, parts, 1, i + 1)
                    projected(dve, 2, i)
                    dve.tensor_tensor(yT[:, ds(i, 1), :].rearrange("p a t -> p (a t)"), conv[:, 0, :], ps[:, 2, :], ALU.mult).then_inc(evacuated[2], 1)
                    if not last:
                        split_lo(dve, parts, 2, i + 1)

                with dve.Fori(0, CT - 1) as i:
                    link.loop(i, 3)
                    turn(i, False)
                link.end(CT - 1)
                turn(CT - 1, True)
        end_split(3, CT)
    memory_attention("ma0", 0, io["a_in"], 3 * CONV)
    residual_block("ao", KC, plain(io["a_out"]), 1, None)
    rms_block("f0", [(xT, T, [(hT, gain(vB, ROWS_B["norm_ffn"]), None)])], [EPS2])
    feed_forward("ff0", 0)

    with ExitStack() as local:
        hkv = sb("sw_hkv", [P, KC, T], on=local)
        rms_block("m1", [(xT, T, [(hkv, gain(vB, ROWS_B["kv_norm"]), None), (hT, gain(vB, ROWS_B["norm_mix"] + KC), None)])], [EPS2])
        HALVES = KV_H // 2
        HPT = 2 * GROUP
        qT = sb("sw_q", [P, GROUP, T], on=local)
        kT = sb("sw_k", [P, T], on=local)
        v = sb("sw_v", [P, TT, P], on=local)
        bias = sb("sw_bias_now", [P, HPT, 2 * P], on=local)
        sink = sb("sw_sink_now", [P, HPT], on=local)
        evac, tile_out, sw_v = sem("sw_evac"), sem("sw_tile_out"), sem("sw_chain")
        units = []
        for j in range(GROUP):
            for kv in range(2):
                hp, h = slice(64 * kv, 64 * kv + 64), kv * GROUP + j
                for n in range(TT):
                    first = max(n - 1, 0)
                    w = (n + 1 - first) * P
                    units.append(dict(q=qT[hp, j, n * P:(n + 1) * P], k=[(kT[hp, first * P:(n + 1) * P], w)], sink=sink[:, h:h + 1],
                                      bias=[bias[:, h, 2 * P - w:2 * P]], v=[v[:, b, hp] for b in range(first, n + 1)],
                                      out=ps[hp, 6 + j % 2, n * P:(n + 1) * P]))
        a = Attention("sw", local, units, 4)
        PERJ = 2 * TT
        QW = HPT * DH
        with nc.Block() as block:
            @block.sync
            def _(sp):
                with sp.Fori(0, HALVES) as i:
                    for j in range(GROUP):
                        load_weights(sp, j, i, *[(wslot[:, j, :, kv * DH:(kv + 1) * DH], weights(io["b_q"], i * QW + (kv * GROUP * DH + j * DH), DH))
                                                 for kv in range(2)])
                    for u, c0 in ((3, 0), (4, KV_H * DH)):
                        load_weights(sp, u, i, (wslot[:, u, :, :], weights(io["w_kv"], i * P + c0)))

            @block.tensor
            def _(pe):
                pe.sem_inc(tile_out, 1)
                with pe.Fori(0, HALVES) as i:
                    pe.wait_ge(att_logit_ready, a.at(i))
                    pe.wait_ge(att_pT_ready, a.at(i))
                    for u in range(GROUP + 1):
                        weights_in(pe, u, i, 2 if u < GROUP else 1)
                        for k in range(KC):
                            mm = pe.matmul(ps[:, u, :], wslot[:, u, k, :], (hT if u < GROUP else hkv)[:, k, :], start=k == 0, stop=k == KC - 1)
                        mm.then_inc(mm_done[u], 1)
                    weights_in(pe, 4, i)
                    for t in range(TT):
                        for k in range(KC):
                            mm = pe.matmul(ps[:, 4, t * P:(t + 1) * P], hkv[:, k, t * P:(t + 1) * P], wslot[:, 4, k, :], start=k == 0, stop=k == KC - 1)
                    mm.then_inc(mm_done[4], 1)
                    pe.wait_ge(evac, 5 * i + 5)

                    def accumulator_free(u):
                        if u == 0:
                            pe.wait_ge(tile_out, GROUP * i + 1)
                        if u == 2 * PERJ:
                            pe.wait_ge(tile_out, GROUP * i + 2)

                    att_pe(pe, a, i, accumulator_free)

            @block.scalar
            def _(act):
                with act.Fori(0, HALVES) as i:
                    act.wait_ge(att_weighted, a.at(i))
                    for j in range(GROUP):
                        projected(act, j, i)
                        act.activation(qT[:, j, :], ps[:, j, :], ACT.Copy, scale=DH ** -0.5).then_inc(evac, 1)

                    def tile_done(j):
                        act.wait_ge(att_weighted, a.at(i) + PERJ * (j + 1))
                        act.activation(yT[:, i * GROUP + j, :], ps[:, 6 + j % 2, :], ACT.Copy).then_inc(tile_out, 1)

                    att_act(act, a, i, lambda u: tile_done(u // PERJ - 1) if u >= PERJ and u % PERJ == 1 else None)
                    tile_done(GROUP - 1)

            @block.vector
            def _(dve):
                link = Chain(dve, sw_v)
                with dve.Fori(0, HALVES) as i:
                    link.loop(i, att_links(a) + 1)
                    dve.wait_ge(att_weighted, a.at(i))
                    dve.tensor_copy(sink[:, :], sinks[:, ds(i * HPT, HPT)])
                    link(dve.tensor_copy(bias[:, :, ::-1], swa_bias[:, ds(i * HPT, HPT), :]))
                    projected(dve, 3, i)
                    dve.tensor_copy(kT[:, :], ps[:, 3, :]).then_inc(evac, 1)
                    projected(dve, 4, i)
                    dve.tensor_copy(v[:, :, :].rearrange("p t n -> p (t n)"), ps[:, 4, :]).then_inc(evac, 1)
                    att_dve(dve, a, i, link, None)
                link.end(HALVES)
        end_ring(5, HALVES, [2, 2, 2, 1, 1])
        a.end(HALVES)
    memory_attention("ma1", 1, io["b_q"], Q_WIDTH)
    def heads_tiles(u, c0):
        w = io["b_out"]
        pieces = [(wslot[64 * kv:64 * kv + 64, u, GROUP * n:GROUP * n + GROUP, :],
                   w[n * QW + kv * GROUP * DH:n * QW + (kv + 1) * GROUP * DH, :].rearrange("(j d) n -> d j n", d=DH)[:, :, ds(c0, P)])
                  for n in range(HALVES) for kv in range(2)]
        return pieces + [(wslot[:, u, CT:, :], w[Q_WIDTH:, :].rearrange("(k p) n -> p k n", p=P)[:, :, ds(c0, P)])]

    residual_block("bo", KC, heads_tiles, 5, None)
    rms_block("f1", [(xT, T, [(hT, gain(vB, ROWS_B["norm_ffn"] + KC), None)])], [EPS2])
    feed_forward("ff1", 1)
    rms_block("fin", [(xT, T, [(hT, gain(vB, ROWS_B["final"]), None)])], [EPS2])

    with ExitStack() as local:
        rows = sb("out_rows", [P, TT, D], on=local)
        turned, rows_ready, stored = sem("out_turned"), sem("out_ready"), sem("out_stored")
        with nc.Block() as block:
            @block.tensor
            def _(pe):
                for t in range(TT):
                    for k in range(KC):
                        mm = pe.transpose(ps[:, 2 * t + k // 4, k % 4 * P:(k % 4 + 1) * P], hT[:, k, t * P:(t + 1) * P], ident[:, :])
                    mm.then_inc(turned, 1)

            @block.vector
            def _(dve):
                for t in range(TT):
                    dve.wait_ge(turned, t + 1)
                    dve.tensor_copy(rows[:, t, :], ps[:, 2 * t:2 * t + 2, :].rearrange("p b n -> p (b n)")).then_inc(rows_ready, 1)

            @block.sync
            def _(sp):
                for t in range(TT):
                    sp.wait_ge(rows_ready, t + 1)
                    sp.dma_start(out[t * P:(t + 1) * P, :], rows[:, t, :]).then_inc(stored, 16)
                sp.wait_ge(stored, 16 * TT)


def constants():
    c = {}
    c["ident"] = np.eye(P, dtype=np.float32)
    c["ones"] = np.ones((P, P), np.float32)
    dc, m = np.arange(NDC)[:, None], np.arange(P)[None, :]
    c["spread"] = (dc + m == GRID_W - 1 + NA_KW - 1).astype(np.float32)
    start = np.asarray(bucket_starts())
    dist = np.arange(3 * P)[None, :] - (P - 1)
    c["inbucket"] = ((dist >= start[:-1, None]) & (dist < start[1:, None])).astype(np.float32)
    c["farmask"] = np.where((dist >= 0) & (dist < MAXD), 0.0, -BIG).astype(np.float32) * np.ones((SWA_H, 1), np.float32)
    col, key = (np.arange(P) % GRID_W)[:, None], np.arange(GRID_W)[None, ::-1]
    first = np.clip(col - NA_KW // 2, 0, GRID_W - NA_KW)
    c["colmask"] = np.where((key >= first) & (key < first + NA_KW), 0.0, -BIG).astype(np.float32)
    s, t = np.arange(CH)[:, None], np.arange(CH)[None, :]
    pairs = np.zeros((P, 2, LEVELS + 1, CH), np.float32)
    for n in range(LEVELS):
        half = CH >> (n + 1)
        same = s // (2 * half) == t // (2 * half)
        pairs[:, 0, n] = same & (s // half % 2 == 0) & (t // half % 2 == 1)
        pairs[:, 1, n] = same & (s // half % 2 == 1) & (t // half % 2 == 0)
    pairs[:, :, LEVELS] = (s == t)[:, None, :]
    c["pairs"] = pairs.reshape(P, -1)
    go = np.ones((P, 2, T), np.float32)
    go[:, 0, 0::CH] = 0
    go[:, 1, CH - 1::CH] = 0
    c["go"] = go.reshape(P, -1)
    c["iota16"] = np.broadcast_to(np.arange(TOPK, dtype=np.float32), (P, TOPK)).copy()
    return c


def layout(inputs):
    a = {k: np.ascontiguousarray(np.asarray(v)) for k, v in inputs.items()}
    rows = lambda x: x.reshape(-1, P)
    out = {
        "x": a["x"].reshape(T, D), "ctx": a["ctx"].reshape(L, D), "mem": a["mem_2"].reshape(MEM, D),
        "c": rows(a["c"]), "c_ctx": rows(a["c_ctx"]), "b_mod": rows(a["b_mod"]), "norm1": rows(a["norm1"]),
        "norm2": rows(a["norm2"]), "norm_f": rows(a["norm_f"]), "hg_norm": rows(a["hg_norm"]), "hg_lb": rows(a["hg_lb"]),
        "norm_mix": rows(a["norm_mix_2"]), "norm_ffn": rows(a["norm_ffn_2"]), "kv_norm": rows(a["kv_norm_2"]),
        "mem_norm": rows(a["mem_norm_2"]), "final": rows(a["final_norm_2"]), "conv": rows(a["a_conv_w_2"]),
        "w_mod": a["w_mod"][0], "w_in": a["w_in"][0], "w_out": a["w_out"][0], "rpb": a["na_rpb"].reshape(NA_H * NDR, NDC),
        "wq": a["peer_wq"][0], "keys": a["peer_keys"][0].reshape(PE_H * 2 * NKEYS, DK), "u": a["peer_u"][0], "v": a["peer_v"][0],
        "a_in": a["a_w_in_2"][0], "a_out": a["a_w_out_2"][0], "w_kv": a["w_kv_2"], "b_q": a["b_w_q_2"][0],
        "sinks": a["b_sinks_2"].reshape(1, SWA_H), "b_out": a["b_w_out_2"][0], "rel_bias": a["rel_bias_2"],
        "mem_kv": a["w_mem_kv_2"].reshape(2 * D, -1), "gate": a["w_gate_2"].reshape(2 * D, D_FF),
        "up": a["w_up_2"].reshape(2 * D, D_FF), "down": a["w_down_2"].reshape(2 * D_FF, D),
    }
    out.update({"const_" + k: v for k, v in constants().items()})
    return out


def kernel(**inputs):
    import concourse.bacc as bacc
    from concourse.bass_utils import run_bass_kernel_spmd

    nc = bacc.Bacc("TRN2", target_bir_lowering=False, num_devices=1)
    arrays, io = {}, {}
    for name, a in layout(inputs).items():
        arrays[f"in_{name}"] = a
        io[name] = nc.dram_tensor(f"in_{name}", a.shape, mybir.dt.from_np(a.dtype), kind="ExternalInput").ap()
    out = nc.dram_tensor("out", (T, D), F32, kind="ExternalOutput").ap()
    program(nc, io, out)
    r = run_bass_kernel_spmd(nc, [arrays], core_ids=[0])
    return r.results[0]["out"].reshape(1, T, D)
```

```python
from contextlib import ExitStack

import numpy as np
import concourse.bass as bass
from concourse import mybir
from concourse.alu_op_type import AluOpType as ALU

ACT = mybir.ActivationFunctionType
AX = mybir.AxisListType
F32 = mybir.dt.float32
F32R = mybir.dt.float32r
U32 = mybir.dt.uint32
ds = bass.ds

P = 128
D, T, L, MEM = 1024, 512, 256, 256
KC = D // P
TT, LT = T // P, L // P
GRID_W = 64
NA_H, DH = 8, 64
NA_KH, NA_KW = 8, 16
NDR, NDC = 2 * NA_KH - 1, 2 * NA_KW - 1
HG_H, DK = 4, 128
CH = 128
NCH = T // CH
LEVELS = 7
PE_H, NKEYS, TOPK = 8, 128, 16
KV_H, GROUP, SWA_H = 4, 3, 12
BUCKETS, MAXD = 32, 128
D_FF = 2816
FT = D_FF // P
CONV = 768
Q_WIDTH = SWA_H * DH
EPS1, EPS2 = 1e-6, 1e-5
BIG = 1e30

ROWS_A = dict(c=0, c_ctx=8, b_mod=16, norm1=64, norm2=72, norm_f=80, hg_norm=88, hg_lb=92)
ROWS_B = dict(norm_mix=0, norm_ffn=16, kv_norm=32, mem_norm=40, final=48, conv=56)
NA_ROWS, NB_ROWS = 108, 74


def bucket_starts():
    half = BUCKETS // 2
    dist = np.arange(MAXD)
    near = np.maximum(dist, 1).astype(np.float32)
    far = half + (np.log(near / np.float32(half)) / np.float32(np.log(MAXD / half)) * np.float32(BUCKETS - half)).astype(np.int32)
    bucket = np.where(dist < half, dist, np.minimum(far, BUCKETS - 1))
    return [int(np.argmax(bucket >= b)) if (bucket >= b).any() else MAXD for b in range(BUCKETS)] + [MAXD]


class Chain:

    def __init__(self, engine, sem):
        self.engine, self.sem, self.done, self.turn = engine, sem, 0, 0

    def __call__(self, ins):
        self.done = self.done + 1
        ins.then_inc(self.sem, 1)
        self.engine.wait_ge(self.sem, self.turn + self.done)

    def loop(self, i, per):
        self.before, self.per, self.turn, self.done = self.done, per, i * per + self.done, 0

    def end(self, turns):
        assert self.done == self.per, (self.done, self.per)
        self.done, self.turn = self.before + turns * self.per, 0


def program(nc, io, out):
    whole = ExitStack()

    def sb(name, shape, dt=F32, on=whole):
        return on.enter_context(nc.sbuf_tensor(name, shape, dt))

    def sem(name):
        return whole.enter_context(nc.semaphore(name))

    ps = whole.enter_context(nc.psum_tensor("ps", [P, 8, 512], F32))

    ident = sb("ident", [P, P])
    ones = sb("ones", [P, P])
    xT = sb("xT", [P, KC, T])
    hT = sb("hT", [P, KC, T])
    yT = sb("yT", [P, KC, T])
    rstd = sb("rstd", [P, T])
    memT = sb("memT", [P, KC, MEM])
    mem_kv = memT[:, :, :].rearrange("p (b two) n -> p b (two n)", two=2)
    vA = sb("vA", [P, NA_ROWS])
    vB = sb("vB", [P, NB_ROWS])
    mod = sb("mod", [P, 6 * KC, 2])
    gain1 = sb("gain1", [P, KC, 2])
    gain2 = sb("gain2", [P, KC])
    wring = sb("wring", [P, 6 * KC * P])
    wslot = wring[:, :].rearrange("p (s k n) -> p s k n", s=6, k=KC)

    SLOTS = 6
    w_landed = [sem(f"w_landed{u}") for u in range(SLOTS)]
    mm_done = [sem(f"mm_done{u}") for u in range(SLOTS)]
    evacuated = [sem(f"evacuated{u}") for u in range(SLOTS)]
    landed, turns, left = [0] * SLOTS, [1] * SLOTS, [1] * SLOTS

    def load_weights(sp, u, it, *pieces):
        sp.wait_ge(mm_done[u], turns[u] + it)
        sp.nop(nofuse=True)
        for dst, src in pieces:
            sp.dma_start(dst, src).then_inc(w_landed[u], 16)

    def weights_in(pe, u, it, pieces=1):
        pe.wait_ge(w_landed[u], 16 * (landed[u] + pieces * (it + 1)))

    def projected(eng, u, it):
        eng.wait_ge(mm_done[u], turns[u] + it + 1)

    def end_ring(slots, times, pieces=1, evacuations=False):
        for u in range(slots):
            landed[u] += times * (pieces if isinstance(pieces, int) else pieces[u])
            turns[u] += times
            left[u] += times if evacuations else 0

    SPLIT = 4
    hi_ready = [sem(f"hi_ready{u}") for u in range(SPLIT)]
    split_done = [sem(f"split_done{u}") for u in range(SPLIT)]
    rhs_hi_ready, rhs_ready = sem("rhs_hi_ready"), sem("rhs_ready")
    his, splits = [0] * SPLIT, [1] * SPLIT
    rhs_chunks = [0]

    def split_buffers(on, name):
        return [sb(f"{name}_{x}", shape, F32R, on=on) for x, shape in
                (("w_hi", [P, SPLIT, KC, P]), ("w_lo", [P, SPLIT, KC, P]), ("r_hi", [P, KC, T]), ("r_lo", [P, KC, T]))]

    def load_split(sp, u, t, *pieces):
        sp.wait_ge(split_done[u], splits[u] + t)
        sp.nop(nofuse=True)
        for dst, src in pieces:
            sp.dma_start(dst, src).then_inc(w_landed[u], 16)

    def split_hi(act, parts, u, t, pieces=1):
        weights_in(act, u, t, pieces)
        act.wait_ge(mm_done[u], turns[u] + t)
        act.activation(parts[0][:, u, :, :], wslot[:, u, :, :], ACT.Copy).then_inc(hi_ready[u], 1)

    def split_lo(dve, parts, u, t):
        dve.wait_ge(hi_ready[u], his[u] + t + 1)
        dve.tensor_tensor(parts[1][:, u, :, :], wslot[:, u, :, :], parts[0][:, u, :, :].bitcast(F32), ALU.subtract).then_inc(split_done[u], 1)

    def first_hi(act, parts, src, slots, pieces=1):
        for k in range(KC):
            act.activation(parts[2][:, k, :], src[:, k, :], ACT.Copy).then_inc(rhs_hi_ready, 1)
            if k == KC // 2 - 1:
                split_hi(act, parts, 0, 0, pieces)
        for u in range(1, slots):
            split_hi(act, parts, u, 0, pieces)

    def first_lo(dve, parts, src, slots):
        for k in range(KC):
            dve.wait_ge(rhs_hi_ready, rhs_chunks[0] + k + 1)
            dve.tensor_tensor(parts[3][:, k, :], src[:, k, :], parts[2][:, k, :].bitcast(F32), ALU.subtract).then_inc(rhs_ready, 1)
            if k == KC // 2 - 1:
                split_lo(dve, parts, 0, 0)
        for u in range(1, slots):
            split_lo(dve, parts, u, 0)

    def product(pe, parts, u, t, bank, hi, lo, n=KC, chunk_in=None):
        pe.wait_ge(split_done[u], splits[u] + t + 1)
        pe.wait_ge(evacuated[u], left[u] + t)
        for k in range(n):
            if chunk_in is not None:
                chunk_in(k)
            pe.matmul(bank, parts[0][:, u, k, :], hi[:, k, :], start=k == 0, stop=False)
            pe.matmul(bank, parts[0][:, u, k, :], lo[:, k, :], start=False, stop=False)
            mm = pe.matmul(bank, parts[1][:, u, k, :], hi[:, k, :], start=False, stop=k == n - 1)
        mm.then_inc(mm_done[u], 1)

    def rhs_in(pe):
        return lambda k: pe.wait_ge(rhs_ready, rhs_chunks[0] + k + 1)

    def end_split(slots, times, pieces=1):
        end_ring(slots, times, pieces, True)
        rhs_chunks[0] += KC
        for u in range(slots):
            his[u] += times
            splits[u] += times

    norm_meaned, norm_rooted, norm_scaled, norm_chain = [sem(f"norm_{s}") for s in ("meaned", "rooted", "scaled", "chain")]
    norms = dict(parts=0, scaled=0)

    chunk_squared, chunk_added = sem("chunk_squared"), sem("chunk_added")
    chunks = [0]

    def square_chunk(act, sqr, j):
        if j >= 2:
            act.wait_ge(chunk_added, chunks[0] + j - 1)
        act.activation(sqr[:, j % 2, :], xT[:, j, :], ACT.Square).then_inc(chunk_squared, 1)

    def add_chunk(pe, sqr, j):
        pe.wait_ge(chunk_squared, chunks[0] + j + 1)
        pe.matmul(ps[:, 7, :], ones[:, :], sqr[:, j % 2, :], start=j == 0, stop=j == KC - 1).then_inc(chunk_added, 1)

    def rms_block(name, eps, outs, sum_again=False, prefetch=None):
        n, scaled_before = norms["parts"], norms["scaled"]
        with ExitStack() as local:
            sqr = sb(f"{name}_sqr", [P, 2, T], on=local)
            with nc.Block() as block:
                @block.sync
                def _(sp):
                    if prefetch is not None:
                        prefetch(sp)

                @block.scalar
                def _(act):
                    done = scaled_before
                    act.wait_ge(norm_meaned, n + 1)
                    act.activation(rstd[:, :], rstd[:, :], ACT.Sqrt).then_inc(norm_rooted, 1)
                    for dst, gain, shift in outs:
                        for k in range(KC):
                            done += 1
                            if shift is not None or sum_again:
                                act.wait_ge(norm_scaled, done)
                            if shift is not None:
                                act.activation(dst[:, k, :], dst[:, k, :], ACT.Identity, bias=shift(k))
                            if sum_again:
                                square_chunk(act, sqr, k)

                @block.tensor
                def _(pe):
                    for k in range(KC if sum_again else 0):
                        add_chunk(pe, sqr, k)

                @block.vector
                def _(dve):
                    link = Chain(dve, norm_chain)
                    link.done = n
                    dve.tensor_scalar(rstd[:, :], ps[:, 7, :], 1.0 / D, eps, ALU.mult, ALU.add).then_inc(norm_meaned, 1)
                    dve.wait_ge(norm_rooted, n + 1)
                    link(dve.reciprocal(rstd[:, :], rstd[:, :]))
                    for dst, gain, shift in outs:
                        for k in range(KC):
                            dve.scalar_tensor_tensor(dst[:, k, :], xT[:, k, :], gain(k), rstd[:, :], ALU.mult, ALU.mult).then_inc(norm_scaled, 1)
        norms["parts"] += 1
        norms["scaled"] += KC * len(outs)
        chunks[0] += KC if sum_again else 0

    att_scored, att_logit_ready, att_exp_ready, att_prob_ready, att_turned, att_pT_ready, att_weighted = [
        sem(f"att_{x}") for x in ("scored", "logit_ready", "exp_ready", "prob_ready", "turned", "pT_ready", "weighted")]
    att_units = [1]

    class Attention:

        def __init__(self, name, local, units, depth):
            self.units, self.n, self.depth, self.lag = units, len(units), depth, depth - 1
            width = max(keys_of(u) for u in units)
            self.s = sb(f"{name}_s", [P, depth, width], on=local)
            self.pT = sb(f"{name}_pT", [P, 2, width], on=local)
            self.small = sb(f"{name}_small", [P, depth, 8], on=local)
            self.before = att_units[0]

        def at(self, i):
            return self.before + self.n * i

        def end(self, turns):
            att_units[0] += self.n * turns

    def col(a, u, j):
        return a.small[:, u % a.depth, j:j + 1]

    def score_bank(a, u):
        b, per = 4 // a.depth * (u % a.depth), 4 // a.depth
        return ps[:, b:b + per, :].rearrange("p b n -> p (b n)")

    def turn_bank(a, u):
        banks = ps[:, 4:6, :] if a.depth == 2 else ps[:, 4 + u % 2:5 + u % 2, :]
        return banks.rearrange("p b n -> p (b n)")

    def keys_of(unit):
        return sum(w for _, w in unit["k"])

    def att_score(pe, a, i, u):
        pe.wait_ge(att_logit_ready, a.at(i) + max(u - a.lag, 0))
        at = 0
        for seg, w in a.units[u]["k"]:
            mm = pe.matmul(score_bank(a, u)[:, at:at + w], a.units[u]["q"], seg, start=True, stop=True)
            at += w
        mm.then_inc(att_scored, 1)

    def att_turn(pe, a, i, u):
        pe.wait_ge(att_prob_ready, a.at(i) + u + 1)
        pe.wait_ge(att_pT_ready, a.at(i) + (u if a.depth == 2 else max(u - 1, 0)))
        for b in range(keys_of(a.units[u]) // P):
            mm = pe.transpose(turn_bank(a, u)[:, b * P:(b + 1) * P], a.s[:, u % a.depth, b * P:(b + 1) * P], ident[:, :])
        mm.then_inc(att_turned, 1)

    def att_weigh(pe, a, i, u, before):
        unit = a.units[u]
        pe.wait_ge(att_pT_ready, a.at(i) + u + 1)
        before(u)
        for b, v in enumerate(unit["v"]):
            mm = pe.matmul(unit["out"], v, a.pT[:, u % 2, b * P:(b + 1) * P], start=b == 0, stop=b == len(unit["v"]) - 1)
        mm.then_inc(att_weighted, 1)

    def att_pe(pe, a, i, before, fresh=lambda u: None, between=lambda u: None):
        for u in range(a.n + a.lag + 1):
            if u < a.n:
                fresh(u)
                att_score(pe, a, i, u)
            if a.depth > 2 and a.lag <= u < a.n + a.lag:
                att_turn(pe, a, i, u - a.lag)
            if u > a.lag:
                att_weigh(pe, a, i, u - a.lag - 1, before)
            between(u)
            if a.depth == 2 and a.lag <= u < a.n + a.lag:
                att_turn(pe, a, i, u - a.lag)

    def att_links(a):
        return sum(2 + (x["sink"] is not None) for x in a.units)

    def att_logits(dve, a, i, u, link, zeros):
        unit = a.units[u]
        dve.wait_ge(att_scored, a.at(i) + u + 1)
        dve.wait_ge(att_turned, a.at(i) + max(u - a.lag, 0))
        dve.nop(nofuse=True)
        at, start = 0, -BIG if unit["sink"] is None else unit["sink"]
        for j, (seg, w) in enumerate(unit["k"]):
            bias = zeros[:, 0:w] if unit["bias"][j] is None else unit["bias"][j]
            last = dve.tensor_tensor_reduce(a.s[:, u % a.depth, at:at + w], score_bank(a, u)[:, at:at + w], bias,
                                            1.0, start, ALU.add, ALU.max, col(a, u, 4 + j))
            at += w
        link(last)
        dve.tensor_scalar(col(a, u, 0), col(a, u, 4), col(a, u, 3 + len(unit["k"])), -1.0, ALU.max, ALU.mult).then_inc(att_logit_ready, 1)

    def att_probs(dve, a, i, u, link):
        n = keys_of(a.units[u])
        dve.wait_ge(att_exp_ready, a.at(i) + u + 1)
        if a.units[u]["sink"] is not None:
            link(dve.tensor_tensor(col(a, u, 1), col(a, u, 1), col(a, u, 2), ALU.add))
        link(dve.reciprocal(col(a, u, 3), col(a, u, 1)))
        dve.tensor_scalar(a.s[:, u % a.depth, 0:n], a.s[:, u % a.depth, 0:n], col(a, u, 3), None, ALU.mult).then_inc(att_prob_ready, 1)

    def att_dve(dve, a, i, link, zeros, between=lambda u: None):
        for u in range(a.n + 1):
            if a.depth == 2 and u >= 1:
                att_probs(dve, a, i, u - 1, link)
            if u < a.n:
                att_logits(dve, a, i, u, link, zeros)
            if a.depth > 2 and u >= 1:
                att_probs(dve, a, i, u - 1, link)
            between(u)

    def att_act(act, a, i, after=lambda v: None):
        def exps(u):
            n = keys_of(a.units[u])
            act.wait_ge(att_logit_ready, a.at(i) + u + 1)
            if a.units[u]["sink"] is not None:
                act.activation(col(a, u, 2), a.units[u]["sink"], ACT.Exp, bias=col(a, u, 0))
            act.activation(a.s[:, u % a.depth, 0:n], a.s[:, u % a.depth, 0:n], ACT.Exp, bias=col(a, u, 0),
                           accum_out=col(a, u, 1)).then_inc(att_exp_ready, 1)

        def turned_probs(u):
            n = keys_of(a.units[u])
            act.wait_ge(att_turned, a.at(i) + u + 1)
            act.wait_ge(att_weighted, a.at(i) + max(u - 1, 0))
            act.activation(a.pT[:, u % 2, 0:n], turn_bank(a, u)[:, 0:n], ACT.Copy).then_inc(att_pT_ready, 1)
            after(u)

        for u in range(a.n + a.lag):
            if a.depth == 2 and u < a.n:
                exps(u)
            if u >= a.lag:
                turned_probs(u - a.lag)
            if a.depth > 2 and u < a.n:
                exps(u)

    def gain(v, at):
        return lambda k: v[:, at + k:at + k + 1]

    def weights(w, c0, n=P):
        return w.rearrange("(k p) n -> p k n", p=P)[:, :, ds(c0, n)]

    rpb_scr = nc.dram_tensor("rpb_scr", [NA_H * NDR, P], F32, kind="Internal")
    rel_scr = nc.dram_tensor("rel_scr", [SWA_H, 3 * P], F32, kind="Internal")
    swa_bias = sb("swa_bias", [P, SWA_H, 2 * P])
    sinks = sb("sinks", [P, SWA_H])
    lb = sb("lb", [P, 2, 2, HG_H])
    ctx_mem = ExitStack()
    with ctx_mem:
        ctxT = sb("ctxT", [P, KC, L], on=ctx_mem)
        rstds = sb("rstds", [P, T + L + MEM], on=ctx_mem)
        na_stack = ctx_mem.enter_context(ExitStack())
        na_bias = sb("na_bias", [P, NA_H, 16, GRID_W], on=na_stack)
        with ExitStack() as local:
            tok = [half.rearrange("p (t k) n -> p t (k n)", t=TT)[:, t, :] for half in (hT[:, :, :], yT[:, :, :]) for t in range(TT)]
            rows = sb("rows", [P, 2, P], on=local)
            cT = sb("cT", [P, KC, 2], on=local)
            mod_rows = sb("mod_rows", [2, 6 * D], on=local)
            SQ = 4
            sq = sb("setup_sq", [P, SQ, T], on=local)
            rpb = sb("rpb", [NA_H * NDR, NDC], on=local)
            rpbT = sb("rpbT", [NDC, NA_H * NDR], on=local)
            spread = sb("spread", [NDC, P], on=local)
            inbucket = sb("inbucket", [BUCKETS, 3 * P], on=local)
            relb = sb("relb", [BUCKETS, SWA_H], on=local)
            wide = sb("wide", [NA_H * NDR, P], on=local)
            far = sb("far", [SWA_H, 3 * P], on=local)
            farmask = sb("farmask", [SWA_H, 3 * P], on=local)
            sink1 = sb("sink1", [1, SWA_H], on=local)
            consts_in, rows_in, rpb_in = sem("consts_in"), sem("rows_in"), sem("rpb_in")
            tok_in = [sem(f"tok_in{n}") for n in range(TT + 2 * LT)]
            rows_turned, silu_ready = sem("rows_turned"), sem("silu_ready")
            x_turned, x_ready, x_squared, x_added = sem("x_turned"), sem("x_ready"), sem("x_squared"), sem("x_added")
            x_meaned, x_rooted, mod_turned = sem("x_meaned"), sem("x_rooted"), sem("mod_turned")
            rpb_turned, rpb_ready, rpb_spread, bias_ready = sem("rpb_turned"), sem("rpb_ready"), sem("rpb_spread"), sem("bias_ready")
            scr_written, bias_in = sem("scr_written"), sem("bias_in")
            na_zero, setup_v, cT_ready = sem("na_zero"), sem("setup_v"), sem("cT_ready")
            MS = 3
            modw = wring[:, :].rearrange("p (s k n) -> p s k n", s=MS, k=KC)
            sum_bank = [ps[:, 4, :], ps[:, 5, 0:L], ps[:, 6, 0:MEM]]
            mod_bank = [ps[0:2, u, 0:2 * P] for u in range(MS)]
            ends = [KC, KC + KC // 2, 2 * KC]
            rstd_of = [rstds[:, 0:T], rstds[:, T:T + L], rstds[:, T + L:]]
            groups = [(0, k) for k in range(KC)] + [(TT, k) for k in range(0, KC, 2)] + [(TT + LT, k) for k in range(0, KC, 2)]

            def in_group(t0, k):
                return xT[:, k, :] if t0 == 0 else (ctxT if t0 == TT else memT)[:, k:k + 2, :].rearrange("p k n -> p (k n)")

            with nc.Block() as block:
                @block.sync
                def _(sp):
                    for dst, name in ((ident, "ident"), (spread, "spread"), (inbucket, "inbucket"), (farmask, "farmask"), (ones, "ones")):
                        sp.dma_start(dst[:, :], io["const_" + name]).then_inc(consts_in, 16)
                    for at, names, where in ((0, ("c", "c_ctx", "b_mod", "norm1", "norm2", "norm_f", "hg_norm", "hg_lb"), ROWS_A),
                                             (1, ("norm_mix", "norm_ffn", "kv_norm", "mem_norm", "final", "conv"), ROWS_B)):
                        for name in names:
                            n = io[name].shape[0]
                            sp.dma_start(rows[where[name]:where[name] + n, at, :], io[name]).then_inc(rows_in, 16)
                    for n in range(TT + 2 * LT):
                        src, r = ((io["x"], n) if n < TT else (io["ctx"], n - TT) if n < TT + LT else (io["mem"], n - TT - LT))
                        sp.dma_start(tok[n], src[r * P:(r + 1) * P, :]).then_inc(tok_in[n], 16)
                    with sp.Fori(0, 6 * KC // 2 // MS) as i:
                        for u in range(MS):
                            load_weights(sp, u, i, (modw[:, u, :, :], weights(io["w_mod"], i * (MS * 2 * P) + u * 2 * P, 2 * P)))

                @block.gpsimd
                def _(pool):
                    pool.memset(na_bias[:, :, :, :], 0.0).then_inc(na_zero, 1)
                    pool.dma_start(rpb[:, :], io["rpb"]).then_inc(rpb_in, 16)
                    pool.dma_start(relb[:, :], io["rel_bias"]).then_inc(rpb_in, 16)
                    pool.dma_start(sink1[:, :], io["sinks"]).then_inc(rpb_in, 16)
                    pool.wait_ge(bias_ready, 2)
                    pool.dma_start(rpb_scr[:, :], wide[:, :]).then_inc(scr_written, 16)
                    pool.dma_start(rel_scr[:, :], far[:, :]).then_inc(scr_written, 16)
                    pool.wait_ge(scr_written, 32)
                    pool.wait_ge(na_zero, 1)
                    for half in range(2):
                        for h in range(NA_H):
                            pool.dma_start(na_bias[half * 64:half * 64 + 64, h, half:half + NDR, :],
                                           bass.AP(rpb_scr, h * NDR * P, [[1, GRID_W], [P, NDR], [1, GRID_W]])).then_inc(bias_in, 16)
                    pool.dma_start(swa_bias[:, :, :], bass.AP(rel_scr, 0, [[1, P], [3 * P, SWA_H], [1, 2 * P]])).then_inc(bias_in, 16)
                    pool.wait_ge(bias_in, 16 * (2 * NA_H + 1))

                @block.tensor
                def _(pe):
                    for u in range(SLOTS):
                        pe.sem_inc(mm_done[u], 1)
                        pe.sem_inc(evacuated[u], 1)
                    for u in range(SPLIT):
                        pe.sem_inc(split_done[u], 1)
                    for credit in (att_scored, att_logit_ready, att_exp_ready, att_prob_ready, att_turned, att_pT_ready, att_weighted):
                        pe.sem_inc(credit, 1)
                    pe.wait_ge(consts_in, 16 * 5)
                    pe.wait_ge(rows_in, 16 * 14)
                    pe.transpose(ps[:, 7, 0:NA_ROWS], rows[0:NA_ROWS, 0, :], ident[0:NA_ROWS, 0:NA_ROWS])
                    pe.transpose(ps[:, 7, P:P + NB_ROWS], rows[0:NB_ROWS, 1, :], ident[0:NB_ROWS, 0:NB_ROWS]).then_inc(rows_turned, 1)
                    pe.wait_ge(rpb_in, 48)
                    pe.transpose(ps[0:NDC, 5, 0:NA_H * NDR], rpb[:, :], ident[0:NA_H * NDR, 0:NA_H * NDR])
                    pe.matmul(ps[0:SWA_H, 5, P:P + 3 * P], relb[:, :], inbucket[:, :], start=True, stop=True).then_inc(rpb_turned, 1)
                    pe.matmul(ps[:, 4, P:P + SWA_H], ones[0:1, :], sink1[:, :], start=True, stop=True)
                    pe.wait_ge(rpb_ready, 1)
                    pe.matmul(ps[0:NA_H * NDR, 4, 0:P], rpbT[:, :], spread[:, :], start=True, stop=True).then_inc(rpb_spread, 1)
                    for g, (t0, k) in enumerate(groups):
                        if g >= 4:
                            pe.wait_ge(x_ready, g - 3)
                        for b in range(4):
                            t, kk = (t0 + b, k) if t0 == 0 else (t0 + b % 2, k + b // 2)
                            if k == 0 and b < (4 if t0 == 0 else 2):
                                pe.wait_ge(tok_in[t], 16)
                            mm = pe.transpose(ps[:, g % 4, b * P:(b + 1) * P], tok[t][:, kk * P:(kk + 1) * P], ident[:, :])
                        mm.then_inc(x_turned, 1)
                    pe.wait_ge(silu_ready, 1)
                    for g, (t0, k) in enumerate(groups):
                        pe.wait_ge(x_squared, g + 1)
                        if t0 == 0:
                            mm = pe.matmul(sum_bank[0], ones[:, :], sq[:, g % SQ, :], start=k == 0, stop=k == KC - 1)
                        else:
                            for b in range(2):
                                mm = pe.matmul(sum_bank[1 if t0 == TT else 2], ones[:, :], sq[:, g % SQ, b * L:(b + 1) * L],
                                               start=k + b == 0, stop=k + b == KC - 1)
                        mm.then_inc(x_added, 1)
                    with pe.Fori(0, 6 * KC // 2 // MS) as i:
                        for u in range(MS):
                            weights_in(pe, u, i)
                            pe.wait_ge(evacuated[u], left[u] + i)
                            for k in range(KC):
                                mm = pe.matmul(mod_bank[u], cT[:, k, :], modw[:, u, k, :], start=k == 0, stop=k == KC - 1)
                            mm.then_inc(mm_done[u], 1)
                    for u in range(MS):
                        pe.wait_ge(evacuated[u], left[u] + 6 * KC // 2 // MS)
                    for m in range(6 * KC):
                        mm = pe.transpose(ps[:, 7, 2 * m:2 * m + 2], mod_rows[:, m * P:(m + 1) * P], ident[0:2, 0:2])
                    mm.then_inc(mod_turned, 1)

                @block.scalar
                def _(act):
                    act.wait_ge(cT_ready, 1)
                    act.activation(cT[:, :, :], cT[:, :, :], ACT.Silu).then_inc(silu_ready, 1)
                    for g, (t0, k) in enumerate(groups):
                        act.wait_ge(x_ready, g + 1)
                        if g >= SQ:
                            act.wait_ge(x_added, g - SQ + 1)
                        act.activation(sq[:, g % SQ, :], in_group(t0, k), ACT.Square).then_inc(x_squared, 1)
                    for n in range(3):
                        act.wait_ge(x_meaned, n + 1)
                        act.activation(rstd_of[n], rstd_of[n], ACT.Sqrt).then_inc(x_rooted, 1)
                    with act.Fori(0, 6 * KC // 2 // MS) as i:
                        for u in range(MS):
                            projected(act, u, i)
                            act.activation(mod_rows[:, ds(i * (MS * 2 * P) + u * 2 * P, 2 * P)], mod_bank[u], ACT.Copy).then_inc(evacuated[u], 1)

                @block.vector
                def _(dve):
                    link = Chain(dve, setup_v)
                    dve.wait_ge(rows_turned, 1)
                    dve.tensor_copy(vA[:, :], ps[:, 7, 0:NA_ROWS])
                    link(dve.tensor_copy(vB[:, :], ps[:, 7, P:P + NB_ROWS]))
                    dve.tensor_copy(cT[:, :, :], vA[:, 0:2 * KC].rearrange("p (a k) -> p k a", a=2)).then_inc(cT_ready, 1)
                    dve.wait_ge(rpb_turned, 1)
                    dve.tensor_tensor(far[:, :], ps[0:SWA_H, 5, P:P + 3 * P], farmask[:, :], ALU.add).then_inc(bias_ready, 1)
                    dve.tensor_copy(rpbT[:, :], ps[0:NDC, 5, 0:NA_H * NDR]).then_inc(rpb_ready, 1)
                    dve.wait_ge(rpb_spread, 1)
                    dve.tensor_copy(sinks[:, :], ps[:, 4, P:P + SWA_H])
                    dve.tensor_copy(wide[:, :], ps[0:NA_H * NDR, 4, 0:P]).then_inc(bias_ready, 1)
                    for g, (t0, k) in enumerate(groups):
                        dve.wait_ge(x_turned, g + 1)
                        dve.tensor_copy(in_group(t0, k), ps[:, g % 4, :]).then_inc(x_ready, 1)
                    for n in range(3):
                        dve.wait_ge(x_added, ends[n])
                        dve.tensor_scalar(rstd_of[n], sum_bank[n], 1.0 / D, [EPS1, EPS1, EPS2][n], ALU.mult, ALU.add).then_inc(x_meaned, 1)
                    for n in range(3):
                        dve.wait_ge(x_rooted, n + 1)
                        link(dve.reciprocal(rstd_of[n], rstd_of[n]))
                    for k in range(KC):
                        dve.scalar_tensor_tensor(memT[:, k, :], memT[:, k, :], vB[:, ROWS_B["mem_norm"] + k:ROWS_B["mem_norm"] + k + 1], rstd_of[2], ALU.mult, ALU.mult)
                    dve.wait_ge(mod_turned, 1)
                    bm = vA[:, ROWS_A["b_mod"]:ROWS_A["b_mod"] + 6 * KC]
                    for a in range(2):
                        last = dve.tensor_tensor(mod[:, :, a], ps[:, 7, 0:12 * KC].rearrange("p (m a) -> p m a", a=2)[:, :, a], bm, ALU.add)
                    link(last)
                    for a in range(2):
                        n1 = vA[:, ROWS_A["norm1"]:ROWS_A["norm1"] + KC]
                        dve.scalar_tensor_tensor(gain1[:, :, a], mod[:, KC:2 * KC, a], 1.0, n1, ALU.add, ALU.mult)
                    n2 = vA[:, ROWS_A["norm2"]:ROWS_A["norm2"] + KC]
                    dve.scalar_tensor_tensor(gain2[:, :], mod[:, 4 * KC:5 * KC, 0], 1.0, n2, ALU.add, ALU.mult)
                    lo = vA[:, ROWS_A["hg_lb"]:ROWS_A["hg_lb"] + 16].rearrange("p (e d h) -> p e d h", e=2, d=2)
                    link(dve.tensor_tensor(lb[:, 0, :, :], lo[:, 0, :, :], lo[:, 1, :, :], ALU.subtract))
            end_ring(MS, 6 * KC // 2 // MS, 1, True)

        def load_qkv(sp, i):
            for u in range(3):
                load_weights(sp, u, i, (wslot[:, u, :, :], weights(io["w_in"], i * P + u * NA_H * DH)))

        with nc.Block() as block:
            @block.sync
            def _(sp):
                load_qkv(sp, 0)

            @block.vector
            def _(dve):
                for dst, src, N, a, r in ((hT, xT, T, 0, rstds[:, 0:T]), (ctxT, ctxT, L, 1, rstds[:, T:T + L])):
                    for k in range(KC):
                        dve.scalar_tensor_tensor(dst[:, k, :], src[:, k, :], gain1[:, k, a:a + 1], r, ALU.mult, ALU.mult).then_inc(norm_scaled, 1)

            @block.scalar
            def _(act):
                for n, (dst, a) in enumerate(((hT, 0), (ctxT, 1))):
                    for k in range(KC):
                        act.wait_ge(norm_scaled, n * KC + k + 1)
                        act.activation(dst[:, k, :], dst[:, k, :], ACT.Identity, bias=mod[:, k, a:a + 1])
        norms["scaled"] = 2 * KC

        with ExitStack() as local:
            qT = sb("na_q", [P, 2, T], on=local)
            kT = sb("na_k", [P, 2, T + L], on=local)
            v = sb("na_v", [P, 2, TT + LT, P], on=local)
            bias = sb("na_bias_now", [P, 2, 2, 16 * GRID_W], on=local)
            zeros = sb("na_zeros", [P, L], on=local)
            colmask = sb("na_colmask", [P, GRID_W], on=local)
            staged, k_done, pair_out, mask_in, na_v = sem("na_staged"), sem("na_k_done"), sem("na_pair_out"), sem("na_mask_in"), sem("na_chain")
            units = []
            for par in range(2):
                for h in range(2):
                    for t in range(TT):
                        off = (NA_KH - 1 - 2 * t) * GRID_W
                        hp = slice(64 * h, 64 * h + 64)
                        units.append(dict(q=qT[hp, par, t * P:(t + 1) * P], k=[(kT[hp, par, 0:T], T), (kT[hp, par, T:T + L], L)], sink=None,
                                          bias=[bias[:, par, h, off:off + T], None], v=[v[:, par, b, hp] for b in range(TT + LT)],
                                          out=ps[hp, 6, t * P:(t + 1) * P]))
            a = Attention("na", local, units, 2)
            PAIRS = NA_H // 2
            TURNS = PAIRS // 2
            U = a.n // 2
            STAGED = 5
            with nc.Block() as block:
                @block.sync
                def _(sp):
                    sp.dma_start(colmask[:, :], io["const_colmask"]).then_inc(mask_in, 16)
                    with sp.Fori(1, PAIRS) as i:
                        load_qkv(sp, i)

                @block.tensor
                def _(pe):
                    def project_rows(r, u):
                        pe.wait_ge(staged, STAGED * r + (u + STAGED))
                        weights_in(pe, u, r)
                        for k in range(KC):
                            mm = pe.matmul(ps[:, 7, :], wslot[:, u, k, :], hT[:, k, :], start=k == 0, stop=k == KC - 1)
                        mm.then_inc(mm_done[0] if u == 0 else k_done, 1)

                    def project_ctx(r):
                        pe.wait_ge(staged, STAGED * r + (2 + STAGED))
                        weights_in(pe, 2, r)
                        for c in range(LT):
                            for k in range(KC):
                                pe.matmul(ps[:, 7, L + c * P:L + (c + 1) * P], ctxT[:, k, c * P:(c + 1) * P], wslot[:, 2, k, :], start=k == 0, stop=k == KC - 1)
                        for k in range(KC):
                            mm = pe.matmul(ps[:, 7, 0:L], wslot[:, 1, k, :], ctxT[:, k, :], start=k == 0, stop=k == KC - 1)
                        mm.then_inc(mm_done[1], 1)

                    def project_v(r):
                        pe.wait_ge(staged, STAGED * r + (4 + STAGED))
                        for t in range(TT):
                            for k in range(KC):
                                mm = pe.matmul(ps[:, 7, t * P:(t + 1) * P], hT[:, k, t * P:(t + 1) * P], wslot[:, 2, k, :], start=k == 0, stop=k == KC - 1)
                        mm.then_inc(mm_done[2], 1)

                    def turn(i, more):
                        def accumulator_free(u):
                            if u % U == 0:
                                pe.wait_ge(pair_out, 2 * i + (u // U + 1))

                        def fresh(u):
                            if u % U == 0:
                                pe.wait_ge(staged, STAGED * 2 * i + STAGED * (u // U + 2))

                        def between(u):
                            r, step = 2 * i + (u // U + 1), u % U
                            if u < U or (more and u < 2 * U):
                                if step == 1:
                                    project_rows(r, 0)
                                elif step == 2:
                                    project_rows(r, 1)
                                elif step == 4:
                                    project_ctx(r)
                                elif step == 6:
                                    project_v(r)

                        att_pe(pe, a, i, accumulator_free, fresh, between)

                    pe.sem_inc(staged, STAGED)
                    pe.sem_inc(pair_out, 1)
                    project_rows(0, 0)
                    project_rows(0, 1)
                    project_ctx(0)
                    project_v(0)
                    with pe.Fori(0, TURNS - 1) as i:
                        turn(i, True)
                    turn(TURNS - 1, False)

                @block.scalar
                def _(act):
                    def stage_q(r, par):
                        act.wait_ge(mm_done[0], turns[0] + r + 1)
                        act.activation(qT[:, par, :], ps[:, 7, :], ACT.Copy, scale=DH ** -0.5).then_inc(staged, 1)

                    def stage_k(r, par):
                        act.wait_ge(k_done, r + 1)
                        act.activation(kT[:, par, 0:T], ps[:, 7, :], ACT.Copy).then_inc(staged, 1)

                    def stage_ctx(r, par):
                        act.wait_ge(mm_done[1], turns[1] + r + 1)
                        act.activation(kT[:, par, T:T + L], ps[:, 7, 0:L], ACT.Copy).then_inc(staged, 1)
                        act.activation(v[:, par, TT:TT + LT, :].rearrange("p t n -> p (t n)"), ps[:, 7, L:2 * L], ACT.Copy).then_inc(staged, 1)

                    def stage_v(r, par):
                        act.wait_ge(mm_done[2], turns[2] + r + 1)
                        act.activation(v[:, par, 0:TT, :].rearrange("p t n -> p (t n)"), ps[:, 7, :], ACT.Copy).then_inc(staged, 1)

                    def turn(i, more):
                        def pair_done(par):
                            act.wait_ge(att_weighted, a.at(i) + U * (par + 1))
                            act.activation(yT[:, ds(2 * i + par, 1), :].rearrange("p a t -> p (a t)"), ps[:, 6, :], ACT.Copy).then_inc(pair_out, 1)

                        def after(u):
                            r, par, step = 2 * i + (u // U + 1), (u // U + 1) % 2, u % U
                            if u == U:
                                pair_done(0)
                            if u < U or more:
                                if step == 0:
                                    stage_q(r, par)
                                elif step == 1:
                                    stage_k(r, par)
                                elif step == 3:
                                    stage_ctx(r, par)
                                elif step == 5:
                                    stage_v(r, par)

                        att_act(act, a, i, after)
                        pair_done(1)

                    stage_q(0, 0)
                    stage_k(0, 0)
                    stage_ctx(0, 0)
                    stage_v(0, 0)
                    with act.Fori(0, TURNS - 1) as i:
                        turn(i, True)
                    turn(TURNS - 1, False)

                @block.vector
                def _(dve):
                    link = Chain(dve, na_v)

                    def window(r, par):
                        link(dve.tensor_tensor(bias[:, par, :, :].rearrange("p h (r c) -> p (h r) c", c=GRID_W)[:, :, ::-1],
                                               na_bias[:, ds(2 * r, 2), :, :].rearrange("p h r c -> p (h r) c"),
                                               colmask[:, :].unsqueeze(1).broadcast_to([P, 32, GRID_W]), ALU.add))

                    def turn(i, more):
                        def between(u):
                            if u % U == 2 and (u < U or more):
                                window(2 * i + (u // U + 1), (u // U + 1) % 2)

                        att_dve(dve, a, i, link, zeros, between)

                    dve.wait_ge(mask_in, 16)
                    link(dve.memset(zeros[:, :], 0.0))
                    window(0, 0)
                    with dve.Fori(0, TURNS - 1) as i:
                        link.loop(i, att_links(a) + 2)
                        turn(i, True)
                    link.end(TURNS - 1)
                    turn(TURNS - 1, False)
            end_ring(3, PAIRS)
            a.end(TURNS)
        na_stack.close()
        with ExitStack() as local:
            pairs = sb("hg_pairs", [P, 2, LEVELS + 1, CH], on=local)
            go = sb("hg_go", [P, 2, T], on=local)
            q = sb("hg_q", [P, T], on=local)
            gate = sb("hg_gate", [P, T], on=local)
            v = sb("hg_v", [P, TT + LT, P], on=local)
            f = sb("hg_f", [P, 2, T + L], on=local)
            key = sb("hg_key", [P, 2, T + L], on=local)
            b = sb("hg_b", [P, 2, T + L], on=local)
            cut = sb("hg_cut", [P, LEVELS, T], on=local)
            kd = sb("hg_kd", [P, T + L], on=local)
            eb = sb("hg_eb", [P, 2, T], on=local)
            qe = sb("hg_qe", [P, 2, T], on=local)
            kdT = sb("hg_kdT", [P, TT + LT, P], on=local)
            masked = sb("hg_masked", [P, 2, LEVELS + 1, CH], on=local)
            at_ = sb("hg_at", [P, 2, NCH, CH], on=local)
            state = sb("hg_state", [P, 2, NCH, P], on=local)
            cur = sb("hg_cur", [P, 5], on=local)
            sq = sb("hg_sq", [P, T], on=local)
            next_q = sb("hg_next_q", [P, T], on=local)
            next_f = sb("hg_next_f", [P, 2, T + L], on=local)
            next_v = sb("hg_next_v", [P, TT + LT, P], on=local)
            next_g = sb("hg_next_g", [P, T], on=local)
            consts_in, hg_v, lb_ready = sem("hg_consts_in"), sem("hg_chain"), sem("hg_lb_ready")
            HG_LINKS = 1 + 1 + 1 + 2 * (1 + (NCH - 2) + NCH) + 2
            staged, v_copied, gates, logs, args, exps, cuts = sem("hg_staged"), sem("hg_v_copied"), sem("hg_gates"), sem("hg_logs"), sem("hg_args"), sem("hg_exps"), sem("hg_cuts")
            multiplied, masked_ready, kd_ready, turned, kdT_ready, states_summed = (sem("hg_multiplied"), sem("hg_masked_ready"), sem("hg_kd_ready"),
                                                                           sem("hg_turned"), sem("hg_kdT_ready"), sem("hg_states_summed"))
            states_ready, read_out, squared, summed, meaned, rooted, head_done = (sem("hg_states_ready"), sem("hg_read_out"), sem("hg_squared"), sem("hg_summed"),
                                                                       sem("hg_meaned"), sem("hg_rooted"), sem("hg_head_done"))
            COL0 = 3 * NA_H * DH
            HW = HG_H * DK
            order = [list(range(NCH)), list(range(NCH))[::-1]]
            last_of = [lambda c: c * CH + CH - 1, lambda c: c * CH]

            def halves(x, n, d):
                half = CH >> (n + 1)
                y = x.rearrange("p (b e j) -> p b e j", e=2, j=half)
                lo, hi = y[:, :, 0, :], y[:, :, 1, :]
                return (hi, lo, lo[:, :, half - 1:half]) if d == 0 else (lo, hi, hi[:, :, 0:1])

            with nc.Block() as block:
                @block.sync
                def _(sp):
                    sp.dma_start(pairs[:, :, :, :].rearrange("p a l t -> p (a l t)"), io["const_pairs"]).then_inc(consts_in, 16)
                    sp.dma_start(go[:, :, :].rearrange("p a t -> p (a t)"), io["const_go"]).then_inc(consts_in, 16)
                    with sp.Fori(0, HG_H) as i:
                        for u in (0, 1, 3, 4, 2):
                            load_weights(sp, u, i, (wslot[:, u, :, :], weights(io["w_in"], i * DK + (COL0 + u * HW))))
                    for u in range(SPLIT):
                        sp.wait_ge(mm_done[u], turns[u] + HG_H)
                        load_split(sp, u, 0, (wslot[:, u, :, :], weights(io["w_out"], u * P)))

                STAGED = 8

                @block.tensor
                def _(pe):
                    def project_rows(r, u, bank, ctx):
                        weights_in(pe, u, r)
                        for k in range(KC):
                            mm = pe.matmul(bank, wslot[:, u, k, :], hT[:, k, :], start=k == 0, stop=k == KC - 1)
                        if ctx is not None:
                            for k in range(KC):
                                mm = pe.matmul(ctx, wslot[:, u, k, :], ctxT[:, k, :], start=k == 0, stop=k == KC - 1)
                        mm.then_inc(mm_done[u], 1)

                    def project_v(r, tiles):
                        for t in tiles:
                            if t == 0:
                                weights_in(pe, 3, r)
                            src, c = (hT, t) if t < TT else (ctxT, t - TT)
                            bank = ps[:, 7, t * P:(t + 1) * P] if t < TT else ps[:, 5, L + c * P:L + (c + 1) * P]
                            for k in range(KC):
                                mm = pe.matmul(bank, src[:, k, c * P:(c + 1) * P], wslot[:, 3, k, :], start=k == 0, stop=k == KC - 1)
                            if t == TT + LT - 1:
                                mm.then_inc(mm_done[3], 1)

                    def project_q_forward(r):
                        project_rows(r, 0, ps[:, 0, :], None)
                        project_rows(r, 1, ps[:, 1, :], ps[:, 3, 0:L])

                    def project_g(r):
                        pe.wait_ge(staged, STAGED * r + 5)
                        project_rows(r, 4, ps[:, 7, :], None)

                    def project_backward(r):
                        pe.wait_ge(staged, STAGED * r + 6)
                        project_rows(r, 2, ps[:, 7, :], ps[:, 3, 0:L])

                    def head(i, more):
                        if more:
                            pe.wait_ge(staged, STAGED * i + STAGED)
                            project_q_forward(i + 1)
                        pe.wait_ge(head_done, i + 1)
                        for d in range(2):
                            pe.wait_ge(kd_ready, 2 * i + d + 1)
                            if d:
                                pe.wait_ge(kdT_ready, 4 * i + 2)
                            for t in range(TT + LT):
                                mm = pe.transpose(ps[:, 4 + t // 4, t % 4 * P:(t % 4 + 1) * P], kd[:, t * P:(t + 1) * P], ident[:, :])
                            mm.then_inc(turned, 1)
                            if more and d == 0:
                                project_v(i + 1, [0, 1])
                            if more and d == 1:
                                pe.wait_ge(masked_ready, 8 * i + 5)
                                project_backward(i + 1)
                            pe.wait_ge(kdT_ready, 4 * i + 2 * d + 2)
                            if d:
                                pe.wait_ge(states_ready, 2 * i + 1)
                            for c in order[d][:-1]:
                                pe.matmul(ps[:, 6, c * P:(c + 1) * P], kdT[:, c, :], v[:, c, :], start=True, stop=True)
                            c = order[d][-1]
                            for t in range(LT):
                                mm = pe.matmul(ps[:, 6, c * P:(c + 1) * P], kdT[:, TT + t, :], v[:, TT + t, :], start=t == 0, stop=t == LT - 1)
                            mm.then_inc(states_summed, 1)
                            pe.wait_ge(cuts, 2 * i + d + 1)
                            if more and d == 0:
                                pe.wait_ge(staged, STAGED * (i + 1) + 3)
                            for c in range(NCH):
                                n = NCH * d + c
                                tok_ = slice(c * CH, (c + 1) * CH)
                                pe.wait_ge(masked_ready, 8 * i + max(n - 1, 0) + 1)
                                if more and d == 1 and c == 1:
                                    pe.wait_ge(staged, STAGED * (i + 1) + STAGED)
                                for l in range(LEVELS + 1):
                                    lhs, rhs = (cut[:, l, tok_], cut[:, l, tok_]) if l < LEVELS else (key[:, d, tok_], q[:, tok_])
                                    mm = pe.matmul(ps[:, 2 * (n % 2) + l // 4, (l % 4) * P:(l % 4 + 1) * P], lhs, rhs, start=True, stop=True)
                                mm.then_inc(multiplied, 1)
                                if more and d == 0:
                                    project_v(i + 1, [c + 2])
                            if more and d == 0:
                                project_g(i + 1)
                        pe.wait_ge(masked_ready, 8 * i + 9)
                        pe.wait_ge(states_ready, 2 * i + 2)
                        for c in range(NCH):
                            for d in range(2):
                                pe.matmul(ps[:, 7, c * CH:(c + 1) * CH], v[:, c, :], at_[:, d, c, :], start=d == 0, stop=False)
                                mm = pe.matmul(ps[:, 7, c * CH:(c + 1) * CH], state[:, d, c, :], qe[:, d, c * CH:(c + 1) * CH], start=False, stop=d == 1)
                        mm.then_inc(read_out, 1)
                        pe.wait_ge(squared, i + 1)
                        pe.matmul(ps[:, 6, :], ones[:, :], sq[:, :], start=True, stop=True).then_inc(summed, 1)

                    pe.sem_inc(head_done, 1)
                    pe.sem_inc(masked_ready, 1)
                    pe.sem_inc(read_out, 1)
                    project_q_forward(0)
                    project_v(0, range(TT + LT))
                    project_g(0)
                    project_backward(0)
                    with pe.Fori(0, HG_H - 1) as i:
                        head(i, True)
                    head(HG_H - 1, False)

                @block.scalar
                def _(act):
                    def stage_rows(r, u, dst, src, ctx_dst=None):
                        act.wait_ge(mm_done[u], turns[u] + r + 1)
                        act.activation(dst, src, ACT.Copy).then_inc(staged, 1)
                        if ctx_dst is not None:
                            act.activation(ctx_dst, ps[:, 5, L:2 * L] if u == 3 else ps[:, 3, 0:L], ACT.Copy).then_inc(staged, 1)

                    def stage_q(r):
                        stage_rows(r, 0, next_q[:, :], ps[:, 0, :])

                    def stage_forward(r):
                        stage_rows(r, 1, next_f[:, 0, 0:T], ps[:, 1, :], next_f[:, 0, T:])

                    def stage_v(r):
                        stage_rows(r, 3, next_v[:, 0:TT, :].rearrange("p t n -> p (t n)"), ps[:, 7, :],
                                   next_v[:, TT:, :].rearrange("p t n -> p (t n)"))

                    def stage_g(r):
                        stage_rows(r, 4, next_g[:, :], ps[:, 7, :])

                    def stage_backward(r):
                        stage_rows(r, 2, next_f[:, 1, 0:T], ps[:, 7, :], next_f[:, 1, T:])

                    def decays(i, d):
                        act.wait_ge(args, 4 * i + 2 * d + 1)
                        act.activation(kd[:, :], kd[:, :], ACT.Exp).then_inc(exps, 1)
                        act.activation(eb[:, d, :], b[:, d, 0:T], ACT.Exp).then_inc(exps, 1)

                    def cut_decays(i, d):
                        act.wait_ge(args, 4 * i + 2 * d + 2)
                        act.activation(cut[:, :, :], cut[:, :, :], ACT.Exp).then_inc(exps, 1)

                    def turned_keys(i, d):
                        act.wait_ge(turned, 2 * i + d + 1)
                        if d:
                            act.wait_ge(states_summed, 2 * i + 1)
                        act.activation(kdT[:, 0:TT, :].rearrange("p t n -> p (t n)"), ps[:, 4, :], ACT.Copy).then_inc(kdT_ready, 1)
                        act.activation(kdT[:, TT:, :].rearrange("p t n -> p (t n)"), ps[:, 5, 0:LT * P], ACT.Copy).then_inc(kdT_ready, 1)

                    def head(i, more):
                        act.wait_ge(staged, STAGED * i + STAGED)
                        act.activation(q[:, :], next_q[:, :], ACT.Silu)
                        act.activation(f[:, :, :], next_f[:, :, :], ACT.Sigmoid).then_inc(gates, 1)
                        act.wait_ge(head_done, i + 1)
                        act.activation(gate[:, :], next_g[:, :], ACT.Silu)
                        act.wait_ge(gates, 2 * i + 2)
                        act.activation(f[:, :, :], f[:, :, :], ACT.Ln).then_inc(logs, 1)
                        decays(i, 0)
                        if more:
                            stage_q(i + 1)
                        cut_decays(i, 0)
                        if more:
                            stage_forward(i + 1)
                        turned_keys(i, 0)
                        if more:
                            act.wait_ge(v_copied, i + 1)
                            stage_v(i + 1)
                        decays(i, 1)
                        if more:
                            stage_g(i + 1)
                        cut_decays(i, 1)
                        turned_keys(i, 1)
                        if more:
                            stage_backward(i + 1)
                        act.wait_ge(read_out, i + 2)
                        act.activation(sq[:, :], ps[:, 7, :], ACT.Square).then_inc(squared, 1)
                        act.wait_ge(meaned, i + 1)
                        act.activation(rstd[:, :], rstd[:, :], ACT.Sqrt).then_inc(rooted, 1)

                    act.activation(lb[:, 0, :, :], lb[:, 0, :, :], ACT.Sigmoid).then_inc(lb_ready, 1)
                    stage_q(0)
                    stage_forward(0)
                    stage_v(0)
                    stage_g(0)
                    stage_backward(0)
                    with act.Fori(0, HG_H - 1) as i:
                        head(i, True)
                    head(HG_H - 1, False)

                @block.vector
                def _(dve):
                    link = Chain(dve, hg_v)
                    dve.wait_ge(lb_ready, 1)
                    link(dve.tensor_scalar(lb[:, 1, :, :], lb[:, 0, :, :], -1.0, 1.0, ALU.mult, ALU.add))
                    lbs = lb[:, :, :, :].rearrange("p e d h -> p (e d) h")
                    dve.wait_ge(consts_in, 32)

                    def head(i):
                        dve.tensor_copy(cur[:, 0:4], lbs[:, :, ds(i, 1)].rearrange("p a h -> p (a h)"))
                        link(dve.tensor_copy(cur[:, 4:5], vA[:, ds(i + ROWS_A["hg_norm"], 1)]))
                        dve.wait_ge(read_out, i + 1)
                        dve.wait_ge(staged, STAGED * i + 5)
                        dve.tensor_copy(v[:, :, :], next_v[:, :, :]).then_inc(v_copied, 1)
                        dve.wait_ge(gates, 2 * i + 1)
                        for d in range(2):
                            last = dve.tensor_scalar(f[:, d, :], f[:, d, :], cur[:, 2 + d:3 + d], cur[:, d:d + 1], ALU.mult, ALU.add)
                        link(last)
                        dve.tensor_scalar(key[:, :, :], f[:, :, :], -1.0, 1.0, ALU.mult, ALU.add).then_inc(gates, 1)
                        dve.wait_ge(logs, i + 1)
                        for d in range(2):
                            go_ctx = go[:, 1, 0:1].broadcast_to([P, L])
                            flip = (lambda x: x) if d == 0 else (lambda x: x[:, ::-1])
                            dve.tensor_tensor_scan(flip(b[:, d, 0:T]), flip(go[:, d, :]), flip(f[:, d, 0:T]), 0.0, ALU.mult, ALU.add)
                            last = dve.tensor_tensor_scan(flip(b[:, d, T:T + L]), go_ctx, flip(f[:, d, T:T + L]), 0.0, ALU.mult, ALU.add)
                        link(last)
                        for d in range(2):
                            b4 = b[:, d, 0:T].rearrange("p (c j) -> p c j", j=CH)
                            end = b4[:, :, CH - 1:CH] if d == 0 else b4[:, :, 0:1]
                            ctx_end = b[:, d, T + L - 1:T + L] if d == 0 else b[:, d, T:T + 1]
                            if d:
                                dve.wait_ge(turned, 2 * i + 1)
                            dve.tensor_tensor(kd[:, 0:T].rearrange("p (c j) -> p c j", j=CH), end.broadcast_to([P, NCH, CH]), b4, ALU.subtract)
                            dve.tensor_tensor(kd[:, T:T + L], ctx_end.broadcast_to([P, L]), b[:, d, T:T + L], ALU.subtract).then_inc(args, 1)
                            if d:
                                dve.wait_ge(multiplied, 8 * i + 4)
                            for l in range(LEVELS):
                                bq, bk, mid = halves(b[:, d, 0:T], l, d)
                                oq, ok, _ = halves(cut[:, l, :], l, d)
                                wide = mid.broadcast_to(list(bq.shape))
                                dve.tensor_tensor(oq, bq, wide, ALU.subtract)
                                last = dve.tensor_tensor(ok, wide, bk, ALU.subtract)
                            last.then_inc(args, 1)
                            dve.wait_ge(exps, 6 * i + 3 * d + 1)
                            dve.tensor_tensor(kd[:, :], kd[:, :], key[:, d, :], ALU.mult).then_inc(kd_ready, 1)
                            dve.wait_ge(exps, 6 * i + 3 * d + 2)
                            dve.tensor_tensor(qe[:, d, :], eb[:, d, :], q[:, :], ALU.mult)
                            dve.wait_ge(exps, 6 * i + 3 * d + 3)
                            for l in range(LEVELS):
                                oq, ok, _ = halves(cut[:, l, :], l, d)
                                qq, _, _ = halves(q[:, :], l, d)
                                _, kk, _ = halves(key[:, d, 0:T], l, d)
                                dve.tensor_tensor(oq, oq, qq, ALU.mult)
                                last = dve.tensor_tensor(ok, ok, kk, ALU.mult)
                            last.then_inc(cuts, 1)
                            dve.wait_ge(states_summed, 2 * i + d + 1)
                            c0 = order[d][0]
                            link(dve.tensor_copy(state[:, d, c0, :], ps[:, 6, order[d][-1] * P:(order[d][-1] + 1) * P]))
                            for n, c in enumerate(order[d][:-1]):
                                nxt = order[d][n + 1]
                                e = last_of[d](c)
                                ins = dve.scalar_tensor_tensor(state[:, d, nxt, :], state[:, d, c, :], eb[:, d, e:e + 1],
                                                               ps[:, 6, c * P:(c + 1) * P], ALU.mult, ALU.add)
                                if n < NCH - 2:
                                    link(ins)
                            ins.then_inc(states_ready, 1)
                            for c in range(NCH):
                                n = NCH * d + c
                                dve.wait_ge(multiplied, 8 * i + n + 1)
                                link(dve.tensor_tensor(masked[:, n % 2, :, :].rearrange("p l t -> p (l t)"), ps[:, 2 * (n % 2):2 * (n % 2) + 2, :].rearrange("p b n -> p (b n)"),
                                                       pairs[:, d, :, :].rearrange("p l t -> p (l t)"), ALU.mult))
                                dve.tensor_reduce(at_[:, d, c, :], masked[:, n % 2, :, :].rearrange("p l t -> p t l"), AX.X, ALU.add).then_inc(masked_ready, 1)
                        dve.wait_ge(summed, i + 1)
                        dve.tensor_scalar(rstd[:, :], ps[:, 6, :], 1.0 / DK, EPS1, ALU.mult, ALU.add).then_inc(meaned, 1)
                        dve.wait_ge(rooted, i + 1)
                        link(dve.reciprocal(rstd[:, :], rstd[:, :]))
                        link(dve.scalar_tensor_tensor(sq[:, :], ps[:, 7, :], cur[:, 4:5], rstd[:, :], ALU.mult, ALU.mult))
                        dve.tensor_tensor(yT[:, ds(i + NA_H * DH // P, 1), :].rearrange("p a t -> p (a t)"), sq[:, :], gate[:, :], ALU.mult).then_inc(head_done, 1)

                    with dve.Fori(0, HG_H - 1) as i:
                        link.loop(i, HG_LINKS)
                        head(i)
                    link.end(HG_H - 1)
                    head(HG_H - 1)
            end_ring(5, HG_H)
    def first_tiles(sp, tiles):
        for u in range(SPLIT):
            load_split(sp, u, 0, *tiles(u, u * P))

    def residual_block(name, n, tiles, pieces, gate, prefetched=False):
        per, turns_ = SPLIT, n // SPLIT
        with ExitStack() as local:
            parts = split_buffers(local, name)
            sqr = sb(f"{name}_sqr", [P, 2, T], on=local)
            with nc.Block() as block:
                @block.sync
                def _(sp):
                    with sp.Fori(1 if prefetched else 0, turns_) as i:
                        for u in range(per):
                            load_split(sp, u, i, *tiles(u, i * (per * P) + u * P))

                @block.tensor
                def _(pe):
                    for j in range(n):
                        u, t = j % per, j // per
                        product(pe, parts, u, t, ps[:, u, :], parts[2], parts[3], chunk_in=rhs_in(pe) if j == 0 else None)
                        if j >= 2:
                            add_chunk(pe, sqr, j - 2)
                    for j in (n - 2, n - 1):
                        add_chunk(pe, sqr, j)

                @block.scalar
                def _(act):
                    first_hi(act, parts, yT, per, pieces)
                    for j in range(n):
                        u, t = j % per, j // per
                        if t + 1 < turns_:
                            split_hi(act, parts, u, t + 1, pieces)
                        act.wait_ge(evacuated[u], left[u] + t + 1)
                        square_chunk(act, sqr, j)

                @block.vector
                def _(dve):
                    def add(u, i):
                        projected(dve, u, i)
                        x = xT[:, ds(i * per + u, 1), :].rearrange("p a t -> p (a t)")
                        if gate is None:
                            dve.tensor_tensor(x, ps[:, u, :], x, ALU.add).then_inc(evacuated[u], 1)
                        else:
                            dve.scalar_tensor_tensor(x, ps[:, u, :], gate(i * per + u), x, ALU.mult, ALU.add).then_inc(evacuated[u], 1)

                    first_lo(dve, parts, yT, per)
                    with dve.Fori(1, turns_) as i:
                        for u in range(per):
                            add(u, i - 1)
                            split_lo(dve, parts, u, i)
                    for u in range(per):
                        add(u, turns_ - 1)
            end_split(per, turns_, pieces)
            chunks[0] += KC

    plain = lambda w: (lambda u, c0: [(wslot[:, u, :, :], weights(w, c0))])
    residual_block("wo", KC, plain(io["w_out"]), 1, lambda j: mod[:, ds(j + 2 * KC, 1), 0], prefetched=True)

    def load_wq(sp, r, head):
        for side in range(2):
            load_weights(sp, side, r, (wslot[:, side, :, :], weights(io["wq"], head * (2 * P) + side * P)))

    rms_block("n2", EPS1, [(hT, lambda k: gain2[:, k:k + 1], lambda k: mod[:, 3 * KC + k, 0:1])], prefetch=lambda sp: load_wq(sp, 0, 0))
    with ExitStack() as local:
        RING = TOPK
        htok = sb("pe_htok", [P, TT, D], on=local)
        ring = sb("pe_ring", [P, RING, D], on=local)
        qT = sb("pe_qT", [P, 2, T], on=local)
        keys = sb("pe_keys", [P, 2, P], on=local)
        keysT = sb("pe_keysT", [P, 2, P], on=local)
        s = sb("pe_s", [P, 2, TT, NKEYS], on=local)
        top = sb("pe_top", [P, 2, TT, TOPK], on=local)
        itop = sb("pe_itop", [P, 2, TT, TOPK], U32, on=local)
        itopf = sb("pe_itopf", [P, 2, TT, TOPK], on=local)
        cand = sb("pe_cand", [P, TT, TOPK, TOPK], on=local)
        best = sb("pe_best", [P, TT, TOPK], on=local)
        pos = sb("pe_pos", [P, TT, TOPK], U32, on=local)
        place = sb("pe_place", [P, 2, TT, TOPK], U32, on=local)
        placef = sb("pe_placef", [P, 2, TT, TOPK], on=local)
        pick = sb("pe_pick", [P, 2, TT * TOPK, TOPK], on=local)
        picked = sb("pe_picked", [P, 2, TT, TOPK], on=local)
        idx = sb("pe_idx", [P, 2, TT * TOPK], U32, on=local)
        g = sb("pe_g", [P, 2, TT, TOPK], on=local)
        soft = sb("pe_soft", [P, TT, TOPK], on=local)
        total = sb("pe_total", [P, TT], on=local)
        dots = sb("pe_dots", [P, TT * TOPK], on=local)
        act_ = sb("pe_act", [P, TT * TOPK], on=local)
        wgt = sb("pe_wgt", [P, TT * TOPK], on=local)
        DIAGS = 4
        diag = sb("pe_diag", [P, DIAGS, P], on=local)
        iota16 = sb("pe_iota16", [P, TOPK], on=local)
        acc = yT[:, :, :].rearrange("p (t h) n -> p t (h n)", t=TT)
        h_turned, h_left = sem("pe_h_turned"), sem("pe_h_left")
        land = [sem(f"pe_land{k}") for k in range(RING)]
        dot_done, v_used, gelu_done, wgt_done, diag_done, added = (sem("pe_dot_done"), sem("pe_v_used"), sem("pe_gelu_done"),
                                                            sem("pe_wgt_done"), sem("pe_diag_done"), sem("pe_added"))
        keys_in, keys_turned, q_ready, scored, s_ready, top_done = (sem("pe_keys_in"), sem("pe_keys_turned"), sem("pe_q_ready"),
                                                            sem("pe_scored"), sem("pe_s_ready"), sem("pe_top_done"))
        soft_arg, soft_exp, idx_ready, pe_v, iota_in = sem("pe_soft_arg"), sem("pe_soft_exp"), sem("pe_idx_ready"), sem("pe_chain"), sem("pe_iota_in")
        mem_tiles = [(io["mem_kv"][layer * D:(layer + 1) * D, :], side * 2 * P + pair * P) for side in range(2) for layer in range(2) for pair in range(2)]
        mem_left = sem("pe_mem_left")
        BLOCKS = [("u", 0), ("u", 1), ("v", 0), ("u", 2), ("v", 1), ("u", 3), ("v", 2), ("v", 3)]
        CREDIT = TOPK
        PER = TT * TOPK
        NBLK = len(BLOCKS)
        HEAD_LINKS = 5 + 6 + 7

        HALVES = [slice(0, TT // 2), slice(TT // 2, TT)]
        ALL = slice(0, TT)

        def consumed(eng, kind, h, t, k):
            eng.wait_ge(dot_done if kind == "u" else v_used, h * PER + (t * TOPK + k + 1 + (CREDIT if kind == "v" else 0)))

        def arrived(eng, kind, h, t, k):
            eng.wait_ge(land[k], h * (16 * NBLK) + 16 * (BLOCKS.index((kind, t)) + 1))

        with nc.Block() as block:
            @block.sync
            def _(sp):
                sp.dma_start(iota16[:, :], io["const_iota16"]).then_inc(iota_in, 16)

                def load_keys(r, head, first=False):
                    if not first:
                        sp.wait_ge(keys_turned, r)
                    sp.dma_start(keys[:, :, :], io["keys"][ds(head * (2 * P), 2 * P), :].rearrange("(s k) d -> k s d", s=2)).then_inc(keys_in, 16)

                def load_head(r, head):
                    load_wq(sp, r, head)
                    load_keys(r, head)

                load_keys(0, 0, first=True)
                for n, (w, c0) in enumerate(mem_tiles):
                    load_weights(sp, 2 + n % 4, n // 4, (wslot[:, 2 + n % 4, :, :], weights(w, c0)))
                with sp.Fori(0, PE_H // 2) as i:
                    after = (i * 2 + 2) % PE_H
                    load_head(i * 2 + 1, i * 2 + 1)
                    load_head(i * 2 + 2, after)

            @block.gpsimd
            def _(pool):
                def gathers(h, par):
                    for n, (kind, t) in enumerate(BLOCKS):
                        if n == 0 or (kind, t) == ("u", TT // 2):
                            pool.wait_ge(idx_ready, h * 2 + (1 if n == 0 else 2))
                        for k in range(TOPK):
                            if n:
                                consumed(pool, BLOCKS[n - 1][0], h, BLOCKS[n - 1][1], k)
                            else:
                                pool.wait_ge(v_used, h * PER + k + 1)
                            j = t * TOPK + k
                            pool.nop(nofuse=True)
                            pool.indirect_dma_start(ring[:, k, :], None, io[kind], bass.IndirectOffsetOnAxis(idx[:, par, j:j + 1], 0)).then_inc(land[k], 16)

                with pool.Fori(0, PE_H // 2) as i:
                    for par in range(2):
                        gathers(i * 2 + par, par)

            @block.tensor
            def _(pe):
                def route(r):
                    pe.wait_ge(q_ready, r * 3)
                    for side in range(2):
                        weights_in(pe, side, r)
                        for k in range(KC):
                            mm = pe.matmul(ps[:, 4 + side, :], wslot[:, side, k, :], hT[:, k, :], start=k == 0, stop=k == KC - 1)
                        mm.then_inc(mm_done[side], 1)
                    pe.wait_ge(keys_in, r * 16 + 16)
                    pe.wait_ge(s_ready, r * 2)
                    for side in range(2):
                        mm = pe.transpose(ps[:, 6, side * P:(side + 1) * P], keys[:, side, :], ident[:, :])
                    mm.then_inc(keys_turned, 1)
                    pe.wait_ge(q_ready, r * 3 + 3)
                    for side in range(2):
                        for t in range(TT):
                            mm = pe.matmul(ps[:, 6 + side, t * P:(t + 1) * P], qT[:, side, t * P:(t + 1) * P], keysT[:, side, :], start=True, stop=True)
                    mm.then_inc(scored, 1)

                def sum_v(h, t):
                    pe.wait_ge(added, h * TT + t + 1)
                    for k in range(TOPK):
                        arrived(pe, "v", h, t, k)
                        pe.wait_ge(diag_done, h * PER + t * TOPK + k + 1)
                        for half in range(2):
                            mm = pe.matmul(ps[:, 2 * (t % 2) + half, :], diag[:, k % DIAGS, :], ring[:, k, half * 512:(half + 1) * 512],
                                           start=k == 0, stop=k == TOPK - 1)
                        mm.then_inc(v_used, 1)

                pe.sem_inc(v_used, CREDIT)
                route(0)
                for t in range(TT):
                    if t >= 2:
                        pe.wait_ge(h_left, t - 1)
                    for k in range(KC):
                        mm = pe.transpose(ps[:, 2 * (t % 2) + k // 4, k % 4 * P:(k % 4 + 1) * P], hT[:, k, t * P:(t + 1) * P], ident[:, :])
                    mm.then_inc(h_turned, 1)
                pe.wait_ge(h_left, TT)
                for n in range(len(mem_tiles)):
                    u, bank = 2 + n % 4, ps[:, n // 2, n % 2 * MEM:(n % 2 + 1) * MEM]
                    weights_in(pe, u, n // 4)
                    if n < 4:
                        for k in range(KC):
                            mm = pe.matmul(bank, wslot[:, u, k, :], memT[:, k, :], start=k == 0, stop=k == KC - 1)
                    else:
                        for m in range(MEM // P):
                            for k in range(KC):
                                mm = pe.matmul(bank[:, m * P:(m + 1) * P], memT[:, k, m * P:(m + 1) * P], wslot[:, u, k, :], start=k == 0, stop=k == KC - 1)
                    mm.then_inc(mm_done[u], 1)
                pe.wait_ge(mem_left, 4)
                with pe.Fori(0, PE_H // 2) as i:
                    for par in range(2):
                        route(i * 2 + par + 1)
                        for t in range(TT):
                            sum_v(i * 2 + par, t)

            @block.scalar
            def _(act):
                def route(r, first=False):
                    for side in range(2):
                        act.wait_ge(mm_done[side], turns[side] + r + 1)
                        act.activation(qT[:, side, :], ps[:, 4 + side, :], ACT.Copy).then_inc(q_ready, 1)
                    act.wait_ge(keys_turned, r + 1)
                    act.activation(keysT[:, :, :].rearrange("p s n -> p (s n)"), ps[:, 6, 0:2 * P], ACT.Copy).then_inc(q_ready, 1)
                    act.wait_ge(scored, r + 1)
                    if not first:
                        act.wait_ge(top_done, r + 1)
                    for side in range(2):
                        act.activation(s[:, side, :, :].rearrange("p t n -> p (t n)"), ps[:, 6 + side, :], ACT.Copy).then_inc(s_ready, 1)

                def route_exp(turn, tiles):
                    act.wait_ge(soft_arg, turn + 1)
                    act.activation(soft[:, tiles, :], soft[:, tiles, :], ACT.Exp).then_inc(soft_exp, 1)

                def gelu(h, t):
                    act.wait_ge(dot_done, h * PER + (t + 1) * TOPK)
                    act.activation(act_[:, t * TOPK:(t + 1) * TOPK], dots[:, t * TOPK:(t + 1) * TOPK], ACT.Gelu).then_inc(gelu_done, 1)

                def diags(h, t):
                    act.wait_ge(wgt_done, h * TT + t + 1)
                    for k in range(TOPK):
                        n = t * TOPK + k
                        act.wait_ge(v_used, h * PER + (n + 1 + CREDIT - DIAGS))
                        act.activation(diag[:, k % DIAGS, :], ident[:, :], ACT.Copy, scale=wgt[:, n:n + 1]).then_inc(diag_done, 1)

                route(0, first=True)
                for t in range(TT):
                    act.wait_ge(h_turned, t + 1)
                    act.activation(htok[:, t, :], ps[:, 2 * (t % 2):2 * (t % 2) + 2, :].rearrange("p b n -> p (b n)"), ACT.Copy).then_inc(h_left, 1)
                for part in range(len(HALVES)):
                    route_exp(part, HALVES[part])
                for u in range(2, 6):
                    projected(act, u, 1)
                for b in range(4):
                    act.activation(mem_kv[:, b, :], ps[:, b, :], ACT.Copy).then_inc(mem_left, 1)
                with act.Fori(0, PE_H // 2) as i:
                    for par in range(2):
                        h = i * 2 + par
                        gelu(h, 0)
                        route(h + 1)
                        gelu(h, 1)
                        diags(h, 0)
                        gelu(h, 2)
                        diags(h, 1)
                        gelu(h, 3)
                        route_exp(h + 2, ALL)
                        diags(h, 2)
                        diags(h, 3)

            @block.vector
            def _(dve):
                link = Chain(dve, pe_v)
                def best_keys(heads, part):
                    tiles = [(side, t) for side in range(2) for t in range(part.start, part.stop)]
                    dve.wait_ge(s_ready, heads * 2)
                    for lo in (0, 8):
                        dve.nop(nofuse=True)
                        for side, t in tiles:
                            last = dve.max(top[:, side, t, lo:lo + 8], s[:, side, t, :])
                        link(last)
                        dve.nop(nofuse=True)
                        for side, t in tiles:
                            last = dve.max_index(itop[:, side, t, lo:lo + 8], top[:, side, t, lo:lo + 8], s[:, side, t, :])
                        link(last)
                        if lo == 0:
                            dve.nop(nofuse=True)
                            for side, t in tiles:
                                last = dve.match_replace(s[:, side, t, :], top[:, side, t, 0:8], s[:, side, t, :], -3e38)
                            link(last)
                    dve.tensor_copy(itopf[:, :, part, :], itop[:, :, part, :]).then_inc(top_done, 1)

                def best_pairs(part):
                    shape = [P, part.stop - part.start, TOPK, TOPK]
                    link(dve.tensor_tensor(cand[:, part, :, :], top[:, 0, part, :].unsqueeze(3).broadcast_to(shape),
                                           top[:, 1, part, :].unsqueeze(2).broadcast_to(shape), ALU.add))
                    tiles = range(part.start, part.stop)
                    flat = [cand[:, t, :, :].rearrange("p a b -> p (a b)") for t in range(TT)]
                    for lo in (0, 8):
                        dve.nop(nofuse=True)
                        for t in tiles:
                            last = dve.max(best[:, t, lo:lo + 8], flat[t])
                        link(last)
                        dve.nop(nofuse=True)
                        for t in tiles:
                            last = dve.max_index(pos[:, t, lo:lo + 8], best[:, t, lo:lo + 8], flat[t])
                        link(last)
                        if lo == 0:
                            dve.nop(nofuse=True)
                            for t in tiles:
                                last = dve.match_replace(flat[t], best[:, t, 0:8], flat[t], -3e38)
                            link(last)
                    dve.tensor_tensor(soft[:, part, :], best[:, part, :], best[:, part, 0:1].broadcast_to(shape[:3]), ALU.subtract).then_inc(soft_arg, 1)

                def experts(turn, par, part):
                    n = part.stop - part.start
                    cols = slice(part.start * TOPK, part.stop * TOPK)
                    dve.tensor_scalar(place[:, 0, part, :], pos[:, part, :], 4, None, ALU.logical_shift_right)
                    link(dve.tensor_scalar(place[:, 1, part, :], pos[:, part, :], TOPK - 1, None, ALU.bitwise_and))
                    link(dve.tensor_copy(placef[:, :, part, :], place[:, :, part, :]))
                    for side in range(2):
                        last = dve.tensor_tensor(pick[:, side, cols, :], placef[:, side, part, :].rearrange("p t k -> p (t k)").unsqueeze(2).broadcast_to([P, n * TOPK, TOPK]),
                                                 iota16[:, :].unsqueeze(1).broadcast_to([P, n * TOPK, TOPK]), ALU.is_equal)
                    link(last)
                    for side in range(2):
                        p4 = pick[:, side, cols, :].rearrange("p (t k) a -> p t k a", t=n)
                        last = dve.tensor_tensor(p4, p4, itopf[:, side, part, :].unsqueeze(2).broadcast_to([P, n, TOPK, TOPK]), ALU.mult)
                    link(last)
                    for side in range(2):
                        last = dve.tensor_reduce(picked[:, side, part, :].rearrange("p t k -> p (t k)"), pick[:, side, cols, :], AX.X, ALU.add)
                    link(last)
                    dve.wait_ge(soft_exp, turn + 1)
                    link(dve.tensor_reduce(total[:, part], soft[:, part, :], AX.X, ALU.add))
                    link(dve.reciprocal(total[:, part], total[:, part]))
                    dve.tensor_tensor(g[:, par, part, :], soft[:, part, :], total[:, part].unsqueeze(2).broadcast_to([P, n, TOPK]), ALU.mult)
                    flat = lambda x, half: x[:, half, :].rearrange("p t k -> p (t k)")
                    for half in HALVES if part is ALL else [part]:
                        dve.scalar_tensor_tensor(idx[:, par, half.start * TOPK:half.stop * TOPK], flat(picked[:, 0, :, :], half), float(NKEYS),
                                                 flat(picked[:, 1, :, :], half), ALU.mult, ALU.add).then_inc(idx_ready, 1)

                def dot(h, t):
                    for k in range(TOPK):
                        arrived(dve, "u", h, t, k)
                        j = t * TOPK + k
                        dve.tensor_tensor_reduce(ring[:, k, :], ring[:, k, :], htok[:, t, :], 1.0, 0.0, ALU.mult, ALU.add, dots[:, j:j + 1]).then_inc(dot_done, 1)

                def weigh(h, t, par):
                    dve.wait_ge(gelu_done, h * TT + t + 1)
                    dve.tensor_tensor(wgt[:, t * TOPK:(t + 1) * TOPK], act_[:, t * TOPK:(t + 1) * TOPK], g[:, par, t, :], ALU.mult).then_inc(wgt_done, 1)

                def add_v(h, t):
                    dve.wait_ge(v_used, h * PER + (t * TOPK + TOPK + CREDIT))
                    dve.tensor_tensor(acc[:, t, :], ps[:, 2 * (t % 2):2 * (t % 2) + 2, :].rearrange("p b n -> p (b n)"), acc[:, t, :], ALU.add).then_inc(added, 1)

                dve.sem_inc(added, 2)
                dve.wait_ge(iota_in, 16)
                link(dve.memset(acc, 0.0))
                for n, half in enumerate(HALVES):
                    best_keys(1, half)
                    best_pairs(half)
                    experts(n, 0, half)
                dve.wait_ge(h_left, TT)
                with dve.Fori(0, PE_H // 2) as i:
                    link.loop(i, 2 * HEAD_LINKS)
                    for par in range(2):
                        h = i * 2 + par
                        dot(h, 0)
                        dot(h, 1)
                        weigh(h, 0, par)
                        best_keys(h + 2, ALL)
                        dot(h, 2)
                        weigh(h, 1, par)
                        add_v(h, 0)
                        best_pairs(ALL)
                        dot(h, 3)
                        weigh(h, 2, par)
                        add_v(h, 1)
                        experts(h + 2, 1 - par, ALL)
                        weigh(h, 3, par)
                        add_v(h, 2)
                        add_v(h, 3)
                link.end(PE_H // 2)
        end_ring(2, PE_H + 1)
        for u in range(2, 6):
            landed[u] += len(mem_tiles) // 4
            turns[u] += len(mem_tiles) // 4
        o_turned, o_left = sem("pe_o_turned"), sem("pe_o_left")
        sqr = cand[:, :, :, :].rearrange("p t a b -> p (t a b)").rearrange("p (s n) -> p s n", s=2)
        with nc.Block() as block:
            @block.tensor
            def _(pe):
                for k in range(KC):
                    if k >= 4:
                        pe.wait_ge(o_left, k - 3)
                    for t in range(TT):
                        mm = pe.transpose(ps[:, k % 4, t * P:(t + 1) * P], acc[:, t, k * P:(k + 1) * P], ident[:, :])
                    mm.then_inc(o_turned, 1)
                    if k >= 2:
                        add_chunk(pe, sqr, k - 2)
                for k in (KC - 2, KC - 1):
                    add_chunk(pe, sqr, k)

            @block.scalar
            def _(act):
                for k in range(KC):
                    act.wait_ge(o_left, k + 1)
                    square_chunk(act, sqr, k)

            @block.vector
            def _(dve):
                for k in range(KC):
                    dve.wait_ge(o_turned, k + 1)
                    dve.scalar_tensor_tensor(xT[:, k, :], ps[:, k % 4, :], mod[:, 5 * KC + k, 0:1], xT[:, k, :], ALU.mult, ALU.add).then_inc(o_left, 1)
        chunks[0] += KC
    rms_block("nf", EPS1, [(xT, gain(vA, ROWS_A["norm_f"]), None)], sum_again=True)

    MEM_SLOT = 5

    def load_mem_q(sp, i, w_q, q0):
        load_weights(sp, MEM_SLOT, i, (wslot[:, MEM_SLOT, :, :], weights(w_q, i * P + q0)))

    def memory_attention(name, layer, w_q, q0, tiles):
        PAIRS = 2
        with ExitStack() as local:
            qT = sb(f"{name}_q", [P, T], on=local)
            kT = sb(f"{name}_k", [P, MEM], on=local)
            v = sb(f"{name}_v", [P, MEM // P, P], on=local)
            zeros = sb(f"{name}_zeros", [P, MEM], on=local)
            evac, pair_out, chain = sem(f"{name}_evac"), sem(f"{name}_pair_out"), sem(f"{name}_chain")
            units = [dict(q=qT[64 * h:64 * h + 64, t * P:(t + 1) * P], k=[(kT[64 * h:64 * h + 64, :], MEM)], sink=None, bias=[None],
                          v=[v[:, m, 64 * h:64 * h + 64] for m in range(MEM // P)], out=ps[64 * h:64 * h + 64, 6, t * P:(t + 1) * P])
                     for h in range(2) for t in range(TT)]
            a = Attention(name, local, units, 4)
            with nc.Block() as block:
                @block.sync
                def _(sp):
                    first_tiles(sp, tiles)
                    with sp.Fori(1, PAIRS) as i:
                        load_mem_q(sp, i, w_q, q0)

                @block.tensor
                def _(pe):
                    pe.sem_inc(pair_out, 1)
                    with pe.Fori(0, PAIRS) as i:
                        pe.wait_ge(att_logit_ready, a.at(i))
                        weights_in(pe, MEM_SLOT, i)
                        for k in range(KC):
                            mm = pe.matmul(ps[:, 0, :], wslot[:, MEM_SLOT, k, :], hT[:, k, :], start=k == 0, stop=k == KC - 1)
                        mm.then_inc(mm_done[MEM_SLOT], 1)
                        pe.wait_ge(evac, 3 * i + 3)
                        att_pe(pe, a, i, lambda u: pe.wait_ge(pair_out, i + 1) if u == 0 else None)

                @block.scalar
                def _(act):
                    with act.Fori(0, PAIRS) as i:
                        act.wait_ge(att_weighted, a.at(i))
                        projected(act, MEM_SLOT, i)
                        act.activation(qT[:, :], ps[:, 0, :], ACT.Copy, scale=DH ** -0.5).then_inc(evac, 1)
                        att_act(act, a, i)
                        act.wait_ge(att_weighted, a.at(i) + a.n)
                        act.activation(yT[:, i + CONV // P, :], ps[:, 6, :], ACT.Copy).then_inc(pair_out, 1)

                @block.vector
                def _(dve):
                    link = Chain(dve, chain)
                    link(dve.memset(zeros[:, :], 0.0))
                    with dve.Fori(0, PAIRS) as i:
                        link.loop(i, att_links(a))
                        dve.wait_ge(att_weighted, a.at(i))
                        dve.tensor_copy(kT[:, :], mem_kv[:, layer, ds(i * MEM, MEM)]).then_inc(evac, 1)
                        dve.tensor_copy(v[:, :, :].rearrange("p t n -> p (t n)"), mem_kv[:, 2 + layer, ds(i * MEM, MEM)]).then_inc(evac, 1)
                        att_dve(dve, a, i, link, zeros)
                    link.end(PAIRS)
            landed[MEM_SLOT] += PAIRS
            turns[MEM_SLOT] += PAIRS
            a.end(PAIRS)

    FFN_TILES = 2

    def load_gate_up(sp, layer, i, f0, t):
        for u in range(SPLIT):
            w = io["gate" if u % 2 == 0 else "up"][layer * D:(layer + 1) * D, :]
            load_split(sp, u, t, (wslot[:, u, :, :], weights(w, i * (FFN_TILES * P) + (f0 + u // 2) * P)))

    def feed_forward(name, layer):
        per = FFN_TILES
        stages, t0 = [], 0
        for f0 in range(0, FT, KC):
            n = min(KC, FT - f0)
            stages += [("in", f0, n, t0, n // per), ("out", f0, n, t0 + n // per, KC // SPLIT)]
            t0 += n // per + KC // SPLIT
        TURNS = t0
        with ExitStack() as local:
            parts = split_buffers(local, name)
            hid_hi = sb(f"{name}_hid_hi", [P, KC, T], F32R, on=local)
            hid_lo = sb(f"{name}_hid_lo", [P, KC, T], F32R, on=local)
            half = sb(f"{name}_half", [P, per, T], on=local)
            sqr = sb(f"{name}_sqr", [P, 2, T], on=local)
            hidden = sb(f"{name}_hidden", [P, per, T], on=local)
            hid_hi_ready, hid_ready = sem(f"{name}_hid_hi_ready"), sem(f"{name}_hid_ready")
            with nc.Block() as block:
                @block.sync
                def _(sp):
                    for kind, f0, n, b, count in stages:
                        down = io["down"][layer * D_FF + f0 * P:layer * D_FF + (f0 + n) * P, :].rearrange("(k p) n -> p k n", p=P)
                        with sp.Fori(1 if b == 0 else 0, count) as i:
                            if kind == "in":
                                load_gate_up(sp, layer, i, f0, i + b)
                            else:
                                for u in range(SPLIT):
                                    load_split(sp, u, i + b, (wslot[:, u, 0:n, :], down[:, :, ds(i * (SPLIT * P) + u * P, P)]))

                @block.tensor
                def _(pe):
                    for kind, f0, n, b, count in stages:
                        def turn(t, chunk_in, finished=None):
                            for u in range(SPLIT):
                                hi, lo = (parts[2], parts[3]) if kind == "in" else (hid_hi, hid_lo)
                                product(pe, parts, u, t, ps[:, u, :], hi, lo, KC if kind == "in" else n, chunk_in if u == 0 else None)
                                if finished is not None and finished + u >= 2:
                                    add_chunk(pe, sqr, finished + u - 2)

                        if kind == "in":
                            turn(b, rhs_in(pe) if f0 == 0 else None)
                        else:
                            turn(b, lambda k: pe.wait_ge(hid_ready, f0 + k + 1), 0 if b + count == TURNS else None)
                        if b + count == TURNS:
                            for i in range(1, count):
                                turn(b + i, None, i * SPLIT)
                            for j in (KC - 2, KC - 1):
                                add_chunk(pe, sqr, j)
                        else:
                            with pe.Fori(b + 1, b + count) as t:
                                turn(t, None)

                @block.scalar
                def _(act):
                    first_hi(act, parts, hT, SPLIT)
                    for kind, f0, n, b, count in stages:
                        def turn(i, last):
                            t = i + b
                            if kind == "in":
                                for m in range(per):
                                    projected(act, 2 * m, t)
                                    act.activation(half[:, m, :], ps[:, 2 * m, :], ACT.Silu).then_inc(evacuated[2 * m], 1)
                                    split_hi(act, parts, 2 * m, t + 1)
                                    act.wait_ge(evacuated[2 * m + 1], left[2 * m + 1] + t + 1)
                                    act.activation(hid_hi[:, ds(i * per + m, 1), :].rearrange("p a t -> p (a t)"), hidden[:, m, :],
                                                   ACT.Copy).then_inc(hid_hi_ready, 1)
                                    split_hi(act, parts, 2 * m + 1, t + 1)
                            else:
                                for u in range(SPLIT):
                                    if not last:
                                        split_hi(act, parts, u, t + 1)
                                    if finishing:
                                        act.wait_ge(evacuated[u], left[u] + t + 1)
                                        square_chunk(act, sqr, i * SPLIT + u)

                        finishing = b + count == TURNS
                        if finishing:
                            for i in range(count):
                                turn(i, i == count - 1)
                        else:
                            with act.Fori(0, count) as i:
                                turn(i, False)

                @block.vector
                def _(dve):
                    first_lo(dve, parts, hT, SPLIT)
                    for kind, f0, n, b, count in stages:
                        def turn(i, last):
                            t = i + b
                            if kind == "in":
                                for m in range(per):
                                    split_lo(dve, parts, 2 * m, t + 1)
                                    dve.wait_ge(evacuated[2 * m], left[2 * m] + t + 1)
                                    projected(dve, 2 * m + 1, t)
                                    dve.tensor_tensor(hidden[:, m, :], half[:, m, :], ps[:, 2 * m + 1, :], ALU.mult).then_inc(evacuated[2 * m + 1], 1)
                                    dve.wait_ge(hid_hi_ready, i * per + (f0 + m + 1))
                                    dve.tensor_tensor(hid_lo[:, ds(i * per + m, 1), :].rearrange("p a t -> p (a t)"), hidden[:, m, :],
                                                      hid_hi[:, ds(i * per + m, 1), :].rearrange("p a t -> p (a t)").bitcast(F32), ALU.subtract).then_inc(hid_ready, 1)
                                    split_lo(dve, parts, 2 * m + 1, t + 1)
                            else:
                                for u in range(SPLIT):
                                    projected(dve, u, t)
                                    x = xT[:, ds(i * SPLIT + u, 1), :].rearrange("p a t -> p (a t)")
                                    dve.tensor_tensor(x, ps[:, u, :], x, ALU.add).then_inc(evacuated[u], 1)
                                    if not last:
                                        split_lo(dve, parts, u, t + 1)

                        end = b + count == TURNS
                        with dve.Fori(0, count - end) as i:
                            turn(i, False)
                        if end:
                            turn(count - 1, True)
            end_split(SPLIT, TURNS)
            chunks[0] += KC

    CT = CONV // P

    def load_conv(sp, i):
        for u, c0 in ((0, 0), (1, 2 * CONV), (2, CONV)):
            load_split(sp, u, i, (wslot[:, u, :, :], weights(io["a_in"], i * P + c0)))

    rms_block("m0", EPS2, [(hT, gain(vB, ROWS_B["norm_mix"]), None)], prefetch=lambda sp: load_conv(sp, 0))
    with ExitStack() as local:
        PAD = 2
        parts = split_buffers(local, "cv")
        gated = sb("cv_gated", [P, PAD + T], on=local)
        uu = sb("cv_u", [P, T], on=local)
        conv = sb("cv_conv", [P, 2, T], on=local)
        taps = sb("cv_taps", [P, 3], on=local)
        cv_v = sem("cv_chain")
        with nc.Block() as block:
            @block.sync
            def _(sp):
                with sp.Fori(1, CT) as i:
                    load_conv(sp, i)
                load_mem_q(sp, 0, io["a_in"], 3 * CONV)

            @block.tensor
            def _(pe):
                for u in range(3):
                    product(pe, parts, u, 0, ps[:, u, :], parts[2], parts[3], chunk_in=rhs_in(pe) if u == 0 else None)
                with pe.Fori(1, CT) as i:
                    for u in range(3):
                        product(pe, parts, u, i, ps[:, u, :], parts[2], parts[3])

            @block.scalar
            def _(act):
                first_hi(act, parts, hT, 3)

                def turn(i, last):
                    act.wait_ge(evacuated[1], left[1] + i)
                    projected(act, 0, i)
                    act.activation(uu[:, :], ps[:, 0, :], ACT.Copy).then_inc(evacuated[0], 1)
                    for u in range(0 if last else 3):
                        split_hi(act, parts, u, i + 1)

                with act.Fori(0, CT - 1) as i:
                    turn(i, False)
                turn(CT - 1, True)

            @block.vector
            def _(dve):
                link = Chain(dve, cv_v)
                first_lo(dve, parts, hT, 3)
                link(dve.memset(gated[:, 0:PAD], 0.0))

                def turn(i, last):
                    dve.tensor_copy(taps[:, :], vB[:, ROWS_B["conv"]:ROWS_B["conv"] + 3 * CT].rearrange("p (k j) -> p j k", k=3)[:, ds(i, 1), :].rearrange("p a k -> p (a k)"))
                    dve.wait_ge(evacuated[0], left[0] + i + 1)
                    projected(dve, 1, i)
                    dve.tensor_tensor(gated[:, PAD:], uu[:, :], ps[:, 1, :], ALU.mult).then_inc(evacuated[1], 1)
                    if not last:
                        split_lo(dve, parts, 0, i + 1)
                    dve.wait_ge(evacuated[1], left[1] + i + 1)
                    link(dve.tensor_scalar(conv[:, 0, :], gated[:, 0:T], taps[:, 0:1], None, ALU.mult))
                    link(dve.scalar_tensor_tensor(conv[:, 1, :], gated[:, 1:T + 1], taps[:, 1:2], conv[:, 0, :], ALU.mult, ALU.add))
                    link(dve.scalar_tensor_tensor(conv[:, 0, :], gated[:, 2:T + 2], taps[:, 2:3], conv[:, 1, :], ALU.mult, ALU.add))
                    if not last:
                        split_lo(dve, parts, 1, i + 1)
                    projected(dve, 2, i)
                    dve.tensor_tensor(yT[:, ds(i, 1), :].rearrange("p a t -> p (a t)"), conv[:, 0, :], ps[:, 2, :], ALU.mult).then_inc(evacuated[2], 1)
                    if not last:
                        split_lo(dve, parts, 2, i + 1)

                with dve.Fori(0, CT - 1) as i:
                    link.loop(i, 3)
                    turn(i, False)
                link.end(CT - 1)
                turn(CT - 1, True)
        end_split(3, CT)
    memory_attention("ma0", 0, io["a_in"], 3 * CONV, plain(io["a_out"]))
    residual_block("ao", KC, plain(io["a_out"]), 1, None, prefetched=True)
    rms_block("f0", EPS2, [(hT, gain(vB, ROWS_B["norm_ffn"]), None)], prefetch=lambda sp: load_gate_up(sp, 0, 0, 0, 0))
    feed_forward("ff0", 0)

    with ExitStack() as local:
        hkv = sb("sw_hkv", [P, KC, T], on=local)
        HALVES = KV_H // 2
        HPT = 2 * GROUP
        QW = HPT * DH

        def load_swa(sp, i):
            for j in range(GROUP):
                load_weights(sp, j, i, *[(wslot[:, j, :, kv * DH:(kv + 1) * DH], weights(io["b_q"], i * QW + (kv * GROUP * DH + j * DH), DH))
                                         for kv in range(2)])
            for u, c0 in ((GROUP, 0), (GROUP + 1, KV_H * DH)):
                load_weights(sp, u, i, (wslot[:, u, :, :], weights(io["w_kv"], i * P + c0)))

        rms_block("m1", EPS2, [(hkv, gain(vB, ROWS_B["kv_norm"]), None), (hT, gain(vB, ROWS_B["norm_mix"] + KC), None)],
                  prefetch=lambda sp: load_swa(sp, 0))
        qT = sb("sw_q", [P, HALVES, GROUP, T], on=local)
        kT = sb("sw_k", [P, HALVES, T], on=local)
        v = sb("sw_v", [P, HALVES, TT, P], on=local)
        bias = sb("sw_bias_now", [P, SWA_H, 2 * P], on=local)
        staged, tile_out, sw_v = sem("sw_staged"), sem("sw_tile_out"), sem("sw_chain")
        units = []
        for half in range(HALVES):
            for j in range(GROUP):
                for kv in range(2):
                    hp, h = slice(64 * kv, 64 * kv + 64), half * HPT + kv * GROUP + j
                    for n in range(TT):
                        first = max(n - 1, 0)
                        w = (n + 1 - first) * P
                        units.append(dict(q=qT[hp, half, j, n * P:(n + 1) * P], k=[(kT[hp, half, first * P:(n + 1) * P], w)], sink=sinks[:, h:h + 1],
                                          bias=[bias[:, h, 2 * P - w:2 * P]], v=[v[:, half, b, hp] for b in range(first, n + 1)],
                                          out=ps[hp, 6, n * P:(n + 1) * P]))
        a = Attention("sw", local, units, 4)
        U = a.n // HALVES
        PERJ = 2 * TT
        PIECES = GROUP + 2
        pieces_of = [2] * GROUP + [1, 1]
        step_of = {2 + 4 * p: p for p in range(PIECES)}
        with nc.Block() as block:
            @block.sync
            def _(sp):
                with sp.Fori(1, HALVES) as i:
                    load_swa(sp, i)
                load_mem_q(sp, 0, io["b_q"], Q_WIDTH)

            def bank_of(half, p):
                return ps[:, p if half == 0 and p < 4 else 7, :]

            @block.tensor
            def _(pe):
                def project(half, p):
                    weights_in(pe, p, half, pieces_of[p])
                    if half:
                        pe.wait_ge(staged, PIECES * half + p)
                    bank = bank_of(half, p)
                    if p <= GROUP:
                        for k in range(KC):
                            mm = pe.matmul(bank, wslot[:, p, k, :], (hT if p < GROUP else hkv)[:, k, :], start=k == 0, stop=k == KC - 1)
                    else:
                        for t in range(TT):
                            for k in range(KC):
                                mm = pe.matmul(bank[:, t * P:(t + 1) * P], hkv[:, k, t * P:(t + 1) * P], wslot[:, p, k, :], start=k == 0, stop=k == KC - 1)
                    mm.then_inc(mm_done[p], 1)

                def accumulator_free(u):
                    if u % PERJ == 0 and u:
                        pe.wait_ge(tile_out, u // PERJ)

                def fresh(u):
                    if u % U == 0:
                        pe.wait_ge(staged, PIECES * (u // U + 1))

                for p in range(PIECES):
                    project(0, p)
                att_pe(pe, a, 0, accumulator_free, fresh, lambda u: project(1, step_of[u]) if u in step_of else None)

            @block.scalar
            def _(act):
                def stage(half, p):
                    projected(act, p, half)
                    dst = (qT[:, half, p, :] if p < GROUP else kT[:, half, :] if p == GROUP else v[:, half, :, :].rearrange("p t n -> p (t n)"))
                    act.activation(dst, bank_of(half, p), ACT.Copy, scale=DH ** -0.5 if p < GROUP else 1.0).then_inc(staged, 1)

                def tile_done(tile):
                    act.wait_ge(att_weighted, a.at(0) + PERJ * (tile + 1))
                    act.activation(yT[:, tile, :], ps[:, 6, :], ACT.Copy).then_inc(tile_out, 1)

                def after(u):
                    if u % PERJ == 0 and u:
                        tile_done(u // PERJ - 1)
                    if u + 1 in step_of:
                        stage(1, step_of[u + 1])

                for p in range(PIECES):
                    stage(0, p)
                att_act(act, a, 0, after)
                tile_done(a.n // PERJ - 1)

            @block.vector
            def _(dve):
                link = Chain(dve, sw_v)
                link(dve.tensor_copy(bias[:, :, ::-1], swa_bias[:, :, :]))
                att_dve(dve, a, 0, link, None)
        end_ring(PIECES, HALVES, pieces_of)
        a.end(1)
    def heads_tiles(u, c0):
        w = io["b_out"]
        pieces = [(wslot[64 * kv:64 * kv + 64, u, GROUP * n:GROUP * n + GROUP, :],
                   w[n * QW + kv * GROUP * DH:n * QW + (kv + 1) * GROUP * DH, :].rearrange("(j d) n -> d j n", d=DH)[:, :, ds(c0, P)])
                  for n in range(HALVES) for kv in range(2)]
        return pieces + [(wslot[:, u, CT:, :], w[Q_WIDTH:, :].rearrange("(k p) n -> p k n", p=P)[:, :, ds(c0, P)])]

    memory_attention("ma1", 1, io["b_q"], Q_WIDTH, heads_tiles)
    residual_block("bo", KC, heads_tiles, 5, None, prefetched=True)
    rms_block("f1", EPS2, [(hT, gain(vB, ROWS_B["norm_ffn"] + KC), None)], prefetch=lambda sp: load_gate_up(sp, 1, 0, 0, 0))
    feed_forward("ff1", 1)
    rms_block("fin", EPS2, [(hT, gain(vB, ROWS_B["final"]), None)])

    with ExitStack() as local:
        rows = sb("out_rows", [P, TT, D], on=local)
        turned, rows_ready, stored = sem("out_turned"), sem("out_ready"), sem("out_stored")
        with nc.Block() as block:
            @block.tensor
            def _(pe):
                for t in range(TT):
                    for k in range(KC):
                        mm = pe.transpose(ps[:, 2 * t + k // 4, k % 4 * P:(k % 4 + 1) * P], hT[:, k, t * P:(t + 1) * P], ident[:, :])
                    mm.then_inc(turned, 1)

            @block.vector
            def _(dve):
                for t in range(TT):
                    dve.wait_ge(turned, t + 1)
                    dve.tensor_copy(rows[:, t, :], ps[:, 2 * t:2 * t + 2, :].rearrange("p b n -> p (b n)")).then_inc(rows_ready, 1)

            @block.sync
            def _(sp):
                for t in range(TT):
                    sp.wait_ge(rows_ready, t + 1)
                    sp.dma_start(out[t * P:(t + 1) * P, :], rows[:, t, :]).then_inc(stored, 16)
                sp.wait_ge(stored, 16 * TT)


def constants():
    c = {}
    c["ident"] = np.eye(P, dtype=np.float32)
    c["ones"] = np.ones((P, P), np.float32)
    dc, m = np.arange(NDC)[:, None], np.arange(P)[None, :]
    c["spread"] = (dc + m == GRID_W - 1 + NA_KW - 1).astype(np.float32)
    start = np.asarray(bucket_starts())
    dist = np.arange(3 * P)[None, :] - (P - 1)
    c["inbucket"] = ((dist >= start[:-1, None]) & (dist < start[1:, None])).astype(np.float32)
    c["farmask"] = np.where((dist >= 0) & (dist < MAXD), 0.0, -BIG).astype(np.float32) * np.ones((SWA_H, 1), np.float32)
    col, key = (np.arange(P) % GRID_W)[:, None], np.arange(GRID_W)[None, ::-1]
    first = np.clip(col - NA_KW // 2, 0, GRID_W - NA_KW)
    c["colmask"] = np.where((key >= first) & (key < first + NA_KW), 0.0, -BIG).astype(np.float32)
    s, t = np.arange(CH)[:, None], np.arange(CH)[None, :]
    pairs = np.zeros((P, 2, LEVELS + 1, CH), np.float32)
    for n in range(LEVELS):
        half = CH >> (n + 1)
        same = s // (2 * half) == t // (2 * half)
        pairs[:, 0, n] = same & (s // half % 2 == 0) & (t // half % 2 == 1)
        pairs[:, 1, n] = same & (s // half % 2 == 1) & (t // half % 2 == 0)
    pairs[:, :, LEVELS] = (s == t)[:, None, :]
    c["pairs"] = pairs.reshape(P, -1)
    go = np.ones((P, 2, T), np.float32)
    go[:, 0, 0::CH] = 0
    go[:, 1, CH - 1::CH] = 0
    c["go"] = go.reshape(P, -1)
    c["iota16"] = np.broadcast_to(np.arange(TOPK, dtype=np.float32), (P, TOPK)).copy()
    return c


def layout(inputs):
    a = {k: np.ascontiguousarray(np.asarray(v)) for k, v in inputs.items()}
    rows = lambda x: x.reshape(-1, P)
    out = {
        "x": a["x"].reshape(T, D), "ctx": a["ctx"].reshape(L, D), "mem": a["mem_2"].reshape(MEM, D),
        "c": rows(a["c"]), "c_ctx": rows(a["c_ctx"]), "b_mod": rows(a["b_mod"]), "norm1": rows(a["norm1"]),
        "norm2": rows(a["norm2"]), "norm_f": rows(a["norm_f"]), "hg_norm": rows(a["hg_norm"]), "hg_lb": rows(a["hg_lb"]),
        "norm_mix": rows(a["norm_mix_2"]), "norm_ffn": rows(a["norm_ffn_2"]), "kv_norm": rows(a["kv_norm_2"]),
        "mem_norm": rows(a["mem_norm_2"]), "final": rows(a["final_norm_2"]), "conv": rows(a["a_conv_w_2"]),
        "w_mod": a["w_mod"][0], "w_in": a["w_in"][0], "w_out": a["w_out"][0], "rpb": a["na_rpb"].reshape(NA_H * NDR, NDC),
        "wq": a["peer_wq"][0], "keys": a["peer_keys"][0].reshape(PE_H * 2 * NKEYS, DK), "u": a["peer_u"][0], "v": a["peer_v"][0],
        "a_in": a["a_w_in_2"][0], "a_out": a["a_w_out_2"][0], "w_kv": a["w_kv_2"], "b_q": a["b_w_q_2"][0],
        "sinks": a["b_sinks_2"].reshape(1, SWA_H), "b_out": a["b_w_out_2"][0], "rel_bias": a["rel_bias_2"],
        "mem_kv": a["w_mem_kv_2"].reshape(2 * D, -1), "gate": a["w_gate_2"].reshape(2 * D, D_FF),
        "up": a["w_up_2"].reshape(2 * D, D_FF), "down": a["w_down_2"].reshape(2 * D_FF, D),
    }
    out.update({"const_" + k: v for k, v in constants().items()})
    return out


def kernel(**inputs):
    import concourse.bacc as bacc
    from concourse.bass_utils import run_bass_kernel_spmd

    nc = bacc.Bacc("TRN2", target_bir_lowering=False, num_devices=1)
    arrays, io = {}, {}
    for name, a in layout(inputs).items():
        arrays[f"in_{name}"] = a
        io[name] = nc.dram_tensor(f"in_{name}", a.shape, mybir.dt.from_np(a.dtype), kind="ExternalInput").ap()
    out = nc.dram_tensor("out", (T, D), F32, kind="ExternalOutput").ap()
    program(nc, io, out)
    r = run_bass_kernel_spmd(nc, [arrays], core_ids=[0])
    return r.results[0]["out"].reshape(1, T, D)
```
